# Optimizing a Trainium2 kernel written in Bass

```python
import math
import jax
import jax.numpy as jnp
from jax import lax
import numpy as np

D_MODEL = 1024
BATCH = 1
SEQ = 512
DEPTH = 2

GRID_W = 64
CTX_LEN = 256

HG_HEADS = 4
HG_DK = 128
HG_DV = 128
HG_WIDTH = HG_HEADS * HG_DK
HG_VWIDTH = HG_HEADS * HG_DV
F_MIN = 1e-30

RET_HEADS = 4
RET_DK = 128
RET_DV = 256
RET_QK = RET_HEADS * RET_DK
RET_V = RET_HEADS * RET_DV
ROPE_BASE = 10000.0

CHUNK = 64

N_GROUPS = 4
EXPERTS_PER_GROUP = 8
N_EXPERTS = N_GROUPS * EXPERTS_PER_GROUP
TOP_K = 2
D_EXPERT = 256
MOE_BLOCK = 128

N_MOD = 6
EPS = 1e-6

IN_SIZES = (HG_WIDTH, HG_WIDTH, HG_WIDTH, HG_VWIDTH, HG_VWIDTH, RET_QK, RET_QK, RET_V, RET_V, D_MODEL, D_MODEL)
D_IN = sum(IN_SIZES)
IN_SPLITS = tuple(int(s) for s in np.cumsum(IN_SIZES)[:-1])

kernel_name = 'hybrid_hgrn2_retention_hmoe_block'

def rms_norm(a, w):
    a32 = a.astype(jnp.float32)
    out = a32 * lax.rsqrt(jnp.mean(a32 * a32, axis=-1, keepdims=True) + EPS) * w.astype(jnp.float32)
    return out.astype(a.dtype)

def modulate(h, shift, scale):
    return h * (1 + scale) + shift

def heads(a, n_heads):
    b, l, w = a.shape
    return a.reshape(b, l, n_heads, w // n_heads).transpose(0, 2, 1, 3)

def merge_heads(o):
    b, h, l, dh = o.shape
    return o.transpose(0, 2, 1, 3).reshape(b, l, h * dh)

def rope_1d(x, pos):
    d = x.shape[-1]
    inv = ROPE_BASE ** (-jnp.arange(0, d, 2, dtype=jnp.float32) / d)
    ang = pos.astype(jnp.float32)[:, None] * inv
    cos, sin = jnp.cos(ang), jnp.sin(ang)
    x1, x2 = jnp.split(x.astype(jnp.float32), 2, axis=-1)
    return jnp.concatenate([x1 * cos - x2 * sin, x1 * sin + x2 * cos], axis=-1).astype(x.dtype)

def rope_2d(x, row_pos, col_pos):
    xr, xc = jnp.split(x, 2, axis=-1)
    return jnp.concatenate([rope_1d(xr, row_pos), rope_1d(xc, col_pos)], axis=-1)

def chunk_recurrence(q, k, v, log_f, s0):
    b_, h_, t_, _ = q.shape
    dv = v.shape[-1]
    dg = log_f.shape[-1]
    n = t_ // CHUNK

    def blocks(a):
        return jnp.moveaxis(a.astype(jnp.float32).reshape(b_, h_, n, CHUNK, a.shape[-1]), 2, 0)

    mask = jnp.tril(jnp.ones((CHUNK, CHUNK), dtype=bool))[:, :, None]

    def step(s, xs):
        qc, kc, vc, gc = xs
        b = jnp.cumsum(gc, axis=2)
        b_last = b[:, :, -1:, :]
        o_inter = jnp.einsum('bhtd,bhde->bhte', qc * jnp.exp(b), s)
        diff = b[:, :, :, None, :] - b[:, :, None, :, :]
        rel = jnp.where(mask, jnp.exp(jnp.minimum(diff, 0.0)), 0.0)
        if dg == 1:
            scores = jnp.einsum('bhtd,bhsd->bhts', qc, kc) * rel[..., 0]
        else:
            scores = jnp.einsum('bhtd,bhsd,bhtsd->bhts', qc, kc, rel)
        o = o_inter + jnp.einsum('bhts,bhse->bhte', scores, vc)
        s_new = s * jnp.exp(b_last[:, :, 0, :])[..., None] + jnp.einsum('bhsd,bhse->bhde', kc * jnp.exp(b_last - b), vc)
        return s_new, o

    s_fin, o = lax.scan(step, s0, (blocks(q), blocks(k), blocks(v), blocks(log_f)))
    return jnp.moveaxis(o, 0, 2).reshape(b_, h_, t_, dv), s_fin

def flip_seq(a):
    return jnp.flip(a, axis=2)

def two_way(ctx_in, lat_in):
    qc, kfc, kbc, vc, gfc, gbc = ctx_in
    ql, kfl, kbl, vl, gfl, gbl = lat_in
    b_, h_, _, dk = qc.shape
    s0 = jnp.zeros((b_, h_, dk, vc.shape[-1]), jnp.float32)
    oc_f, sc_f = chunk_recurrence(qc, kfc, vc, gfc, s0)
    oc_b, sc_b = chunk_recurrence(flip_seq(qc), flip_seq(kbc), flip_seq(vc), flip_seq(gbc), s0)
    ol_f, _ = chunk_recurrence(ql, kfl, vl, gfl, sc_f)
    ol_b, _ = chunk_recurrence(flip_seq(ql), flip_seq(kbl), flip_seq(vl), flip_seq(gbl), sc_b)
    return oc_f + flip_seq(oc_b), ol_f + flip_seq(ol_b)

def hgrn_lower_bounds(logits):
    p = jax.nn.softmax(logits.astype(jnp.float32), axis=0)
    return jnp.clip(jnp.cumsum(p, axis=0) - p[0], 0.0, 1.0 - 1e-6)

def hgrn_forget(z, lb):
    z = z.astype(jnp.float32)
    sig = jax.nn.sigmoid(z)
    f = lb + (1 - lb) * sig
    log_f = jnp.log(jnp.maximum(f, F_MIN))
    k = (1 - lb) * (1 - sig)
    return heads(k, HG_HEADS), heads(log_f, HG_HEADS)

def token_mixer(h, lc, row_pos, col_pos, w_in, lb_f, lb_b, hg_norm_w, ret_logit, ret_gn_w, w_o_hg, w_o_ret, w_out):
    b_, l_, _ = h.shape
    t_ = l_ - lc
    proj = h @ w_in
    hq, hf_f, hf_b, hi, hg, rq, rk, rv, rg, ga, gb = jnp.split(proj, IN_SPLITS, axis=-1)

    q_hg = heads(jax.nn.silu(hq), HG_HEADS) * (HG_DK ** -0.5)
    i_hg = heads(hi, HG_HEADS)
    k_f, lf_f = hgrn_forget(hf_f, lb_f)
    k_b, lf_b = hgrn_forget(hf_b, lb_b)
    parts = (q_hg, k_f, k_b, i_hg, lf_f, lf_b)
    o_hg_c, o_hg_l = two_way([p[:, :, :lc] for p in parts], [p[:, :, lc:] for p in parts])
    o_hg = jnp.concatenate([o_hg_c, o_hg_l], axis=2)
    o_hg = o_hg * lax.rsqrt(jnp.mean(o_hg * o_hg, axis=-1, keepdims=True) + EPS)
    o_hg = merge_heads(o_hg) * hg_norm_w.astype(jnp.float32) * jax.nn.silu(hg.astype(jnp.float32))
    y_hg = o_hg.astype(h.dtype) @ w_o_hg

    q_r = heads(rq, RET_HEADS) * (RET_DK ** -0.5)
    k_r = heads(rk, RET_HEADS)
    v_r = heads(rv, RET_HEADS)
    q_c, q_l = q_r[:, :, :lc], rope_2d(q_r[:, :, lc:], row_pos, col_pos)
    k_c, k_l = k_r[:, :, :lc], rope_2d(k_r[:, :, lc:], row_pos, col_pos)
    log_gamma = jax.nn.log_sigmoid(ret_logit.astype(jnp.float32))

    def decay(direction, length):
        return jnp.broadcast_to(log_gamma[direction][None, :, None, None], (b_, RET_HEADS, length, 1))

    o_r_c, o_r_l = two_way([q_c, k_c, k_c, v_r[:, :, :lc], decay(0, lc), decay(1, lc)],
                           [q_l, k_l, k_l, v_r[:, :, lc:], decay(0, t_), decay(1, t_)])
    o_r = jnp.concatenate([o_r_c, o_r_l], axis=2)
    mu = jnp.mean(o_r, axis=-1, keepdims=True)
    var = jnp.mean(jnp.square(o_r - mu), axis=-1, keepdims=True)
    o_r = merge_heads((o_r - mu) * lax.rsqrt(var + EPS)) * ret_gn_w.astype(jnp.float32)
    o_r = o_r * jax.nn.silu(rg.astype(jnp.float32))
    y_ret = o_r.astype(h.dtype) @ w_o_ret

    y = (jax.nn.sigmoid(ga) * y_hg + jax.nn.sigmoid(gb) * y_ret) @ w_out
    return y[:, :lc], y[:, lc:]

def hierarchical_moe(h, wg, bg, we, be, w_gate, w_up, w_down):
    n_tok, d = h.shape
    h32 = h.astype(jnp.float32)
    g_logits = h32 @ wg.astype(jnp.float32) + bg.astype(jnp.float32)
    g_prob = jax.nn.softmax(g_logits, axis=-1)
    grp = jnp.argmax(g_logits, axis=-1)
    g_val = jnp.take_along_axis(g_prob, grp[:, None], axis=1)
    e_logits = (h32 @ we.astype(jnp.float32) + be.astype(jnp.float32)).reshape(n_tok, N_GROUPS, EXPERTS_PER_GROUP)
    e_in_grp = jnp.take_along_axis(e_logits, grp[:, None, None], axis=1)[:, 0]
    top_val, top_idx = lax.top_k(e_in_grp, TOP_K)
    weights = g_val * jax.nn.softmax(top_val, axis=-1)
    expert = grp[:, None] * EXPERTS_PER_GROUP + top_idx

    n_assign = n_tok * TOP_K
    flat_e = expert.reshape(-1)
    flat_tok = jnp.repeat(jnp.arange(n_tok), TOP_K)
    flat_w = weights.reshape(-1)
    order = jnp.argsort(flat_e)
    e_sorted = flat_e[order]
    tok_sorted = flat_tok[order]
    counts = jnp.bincount(flat_e, length=N_EXPERTS)
    padded = ((counts + MOE_BLOCK - 1) // MOE_BLOCK) * MOE_BLOCK
    seg_start = jnp.cumsum(counts) - counts
    pad_end = jnp.cumsum(padded)
    pad_start = pad_end - padded
    dest = pad_start[e_sorted] + (jnp.arange(n_assign) - seg_start[e_sorted])
    n_blocks = (n_assign + N_EXPERTS * (MOE_BLOCK - 1) + MOE_BLOCK - 1) // MOE_BLOCK
    buf_tok = jnp.full((n_blocks * MOE_BLOCK,), n_tok, jnp.int32).at[dest].set(tok_sorted.astype(jnp.int32))
    block_expert = jnp.minimum(jnp.searchsorted(pad_end, jnp.arange(n_blocks) * MOE_BLOCK, side='right'), N_EXPERTS - 1)
    h_pad = jnp.concatenate([h, jnp.zeros((1, d), h.dtype)], axis=0)
    x_blocks = h_pad[buf_tok].reshape(n_blocks, MOE_BLOCK, d)

    def expert_block(args):
        xb, e = args
        return (jax.nn.silu(xb @ w_gate[e]) * (xb @ w_up[e])) @ w_down[e]

    y_buf = lax.map(expert_block, (x_blocks, block_expert)).reshape(n_blocks * MOE_BLOCK, d)
    y_assign = y_buf[dest] * flat_w[order][:, None].astype(h.dtype)
    return jax.ops.segment_sum(y_assign, tok_sorted, num_segments=n_tok)

def setup_inputs(seed: int = 0) -> dict:
    key = jax.random.key(seed)
    ks = jax.random.split(key, 26)
    f32 = jnp.float32
    d = D_MODEL

    def nrm(k, shape, scale):
        return jax.random.normal(k, shape, f32) * scale

    base_decay_logit = jnp.asarray(np.log(2.0 ** (5 + np.arange(RET_HEADS)) - 1.0), f32)
    return {
        'x': nrm(ks[0], (BATCH, SEQ, d), 1.0),
        'c': nrm(ks[1], (BATCH, d), 1.0),
        'ctx': nrm(ks[2], (BATCH, CTX_LEN, d), 1.0),
        'c_ctx': nrm(ks[3], (d,), 1.0),
        'w_mod': nrm(ks[4], (DEPTH, d, N_MOD * d), 0.5 * d ** -0.5),
        'b_mod': nrm(ks[5], (DEPTH, N_MOD * d), 0.02),
        'norm_mix_w': 1.0 + nrm(ks[6], (DEPTH, d), 0.05),
        'norm_ffn_w': 1.0 + nrm(ks[7], (DEPTH, d), 0.05),
        'w_in': nrm(ks[8], (DEPTH, d, D_IN), d ** -0.5),
        'hgrn_lb_logits': nrm(ks[9], (2, DEPTH, HG_WIDTH), 1.0),
        'hgrn_norm_w': 1.0 + nrm(ks[10], (DEPTH, HG_VWIDTH), 0.05),
        'ret_decay_logit': base_decay_logit + nrm(ks[11], (DEPTH, 2, RET_HEADS), 0.1),
        'ret_gn_w': 1.0 + nrm(ks[12], (DEPTH, RET_V), 0.05),
        'w_o_hgrn': nrm(ks[13], (DEPTH, HG_VWIDTH, d), HG_VWIDTH ** -0.5),
        'w_o_ret': nrm(ks[14], (DEPTH, RET_V, d), RET_V ** -0.5),
        'w_out': nrm(ks[15], (DEPTH, d, d), d ** -0.5),
        'router_group_w': nrm(ks[16], (DEPTH, d, N_GROUPS), d ** -0.5),
        'router_group_b': nrm(ks[17], (DEPTH, N_GROUPS), 0.01),
        'router_expert_w': nrm(ks[18], (DEPTH, d, N_EXPERTS), d ** -0.5),
        'router_expert_b': nrm(ks[19], (DEPTH, N_EXPERTS), 0.01),
        'expert_w_gate': nrm(ks[20], (DEPTH, N_EXPERTS, d, D_EXPERT), d ** -0.5),
        'expert_w_up': nrm(ks[21], (DEPTH, N_EXPERTS, d, D_EXPERT), d ** -0.5),
        'expert_w_down': nrm(ks[22], (DEPTH, N_EXPERTS, D_EXPERT, d), D_EXPERT ** -0.5),
        'final_norm_w': 1.0 + nrm(ks[23], (d,), 0.05),
    }

def reference(x, c, ctx, c_ctx, w_mod, b_mod, norm_mix_w, norm_ffn_w, w_in, hgrn_lb_logits, hgrn_norm_w,
              ret_decay_logit, ret_gn_w, w_o_hgrn, w_o_ret, w_out, router_group_w, router_group_b,
              router_expert_w, router_expert_b, expert_w_gate, expert_w_up, expert_w_down, final_norm_w):
    b_, t_, d = x.shape
    lc = ctx.shape[1]
    ROWS = t_ // GRID_W
    row_pos = jnp.repeat(jnp.arange(ROWS), GRID_W)
    col_pos = jnp.tile(jnp.arange(GRID_W), ROWS)
    lb_fwd = hgrn_lower_bounds(hgrn_lb_logits[0])
    lb_bwd = hgrn_lower_bounds(hgrn_lb_logits[1])
    silu_c = jax.nn.silu(c)
    silu_cc = jax.nn.silu(c_ctx)

    for layer in range(DEPTH):
        mod_x = (silu_c @ w_mod[layer] + b_mod[layer])[:, None, :]
        mod_c = (silu_cc @ w_mod[layer] + b_mod[layer])[None, None, :]
        sh1x, sc1x, g1x, sh2x, sc2x, g2x = jnp.split(mod_x, N_MOD, axis=-1)
        sh1c, sc1c, g1c, sh2c, sc2c, g2c = jnp.split(mod_c, N_MOD, axis=-1)

        h = jnp.concatenate([modulate(rms_norm(ctx, norm_mix_w[layer]), sh1c, sc1c),
                             modulate(rms_norm(x, norm_mix_w[layer]), sh1x, sc1x)], axis=1)
        y_c, y_x = token_mixer(h, lc, row_pos, col_pos, w_in[layer], lb_fwd[layer], lb_bwd[layer],
                               hgrn_norm_w[layer], ret_decay_logit[layer], ret_gn_w[layer],
                               w_o_hgrn[layer], w_o_ret[layer], w_out[layer])
        x = x + g1x * y_x

        moe_args = (router_group_w[layer], router_group_b[layer], router_expert_w[layer], router_expert_b[layer],
                    expert_w_gate[layer], expert_w_up[layer], expert_w_down[layer])
        h_x = modulate(rms_norm(x, norm_ffn_w[layer]), sh2x, sc2x)
        if layer < DEPTH - 1:
            ctx = ctx + g1c * y_c
            h_c = modulate(rms_norm(ctx, norm_ffn_w[layer]), sh2c, sc2c)
            tokens = jnp.concatenate([h_c, h_x], axis=1).reshape(-1, d)
            y = hierarchical_moe(tokens, *moe_args).reshape(b_, lc + t_, d)
            ctx = ctx + g2c * y[:, :lc]
            x = x + g2x * y[:, lc:]
        else:
            y = hierarchical_moe(h_x.reshape(-1, d), *moe_args).reshape(b_, t_, d)
            x = x + g2x * y

    return rms_norm(x, final_norm_w)


_drawn_inputs = setup_inputs


def setup_inputs(seed=0):
    import zlib

    import numpy as np

    out = dict(_drawn_inputs(seed))
    spreads = {}
    factors = {'hgrn_lb_logits': 6.256,
     'hgrn_norm_w': 4.887,
     'ret_gn_w': 4.771,
     'router_group_b': 45.223,
     'router_expert_b': 22.775,
     'norm_ffn_w': 2.721}
    for name, (base, spread) in spreads.items():
        noise = np.random.default_rng([zlib.crc32(name.encode()), seed]).standard_normal(out[name].shape)
        drawn = base * np.exp(spread * noise) if base else spread * noise
        out[name] = jnp.asarray(drawn.astype(out[name].dtype))
    for name, factor in factors.items():
        out[name] = (out[name] * factor).astype(out[name].dtype)
    return out
```

```python
from contextlib import ExitStack

import concourse.bass as bass
from concourse import mybir

F32 = mybir.dt.float32
BF16 = mybir.dt.bfloat16
I32 = mybir.dt.int32
U32 = mybir.dt.uint32
ALU = mybir.AluOpType
ACT = mybir.ActivationFunctionType
AX = mybir.AxisListType

P = 128
D = 1024
KD = D // P
LAT, CTX = 512, 256
TOK = CTX + LAT
TT = TOK // P
DEPTH = 2
SEG = ((0, CTX, 1), (CTX, TOK, 0))
HEADS = 4
DV = 256
C = 64
LEVELS = 6
PART = 256
NPART = TOK // PART
UNITS = HEADS * 2 * NPART
EPS = 1e-6
F_MIN = 1e-30
QSCALE = float(P) ** -0.5
NG, NPG = 4, 8
NE = NG * NPG
DE = 256
BLK = 128
TOPK = 2
NBMAX = NE + TOPK * TOK // BLK
NBMAX += NBMAX % 2
CAP = NBMAX * BLK
XW = TOK + P

GROUPS = [("ff", 512, 0), ("fb", 1024, 0), ("q", 0, 0), ("v", 1536, 1), ("g", 2048, 0),
          ("rq", 2560, 0), ("rk", 3072, 0), ("rv0", 3584, 1), ("rv1", 4096, 1), ("rg0", 4608, 0), ("rg1", 5120, 0),
          ("ga0", 5632, 0), ("ga1", 6144, 0), ("gb0", 6656, 0), ("gb1", 7168, 0)]
NHG = 5
TILES = [(g, m) for g, (_, _, tm) in enumerate(GROUPS) for m in range(TT // 2 if tm else 4)]
TILES_HG = sum(1 for g, _ in TILES if g < NHG)
STEPS = len(TILES) - TILES_HG
SCR = {"rq": 0, "rk": 4, "rg0": 8, "rg1": 12, "ga0": 16, "ga1": 20, "gb0": 24, "gb1": 28}
UNIT_AT = {u * STEPS // UNITS: u for u in range(UNITS)}
NMOD = 6 * D // 512
USES = NMOD + len(GROUPS) + 4

V_BMOD, V_MIX, V_FFN, V_HGN, V_GN, V_FIN, V_RB, V_LB, V_N = 0, 48, 56, 64, 68, 76, 84, 85, 101


PER_LAYER = {}
for _n, _names in (
        (NMOD, "mod_mm mod_ev"), (len(TILES), "proj_mm proj_ev"), (KD, "y_mm y_ev out_mm sq_mix sq_ffn"),
        (16 * 12, "vec_ld"), (1, "final_vec idx0 plan slots vec_mm modT_mm ms_mix ms_ffn rstd_mix rstd_ffn lg_mm lgT Lg_mm rank_mm amod"),
        (16 * STEPS // 2, "spill0 spill1"), (16, "wohg mc_ld idx_clr idxs"), (HEADS, "hgate oT_mm hr"), (32, "rc_ld"),
        (HEADS * TT, "pv_mm rg_done on ro_ev roT_mm rvar rr"), (48 * HEADS // 2, "rqkv0 rqkv1"), (32 * KD // 2, "gab0 gab1"),
        (2 * KD, "x_mid h_mix h_ffn hm_mix hm_ffn"), (TT, "hstg hrow_mm yc_mm"), (16 * TT // 2, "hrow0 hrow1"),
        (32 * TT, "idx_sc"), (KD * TT, "x_end"), (UNITS, "ql kl f k k1 lnf dd ee"),
        (2 * UNITS, "sc_ev sc_mm kT kT_mm pS_mm scT o_mmh o_evh"), (13 * 2 * HEADS, "S"), (8 * HEADS, "rsc_ev rsc_mm"),
        (2 * HEADS, "rot_mm rot"), (2, "Mb gd gx"), (2 * TT, "yc"), (3, "pre pre_a"), (4 * HEADS, "dt"), (4 * TT, "m8"),
        (32 * TT // 2, "yg0 yg1")):
    for _name in _names.split():
        PER_LAYER[_name] = _n


def unit(u):
    h, r = divmod(u, 2 * NPART)
    d, n = divmod(r, NPART)
    part = n if d == 0 or n == 0 else NPART - n
    return h, d, n, part


def build(nc, a):
    with ExitStack() as ctx:
        def sb(name, shape, dt=F32):
            return ctx.enter_context(nc.sbuf_tensor(name, shape, dt))

        sems = {}

        def sem(name):
            if name not in sems:
                sems[name] = ctx.enter_context(nc.semaphore(name))
            return sems[name]

        def after(name, L, n):
            return sem(name), L * PER_LAYER.get(name, 0) + n

        xT = sb("xT", [P, KD, TOK])
        hT = sb("hT", [P, KD, TOK])
        ring = sb("ring", [P, 2, KD, 512])
        cst = sb("cst", [P, 2 * P + 2 * 7 * C])
        ident, meanw = cst[:, 0:P], cst[:, P:2 * P]
        masks = [cst[:, 2 * P + i * 7 * C:2 * P + (i + 1) * 7 * C].rearrange("p (l t) -> p l t", l=7) for i in range(2)]
        eps = sb("eps", [P, 1])
        ccrow = sb("ccrow", [16, P])
        cT = sb("cT", [P, 16])
        vrow = sb("vrow", [V_N, P])
        vec = sb("vec", [P, V_N])
        modT = sb("modT", [P, 48, 2])
        amod = sb("amod", [P, 2, KD, 2])
        lbm = sb("lbm", [P, 4, 8])
        dec = sb("dec", [P, 6, 8])
        wrt = sb("wrt", [P, KD, NG + NE])
        AR = 29000
        arena = sb("arena", [P, AR])

        def ar(off, n, **kw):
            assert off + n <= AR
            v = arena[:, off:off + n]
            return v.rearrange("p (a b) -> p a b", **kw) if kw else v

        xrow = ar(0, TT * D, a=TT)
        rstd = ar(28200, TOK)
        mrow = ar(6144, 6 * D)
        hq = ar(0, 3072, a=4)
        sig = [ar(3072, 3072, a=4), ar(6144, 3072, a=4)]
        hv = ar(9216, 3072, a=TT)
        hgate = ar(12288, 3072, a=4)
        E = ar(15360, 8 * PART, a=8)
        QL = ar(17408, 7 * PART, a=7)
        KL = ar(19200, 7 * PART, a=7)
        Pc = ar(20992, 4 * (C + 1), a=4)
        ff = ar(21252, PART)
        kk = ar(21508, PART)
        gg = ar(21764, 4 * (C + 1), a=4)
        keep = ar(22024, 4 * (C + 1), a=4)
        msk = ar(22284, 7 * C, a=7)
        scT = ar(22732, C)
        kTs = ar(22796, P)
        S = ar(22924, 3 * P, a=3)
        oacc = ar(23308, TT * P, a=TT)
        stage = [ar(24076, 1024), ar(25100, 1024)]
        junk = ar(26124, P)
        ss = ar(26252, 16)
        rgate = ar(15360, 6144, a=8)
        rqk = [ar(0, 1536, a=2), ar(1536, 1536, a=2)]
        rv = [ar(3072, 1536, a=TT), ar(4608, 1536, a=TT)]
        rtmp = ar(6144, LAT)
        PT = ar(6656, 3584)
        Wd = ar(10240, XW)
        Dc = ar(11136, XW)
        rc = ar(21504, 2 * LAT + P + 3 * XW)
        cosT, sinT, perm = rc[:, 0:512], rc[:, 512:1024], rc[:, 1024:1152]
        XX, XP, XN = [rc[:, 1152 + i * XW:1152 + (i + 1) * XW] for i in range(3)]
        on = ar(25344, 512, a=2)
        wtmp = ar(25856, XW)
        dtmp = ar(26752, XW)
        rst = ar(27648, 64)
        merged = ar(0, 6144, a=8)
        gab = [ar(6144, 1536, a=2), ar(7680, 1536, a=2)]
        ytmp = ar(9216, TOK)
        WE = [ar(i * 6144, 6144) for i in range(2)]
        XB = [ar(12288 + i * 1024, 1024) for i in range(2)]
        XT = [ar(14336 + i * 1024, 1024, a=8) for i in range(2)]
        sg = [ar(16384 + i * 256, 256) for i in range(2)]
        hid = [ar(16896 + i * 256, 256) for i in range(2)]
        hidT = [ar(17408 + i * 256, 256, a=2) for i in range(2)]
        YB = [ar(17920 + i * 1024, 1024) for i in range(2)]
        mc = ar(20000, P + NBMAX * NE + NE + NBMAX)
        tri, jm = mc[:, 0:P], mc[:, P:P + NBMAX * NE].rearrange("p (j e) -> p j e", e=NE)
        io = mc[:, P + NBMAX * NE:P + NBMAX * NE + NE]
        lgT = ar(21700, TOK)
        Lg = ar(22470, TT * 36, a=TT)
        ro = ar(22700, 2300)
        hstg = [ar(25000, 1024), ar(26024, 1024)]
        nil = sb("nil", [P, 4])
        trib = sb("trib", [P, 2 * P], BF16)
        Mb = sb("Mb", [P, TT, NE], BF16)
        u8 = sb("u8", [P, 2 * TT, 8], U32)
        slots = sb("slots", [P, 4, TT], U32)
        tokid = sb("tokid", [P, TT], I32)
        idx0 = sb("idx0", [P, NBMAX], I32)
        idxs = sb("idxs", [P, NBMAX], I32)
        idxc = sb("idxc", [P, 2], I32)
        ebi = sb("ebi", [1, NBMAX + 2], I32)

        ps = ctx.enter_context(nc.psum_tensor("ps", [P, 8, 512], F32))

        def pair(b):
            return ps[:, b:b + 2, :].rearrange("p b n -> p (b n)")

        def tokens(b):
            return pair(b)[:, 256:1024]

        def dram(name, shape, dt=F32):
            return nc.dram_tensor(name, shape, dt, kind="Internal").ap()

        scr = dram("scr", (32, P, TOK))
        scrv = dram("scrv", (TOK, 1024))
        hrow = dram("hrow", (TOK, D))
        yrow = dram("yrow", (CAP, D))
        idxd = [dram(f"idxd{i}", (CAP, 1), I32) for i in range(DEPTH)]

        def uses(L):
            out = [a["w_mod"][L][:, g * 512:(g + 1) * 512] for g in range(NMOD)]
            out += [a["w_in"][L][:, c:c + 512] for _, c, _ in GROUPS]
            out += [a[n][L][:, c:c + 512] for n in ("w_o_ret", "w_out") for c in (0, 512)]
            return [x.rearrange("(k p) n -> p k n", p=P) for x in out]

        def used(L, n):
            if n < NMOD:
                return after("mod_mm", L, n + 1)
            n -= NMOD
            if n < len(GROUPS):
                return after("proj_mm", L, 1 + max(i for i, (g, _) in enumerate(TILES) if g == n))
            n -= len(GROUPS)
            return after("y_mm", L, 4 * (n + 1)) if n < 2 else after("out_mm", L, 4 * (n - 1))

        stream = [(L, n, x) for L in range(DEPTH) for n, x in enumerate(uses(L))]

        def ring_ready(eng, L, n):
            i = L * USES + n
            eng.wait_ge(sem(f"ring{i % 2}"), 16 * (i // 2 + 1))

        def reg_wait(eng, s, v, least=1):
            eng.wait_ge(s, v)
            if not isinstance(v, int):
                eng.wait_ge(s, least)

        def ret_transposes(pe, L, i):
            pe.wait_ge(*after("ro_ev", L, i + 1))
            if i >= 2:
                pe.wait_ge(*after("rg_done", L, i - 1))
            for e in range(2):
                mm = pe.transpose(ps[:, 6 + i % 2, e * P:(e + 1) * P], on[:, i % 2, e * P:(e + 1) * P], ident)
            mm.then_inc(sem("roT_mm"), 1)

        def head_gate(dve, L, h):
            dve.wait_ge(*after("oT_mm", L, h + 1))
            dve.scalar_tensor_tensor(out=hgate[:, h, :], in0=pair(6)[:, 0:TOK], scalar=vec[:, V_HGN + h:V_HGN + h + 1],
                                     in1=hgate[:, h, :], op0=ALU.mult, op1=ALU.mult).then_inc(sem("hgate"), 1)

        def ret_gate(dve, L, i):
            h, t = divmod(i, TT)
            dve.wait_ge(*after("roT_mm", L, i + 1))
            for e in range(2):
                x = rgate[:, 2 * h + e, t * P:(t + 1) * P]
                ins = dve.scalar_tensor_tensor(out=x, in0=ps[:, 6 + i % 2, e * P:(e + 1) * P], scalar=vec[:, V_GN + 2 * h + e:V_GN + 2 * h + e + 1],
                                               in1=x, op0=ALU.mult, op1=ALU.mult)
            ins.then_inc(sem("rg_done"), 1)

        block = ctx.enter_context(nc.Block())

        @block.sync
        def _(sp):
            def fill(i):
                if i >= len(stream):
                    return
                if i >= 2:
                    sp.wait_ge(*used(*stream[i - 2][:2]))
                sp.dma_start(ring[:, i % 2], stream[i][2]).then_inc(sem(f"ring{i % 2}"), 16)

            sp.dma_start(cst[:], a["cst"]).then_inc(sem("cst_ld"), 16)
            sp.dma_start(ccrow[0:8, :], a["c"].rearrange("a (k p) -> (a k) p", p=P)).then_inc(sem("cst_ld"), 16)
            sp.dma_start(ccrow[8:16, :], a["c_ctx"].rearrange("(k p) -> k p", p=P)).then_inc(sem("cst_ld"), 16)
            sp.dma_start(xrow[:, 0:2, :], a["ctx"][0].rearrange("(t p) d -> p t d", p=P)).then_inc(sem("x_ld"), 16)
            sp.dma_start(xrow[:, 2:6, :], a["x"][0].rearrange("(t p) d -> p t d", p=P)).then_inc(sem("x_ld"), 16)
            fill(0)
            fill(1)
            for L in range(DEPTH):
                base = L * USES
                if L:
                    sp.wait_ge(*after("final_vec", L - 1, 1))
                else:
                    sp.wait_ge(sem("init"), 1)
                vl = sem("vec_ld")
                for r, x in ((V_BMOD, a["b_mod"][L]), (V_MIX, a["norm_mix_w"][L]), (V_FFN, a["norm_ffn_w"][L]),
                             (V_HGN, a["hgrn_norm_w"][L]), (V_GN, a["ret_gn_w"][L]), (V_FIN, a["final_norm_w"])):
                    x = x.rearrange("(k p) -> k p", p=P)
                    sp.dma_start(vrow[r:r + x.shape[0], :], x).then_inc(vl, 16)
                sp.dma_start(vrow[V_LB:V_LB + 16, :], a["hgrn_lb_logits"].rearrange("d l (h p) -> (d l h) p", p=P)).then_inc(vl, 16)
                sp.dma_start(vrow[V_RB:V_RB + 1, 0:NG], a["router_group_b"][L:L + 1, :]).then_inc(vl, 16)
                sp.dma_start(vrow[V_RB:V_RB + 1, NG:NG + NE], a["router_expert_b"][L:L + 1, :]).then_inc(vl, 16)
                sp.dma_start(dec[:, 0, :], a["ret_decay_logit"][L].rearrange("d h -> (d h)").partition_broadcast(P)).then_inc(vl, 16)
                sp.dma_start(wrt[:, :, 0:NG], a["router_group_w"][L].rearrange("(k p) n -> p k n", p=P)).then_inc(vl, 16)
                sp.dma_start(wrt[:, :, NG:NG + NE], a["router_expert_w"][L].rearrange("(k p) n -> p k n", p=P)).then_inc(vl, 16)
                for n in range(NMOD):
                    fill(base + n + 2)
                for k, (g, m) in enumerate(TILES):
                    i = k - TILES_HG
                    if i >= 0:
                        sp.wait_ge(*after("proj_ev", L, k + 1))
                        name, _, tm = GROUPS[g]
                        if tm:
                            c0 = 512 if name == "rv1" else 0
                            dst = scrv[2 * m * P:(2 * m + 2) * P, c0:c0 + 512].rearrange("(b p) n -> p b n", p=P)
                            src = stage[i % 2].rearrange("p (b n) -> p b n", b=2)
                        else:
                            dst, src = scr[SCR[name] + m], stage[i % 2][:, 0:TOK]
                        sp.dma_start(dst, src).then_inc(sem(f"spill{i % 2}"), 16)
                    if k + 1 == len(TILES) or TILES[k + 1][0] != g:
                        fill(base + NMOD + g + 2)

                sp.wait_ge(*after("proj_mm", L, len(TILES)))
                wohg = hT[:].rearrange("p k t -> p (k t)")[:, 0:4096].rearrange("p (k n) -> p k n", k=4)
                sp.dma_start(wohg, a["w_o_hgrn"][L].rearrange("(k p) n -> p k n", p=P)).then_inc(sem("wohg"), 16)
                for i in range(2):
                    sp.wait_ge(*after(f"spill{i}", L, 16 * (STEPS // 2)))
                sp.wait_ge(*after("hgate", L, HEADS))
                sp.dma_start(rc, a["rc"]).then_inc(sem("rc_ld"), 16)
                sp.dma_start(rgate, scr[8:16].rearrange("m p t -> p m t")).then_inc(sem("rc_ld"), 16)
                for h in range(HEADS):
                    if h >= 2:
                        sp.wait_ge(*after("pv_mm", L, TT * (h - 1)))
                    ld = sem(f"rqkv{h % 2}")
                    sp.dma_start(rqk[h % 2][:, 0], scr[h]).then_inc(ld, 16)
                    sp.dma_start(rqk[h % 2][:, 1], scr[4 + h]).then_inc(ld, 16)
                    sp.dma_start(rv[h % 2], scrv[:, h * DV:(h + 1) * DV].rearrange("(t p) n -> p t n", p=P)).then_inc(ld, 16)
                sp.wait_ge(*after("rg_done", L, HEADS * TT))
                for m in range(KD):
                    if m >= 2:
                        sp.wait_ge(*after("y_ev", L, m - 1))
                    sp.dma_start(gab[m % 2][:, 0], scr[16 + m]).then_inc(sem(f"gab{m % 2}"), 16)
                    sp.dma_start(gab[m % 2][:, 1], scr[24 + m]).then_inc(sem(f"gab{m % 2}"), 16)
                    if m in (3, 7):
                        fill(base + NMOD + len(GROUPS) + (0 if m == 3 else 1) + 2)
                fill(base + NMOD + len(GROUPS) + 2 + 2)
                fill(base + NMOD + len(GROUPS) + 3 + 2)

                sp.wait_ge(*after("x_mid", L, 2 * KD))
                sp.dma_start(mc, a["mc"]).then_inc(sem("mc_ld"), 16)
                sp.wait_ge(*after("idx0", L, 1))
                sp.dma_start(idxd[L].rearrange("(p j) o -> p (j o)", p=P), idx0[:]).then_inc(sem("idx_clr"), 16)
                for t in range(TT):
                    sp.wait_ge(*after("hstg", L, t + 1))
                    sp.dma_start(hrow[t * P:(t + 1) * P, :], hstg[t % 2]).then_inc(sem(f"hrow{t % 2}"), 16)
                sp.wait_ge(*after("idx_sc", L, 16 * 2 * TT))
                sp.dma_start(idxs[:], idxd[L].rearrange("(p j) o -> p (j o)", p=P)).then_inc(sem("idxs"), 16)
                sp.wait_ge(*after("plan", L, 1))
                npairs = sp.value_load(ebi[0:1, NBMAX:NBMAX + 1], min_val=NE // 2, max_val=NBMAX // 2)

                last = sp.value_load(ebi[0:1, NBMAX + 1:NBMAX + 2], min_val=NE - 2, max_val=NBMAX - 2)

                def weights(i, b, which):
                    e = sp.value_load(ebi[0:1, bass.ds(2 * i + b, 1)], min_val=0, max_val=NE - 1)
                    w = WE[b]
                    if not isinstance(i, int):
                        sp.wait_ge(sem(f"d_mm{L}" if which else f"g_mm{L}"), 2 * i + b - 1)
                    if which == 0:
                        for n, o in (("expert_w_gate", 0), ("expert_w_up", 256)):
                            dst = w[:, 0:4096].rearrange("p (k n) -> p k n", k=8)[:, :, o:o + 256]
                            src = a[n][L].rearrange("e (p k) n -> e p k n", k=8)[bass.ds(e, 1)].rearrange("e p k n -> (e p) k n")
                            sp.dma_start(dst, src).then_inc(sem(f"wgu{b}_{L}"), 16)
                    else:
                        src = a["expert_w_down"][L].rearrange("e (p k) n -> e p (k n)", k=2)[bass.ds(e, 1)].rearrange("e p n -> (e p) n")
                        sp.dma_start(w[:, 4096:6144], src).then_inc(sem(f"wd{b}_{L}"), 16)

                def stores(i, b, j):
                    reg_wait(sp, sem(f"yev_a{L}"), 2 * i + b + 1)
                    reg_wait(sp, sem(f"yev_v{L}"), 2 * i + b + 1)
                    dst = yrow[bass.ds(j * BLK, BLK), :]
                    sp.dma_start(dst, YB[b]).then_inc(sem(f"yst{b}_{L}"), 16)

                for b in range(2):
                    weights(0, b, 0)
                    weights(0, b, 1)
                with sp.Fori(1, npairs) as i:
                    for b in range(2):
                        weights(i, b, 0)
                    for b in range(2):
                        weights(i, b, 1)
                        stores(i - 1, b, 2 * i + b - 2)
                for b in range(2):
                    sp.wait_ge(sem(f"yev_a{L}"), last + b + 1)
                    sp.wait_ge(sem(f"yev_v{L}"), last + b + 1)
                    sp.dma_start(yrow[bass.ds((last + b) * BLK, BLK), :], YB[b]).then_inc(sem(f"yst{b}_{L}"), 16)

            for t in range(LAT // P):
                sp.wait_ge(sem("o_ev"), t + 1)
                sp.dma_start(a["out"][0, t * P:(t + 1) * P, :], hstg[t % 2]).then_inc(sem(f"o_st{t % 2}"), 16)
            for i in range(2):
                sp.wait_ge(sem(f"o_st{i}"), 16 * (LAT // P // 2))


        @block.tensor
        def _(pe):
            def seg_mm(bank, lhsT, rhs, first, last):
                for s0, s1, _ in SEG:
                    b, c = (bank, 256) if s0 == 0 else (bank + 1, 0)
                    mm = pe.matmul(ps[0:lhsT.shape[1], b, c:c + s1 - s0], lhsT, rhs[:, s0:s1], start=first, stop=last)
                return mm

            def norm_sum(tag, L):
                for m in range(KD):
                    pe.wait_ge(*after(f"sq{tag}", L, m + 1))
                    mm = seg_mm(0, meanw, hT[:, m, :], m == 0, m == KD - 1)
                mm.then_inc(sem(f"ms{tag}"), 1)

            pe.wait_ge(sem("cst_ld"), 48)
            pe.transpose(ps[:, 7, 0:16], ccrow[:], ident[0:16, 0:16]).then_inc(sem("cc_mm"), 1)
            pe.wait_ge(sem("x_ld"), 32)
            for m in range(KD):
                b = 2 * (m % 2)
                if m >= 2:
                    pe.wait_ge(sem("x_cp"), m - 1)
                for t in range(TT):
                    mm = pe.transpose(tokens(b)[:, t * P:(t + 1) * P], xrow[:, t, m * P:(m + 1) * P], ident)
                mm.then_inc(sem("x_mm"), 1)

            for L in range(DEPTH):
                pe.wait_ge(*after("vec_ld", L, 16 * 12))
                if L == 0:
                    pe.wait_ge(sem("cT"), 2)
                pe.transpose(ps[:, 7, 0:V_N], vrow[:], ident[0:V_N, 0:V_N]).then_inc(sem("vec_mm"), 1)
                if L:
                    pe.wait_ge(*after("x_end", L - 1, KD * TT))
                for g in range(NMOD):
                    ring_ready(pe, L, g)
                    if g >= 2:
                        pe.wait_ge(*after("mod_ev", L, g - 1))
                    r = ring[:, (L * USES + g) % 2]
                    for k in range(KD):
                        mm = pe.matmul(ps[0:2, 4 + g % 2, :], cT[:, k:16:8], r[:, k, :], start=k == 0, stop=k == KD - 1)
                    mm.then_inc(sem("mod_mm"), 1)
                pe.wait_ge(*after("mod_ev", L, NMOD))
                for j in range(48):
                    mm = pe.transpose(ps[:, 6, 2 * j:2 * j + 2], mrow[0:2, j * P:(j + 1) * P], ident[0:2, 0:2])
                mm.then_inc(sem("modT_mm"), 1)
                norm_sum("_mix", L)

                pe.wait_ge(*after("h_mix", L, 2 * KD))

                def head_transposes(h):
                    pe.wait_ge(*after("on", L, TT * (h + 1)))
                    for t in range(TT):
                        mm = pe.transpose(pair(6)[:, t * P:(t + 1) * P], oacc[:, t, :], ident)
                    mm.then_inc(sem("oT_mm"), 1)

                def unit_products(u):
                    h, d, n, part = unit(u)
                    pe.wait_ge(*after("ql", L, u + 1))
                    pe.wait_ge(*after("kl", L, u + 1))
                    kslot, qslot = (6, 0) if d == 0 else (0, 6)
                    lk, lq = (0, 1) if d == 0 else (1, 0)
                    for p_ in range(2):
                        p = p_ if d == 0 else 1 - p_
                        tt = part * 2 + p
                        q = 2 * u + p_
                        if q:
                            pe.wait_ge(*after("sc_ev", L, q))
                        elif h:
                            pass
                        for j in range(2):
                            c0 = p * P + j * C
                            for l in range(LEVELS):
                                pe.matmul(ps[j * C:(j + 1) * C, 4, l * C:(l + 1) * C], KL[:, lk + l, c0:c0 + C],
                                          QL[:, lq + l, c0:c0 + C], start=True, stop=True)
                            mm = pe.matmul(ps[j * C:(j + 1) * C, 4, 6 * C:7 * C], kk[:, c0:c0 + C],
                                           hq[:, h, tt * P + j * C:tt * P + (j + 1) * C], start=True, stop=True)
                        mm.then_inc(sem("sc_mm"), 1)
                        if q == 12 * h and h:
                            pe.wait_ge(*after("hgate", L, h))
                        if q:
                            pe.wait_ge(*after("S", L, HEADS_S(u, 2 * p_)))
                        pe.transpose(ps[:, 6, 0:P], KL[:, kslot, p * P:(p + 1) * P], ident).then_inc(sem("kT_mm"), 1)
                        pe.wait_ge(*after("kT", L, q + 1))
                        for j in range(2):
                            mm = pe.matmul(ps[:, 7 - j, P:2 * P], kTs[j * C:(j + 1) * C, :],
                                           hv[j * C:(j + 1) * C, tt, h * P:(h + 1) * P], start=True, stop=True)
                        mm.then_inc(sem("pS_mm"), 1)
                        pe.wait_ge(*after("scT", L, q + 1))
                        if q:
                            pe.wait_ge(*after("o_evh", L, q))
                        for j_ in range(2):
                            j = j_ if d == 0 else 1 - j_
                            c = n * 4 + 2 * p_ + j_
                            pe.matmul(ps[j * C:(j + 1) * C, 5, 0:P], scT[j * C:(j + 1) * C, :],
                                      hv[j * C:(j + 1) * C, tt, h * P:(h + 1) * P], start=True, stop=False)
                            pe.wait_ge(*after("S", L, HEADS_S(u, 2 * p_ + j_)))
                            mm = pe.matmul(ps[j * C:(j + 1) * C, 5, 0:P], QL[:, qslot, p * P + j * C:p * P + (j + 1) * C],
                                           S[:, c % 3, :], start=False, stop=True)
                        mm.then_inc(sem("o_mmh"), 1)

                for k, (g, m) in enumerate(TILES):
                    if m == 0:
                        ring_ready(pe, L, NMOD + g)
                    b = 2 * (k % 2)
                    if k >= 2:
                        pe.wait_ge(*after("proj_ev", L, k - 1))
                    r = ring[:, (L * USES + NMOD + g) % 2]
                    for k8 in range(KD):
                        if GROUPS[g][2]:
                            for t in range(2):
                                mm = pe.matmul(ps[:, b + t, :], hT[:, k8, (2 * m + t) * P:(2 * m + t + 1) * P], r[:, k8, :],
                                               start=k8 == 0, stop=k8 == KD - 1)
                        else:
                            mm = seg_mm(b, r[:, k8, m * P:(m + 1) * P], hT[:, k8, :], k8 == 0, k8 == KD - 1)
                    mm.then_inc(sem("proj_mm"), 1)
                    st = k - TILES_HG
                    if st in UNIT_AT:
                        u = UNIT_AT[st]
                        if u and u % 6 == 0:
                            head_transposes(u // 6 - 1)
                        unit_products(u)
                head_transposes(HEADS - 1)

                pe.wait_ge(*after("rc_ld", L, 32))
                pe.wait_ge(*after("hgate", L, HEADS))
                for h in range(HEADS):
                    pe.wait_ge(*after(f"rqkv{h % 2}", L, 48 * (h // 2 + 1)))
                    qk = rqk[h % 2]
                    if h:
                        pe.wait_ge(*after("rsc_ev", L, 8 * h))
                    for i in range(2):
                        pe.matmul(ps[:, i, :], perm, qk[:, i, CTX:TOK], start=True, stop=True).then_inc(sem("rot_mm"), 1)
                    pe.wait_ge(*after("rot", L, 2 * (h + 1)))
                    for n, (s0, q0, q1) in enumerate(SCORES):
                        i = 8 * h + n
                        if n >= 4 or h:
                            pe.wait_ge(*after("rsc_ev", L, i - 3))
                        pe.matmul(ps[:, n % 4, 0:q1 - q0], qk[:, 1, s0:s0 + P], qk[:, 0, q0:q1],
                                  start=True, stop=True).then_inc(sem("rsc_mm"), 1)
                    for t in range(TT):
                        i = TT * h + t
                        b = 4 + i % 2
                        terms = [n for n, (s0, q0, q1) in enumerate(SCORES) if q0 <= t * P < q1]
                        if i >= 2:
                            pe.wait_ge(*after("ro_ev", L, i - 1))
                        pe.wait_ge(*after("rsc_ev", L, 8 * h + max(terms) + 1))
                        for n in terms:
                            s0, q0, q1 = SCORES[n]
                            o = PT_AT[n] + t * P - q0
                            mm = pe.matmul(ps[:, b, 0:DV], PT[:, o:o + P], rv[h % 2][:, s0 // P, :], start=n == terms[0],
                                           stop=n == terms[-1])
                        mm.then_inc(sem("pv_mm"), 1)
                        if i:
                            ret_transposes(pe, L, i - 1)
                ret_transposes(pe, L, HEADS * TT - 1)

                wohg = hT[:].rearrange("p k t -> p (k t)")[:, 0:4096].rearrange("p (k n) -> p k n", k=4)
                pe.wait_ge(*after("wohg", L, 16))
                pe.wait_ge(*after("rg_done", L, HEADS * TT))
                for m in range(KD):
                    if m % 4 == 0:
                        ring_ready(pe, L, NMOD + len(GROUPS) + m // 4)
                    r = ring[:, (L * USES + NMOD + len(GROUPS) + m // 4) % 2]
                    b = 4 * (m % 2)
                    if m >= 2:
                        pe.wait_ge(*after("y_ev", L, m - 1))
                    for k in range(4):
                        seg_mm(b, wohg[:, k, m * P:(m + 1) * P], hgate[:, k, :], k == 0, k == 3)
                    for k in range(KD):
                        mm = seg_mm(b + 2, r[:, k, (m % 4) * P:(m % 4 + 1) * P], rgate[:, k, :], k == 0, k == KD - 1)
                    mm.then_inc(sem("y_mm"), 1)
                pe.wait_ge(*after("y_ev", L, KD))
                for m in range(KD):
                    if m % 4 == 0:
                        ring_ready(pe, L, NMOD + len(GROUPS) + 2 + m // 4)
                    r = ring[:, (L * USES + NMOD + len(GROUPS) + 2 + m // 4) % 2]
                    b = 2 * (m % 2)
                    if m >= 2:
                        pe.wait_ge(*after("x_mid", L, 2 * (m - 1)))
                    for k in range(KD):
                        mm = seg_mm(b, r[:, k, (m % 4) * P:(m % 4 + 1) * P], merged[:, k, :], k == 0, k == KD - 1)
                    mm.then_inc(sem("out_mm"), 1)

                norm_sum("_ffn", L)
                pe.wait_ge(*after("h_ffn", L, 2 * KD))
                for k in range(KD):
                    mm = seg_mm(2, wrt[:, k, :], hT[:, k, :], k == 0, k == KD - 1)
                mm.then_inc(sem("lg_mm"), 1)
                pe.wait_ge(*after("lgT", L, 1))
                for t in range(TT):
                    mm = pe.transpose(ps[:, 1, t * 36:(t + 1) * 36], lgT[0:36, t * P:(t + 1) * P], ident[0:36, 0:36])
                mm.then_inc(sem("Lg_mm"), 1)
                for t in range(TT):
                    b = 4 + 2 * (t % 2)
                    if t >= 2:
                        pe.wait_ge(*after("hstg", L, t - 1))
                    for k in range(KD):
                        mm = pe.transpose(pair(b)[:, k * P:(k + 1) * P], hT[:, k, t * P:(t + 1) * P], ident)
                    mm.then_inc(sem("hrow_mm"), 1)
                pe.wait_ge(*after("Mb", L, 2))
                for t in range(TT):
                    for t2 in range(t + 1):
                        pe.matmul(ps[:, 2, t * NE:(t + 1) * NE], trib[:, 0:P] if t2 == t else trib[:, P:2 * P], Mb[:, t2, :],
                                  start=t2 == 0, stop=t2 == t)
                for t in range(TT):
                    mm = pe.matmul(ps[:, 2, TT * NE:(TT + 1) * NE], trib[:, P:2 * P], Mb[:, t, :], start=t == 0, stop=t == TT - 1)
                mm.then_inc(sem("rank_mm"), 1)
                pe.wait_ge(*after("plan", L, 1))
                pe.wait_ge(*after("hstg", L, TT))
                npairs = pe.value_load(ebi[0:1, NBMAX:NBMAX + 1], min_val=NE // 2, max_val=NBMAX // 2)

                def blocks(i):
                    first = isinstance(i, int)
                    for b in range(2):
                        j = 2 * i + b
                        reg_wait(pe, sem(f"xg{b}_{L}"), 16 * i + 16, 16)
                        if not first or b:
                            reg_wait(pe, sem(f"xt_a{L}"), j)
                            reg_wait(pe, sem(f"xt_v{L}"), j)
                        for k in range(KD):
                            mm = pe.transpose(pair(0)[:, k * P:(k + 1) * P], XB[b][:, k:D:KD], ident)
                        mm.then_inc(sem(f"xt_mm{L}"), 1)
                    for b in range(2):
                        j = 2 * i + b
                        reg_wait(pe, sem(f"wgu{b}_{L}"), 32 * i + 32, 32)
                        reg_wait(pe, sem(f"xt_a{L}"), j + 1)
                        reg_wait(pe, sem(f"xt_v{L}"), j + 1)
                        for k in range(KD):
                            mm = pe.matmul(ps[:, 2 + b, :], XT[b][:, k, :], WE[b][:, k * 512:(k + 1) * 512], start=k == 0,
                                           stop=k == KD - 1)
                        mm.then_inc(sem(f"g_mm{L}"), 1)
                    for b in range(2):
                        j = 2 * i + b
                        reg_wait(pe, sem(f"hid{L}"), j + 1)
                        for k in range(2):
                            mm = pe.transpose(ps[:, 4, k * P:(k + 1) * P], hid[b][:, k:DE:2], ident)
                        mm.then_inc(sem(f"ht_mm{L}"), 1)
                        reg_wait(pe, sem(f"hidT{L}"), j + 1)
                        reg_wait(pe, sem(f"wd{b}_{L}"), 16 * i + 16, 16)
                        if not first or b:
                            reg_wait(pe, sem(f"yev_a{L}"), j)
                            reg_wait(pe, sem(f"yev_v{L}"), j)
                        for n in range(2):
                            for k in range(2):
                                mm = pe.matmul(ps[:, 5 + n, :], hidT[b][:, k, :],
                                               WE[b][:, 4096 + k * 1024 + n * 512:4096 + k * 1024 + (n + 1) * 512],
                                               start=k == 0, stop=k == 1)
                        mm.then_inc(sem(f"d_mm{L}"), 1)

                blocks(0)
                with pe.Fori(1, npairs) as i:
                    blocks(i)
                for t in range(TT):
                    b = 2 * (t % 2)
                    pe.wait_ge(*after("yc", L, 2 * (t + 1)))
                    if t >= 2:
                        pe.wait_ge(*after("x_end", L, KD * (t - 1)))
                    for m in range(KD):
                        mm = pe.transpose(pair(b)[:, m * P:(m + 1) * P], XB[t % 2][:, m * P:(m + 1) * P], ident)
                    mm.then_inc(sem("yc_mm"), 1)

            norm_sum("_fin", 0)
            pe.wait_ge(sem("h_fin"), 2 * KD)
            for t in range(LAT // P):
                b = 4 + 2 * (t % 2)
                if t >= 2:
                    pe.wait_ge(sem("o_ev"), t - 1)
                for m in range(KD):
                    mm = pe.transpose(pair(b)[:, m * P:(m + 1) * P], hT[:, m, CTX + t * P:CTX + (t + 1) * P], ident)
                mm.then_inc(sem("o_mm"), 1)


        @block.scalar
        def _(act):
            chain = [0]

            def link(ins):
                chain[0] += 1
                ins.then_inc(sem("act_chain"), 1)
                act.wait_ge(sem("act_chain"), chain[0])

            def norm_squares(tag, L):
                for m in range(KD):
                    act.activation(hT[:, m, :], xT[:, m, :], ACT.Square).then_inc(sem(f"sq{tag}"), 1)

            def norm_rstd(tag, L):
                act.wait_ge(*after(f"ms{tag}", L, 1))
                link(act.activation(rstd, tokens(0), ACT.Ln, bias=eps[:]))
                act.activation(rstd, rstd, ACT.Exp, scale=-0.5).then_inc(sem(f"rstd{tag}"), 1)

            def norm_shift(tag, L, shift, T=SEG):
                n = 0
                for m in range(KD):
                    for s0, s1, s in T:
                        n += 1
                        act.wait_ge(*after(f"hm{tag}", L, n))
                        act.activation(hT[:, m, s0:s1], hT[:, m, s0:s1], ACT.Identity,
                                       bias=modT[:, shift * 8 + m, s:s + 1]).then_inc(sem(f"h{tag}"), 1)

            act.wait_ge(sem("init"), 1)
            act.wait_ge(sem("cc_mm"), 1)
            act.activation(cT[:], ps[:, 7, 0:16], ACT.Silu).then_inc(sem("cT"), 1)
            act.wait_ge(sem("cT"), 1)
            act.activation(eps[:], eps[:], ACT.Copy).then_inc(sem("cT"), 1)

            for L in range(DEPTH):
                for g in range(NMOD):
                    act.wait_ge(*after("mod_mm", L, g + 1))
                    act.activation(mrow[0:2, g * 512:(g + 1) * 512], ps[0:2, 4 + g % 2, :], ACT.Copy).then_inc(sem("mod_ev"), 1)
                act.wait_ge(*after("pre", L, 3))
                act.activation(lbm[:, 0, :], lbm[:, 0, :], ACT.Exp).then_inc(sem("pre_a"), 1)
                act.activation(lbm[:, 1, :], lbm[:, 1, :], ACT.Exp).then_inc(sem("pre_a"), 1)
                link(act.activation(dec[:, 1, :], dec[:, 1, :], ACT.Exp, scale=-1.0))
                act.activation(dec[:, 1, :], dec[:, 1, :], ACT.Ln, bias=1.0).then_inc(sem("pre_a"), 1)
                act.wait_ge(sem("x_cp"), KD)
                if L:
                    act.wait_ge(*after("x_end", L - 1, KD * TT))
                norm_squares("_mix", L)
                norm_rstd("_mix", L)
                act.wait_ge(*after("amod", L, 1))
                norm_shift("_mix", L, 0)

                def unit_log(u):
                    act.wait_ge(*after("f", L, u + 1))
                    act.activation(gg[:, :, 1:C + 1], ff.rearrange("p (c t) -> p c t", t=C), ACT.Ln).then_inc(sem("lnf"), 1)

                def unit_exp(u):
                    act.wait_ge(*after("dd", L, u + 1))
                    act.activation(E, E, ACT.Exp).then_inc(sem("ee"), 1)

                def head_norm(h):
                    act.wait_ge(*after("o_evh", L, 12 * (h + 1)))
                    for t in range(TT):
                        link(act.activation(junk, oacc[:, t, :], ACT.Square, accum_out=ss[:, t:t + 1]))
                    link(act.activation(ss[:, 8:8 + TT], ss[:, 0:TT], ACT.Ln, scale=1.0 / P, bias=eps[:]))
                    act.activation(ss[:, 8:8 + TT], ss[:, 8:8 + TT], ACT.Exp, scale=-0.5).then_inc(sem("hr"), 1)

                for k, (g, m) in enumerate(TILES):
                    name, _, tm = GROUPS[g]
                    b = 2 * (k % 2)
                    st = k - TILES_HG
                    if st == 0:
                        if L == 0:
                            act.wait_ge(sem("yclr"), 16 * (NBMAX - NE))
                        unit_log(0)
                        unit_exp(0)
                    act.wait_ge(*after("proj_mm", L, k + 1))
                    src = tokens(b)
                    if name in ("ff", "fb"):
                        ins = act.activation(sig[name == "fb"][:, m, :], src, ACT.Sigmoid)
                    elif name == "q":
                        ins = act.activation(hq[:, m, :], src, ACT.Silu)
                    elif name == "g":
                        ins = act.activation(hgate[:, m, :], src, ACT.Silu)
                    elif name == "v":
                        ins = act.activation(hv[:, 2 * m:2 * m + 2, :], ps[:, b:b + 2, :], ACT.Copy)
                    else:
                        if st >= 2:
                            act.wait_ge(*after(f"spill{st % 2}", L, 16 * (st // 2)))
                        fn = {"rg": ACT.Silu, "ga": ACT.Sigmoid, "gb": ACT.Sigmoid}.get(name[:2], ACT.Copy)
                        if tm:
                            ins = act.activation(stage[st % 2], pair(b), fn)
                        else:
                            ins = act.activation(stage[st % 2][:, 0:TOK], src, fn, scale=QSCALE if name == "rq" else 1.0)
                    ins.then_inc(sem("proj_ev"), 1)
                    if st in UNIT_AT:
                        u = UNIT_AT[st]
                        if u + 1 < UNITS:
                            unit_log(u + 1)
                            unit_exp(u + 1)
                        if u % 6 == 5:
                            head_norm(u // 6)

                act.wait_ge(*after("rc_ld", L, 32))
                act.wait_ge(*after("hgate", L, HEADS))
                for h in range(HEADS):
                    lf, lb = dec[:, 3, h:h + 1], dec[:, 3, 4 + h:5 + h]
                    if h:
                        act.wait_ge(*after("rsc_ev", L, 8 * h))
                    act.activation(Wd, XP, ACT.Exp, scale=lf).then_inc(sem("dt"), 1)
                    act.activation(wtmp, XN, ACT.Exp, scale=lb).then_inc(sem("dt"), 1)
                    act.activation(Dc, XX, ACT.Exp, scale=lf, bias=dec[:, 4, h:h + 1]).then_inc(sem("dt"), 1)
                    act.activation(dtmp, XX, ACT.Exp, scale=dec[:, 5, 4 + h:5 + h], bias=dec[:, 4, 4 + h:5 + h]).then_inc(sem("dt"), 1)
                    for t in range(TT):
                        i = TT * h + t
                        act.wait_ge(*after("rvar", L, i + 1))
                        r = rst[:, 32 + 4 * (i % 2):33 + 4 * (i % 2)]
                        link(act.activation(r, rst[:, 17 + 4 * (i % 2):18 + 4 * (i % 2)], ACT.Ln, bias=eps[:]))
                        act.activation(r, r, ACT.Exp, scale=-0.5).then_inc(sem("rr"), 1)

                act.wait_ge(*after("x_mid", L, 2 * KD))
                norm_squares("_ffn", L)
                norm_rstd("_ffn", L)
                norm_shift("_ffn", L, 3)
                act.wait_ge(*after("lg_mm", L, 1))
                act.activation(lgT[0:36, :], tokens(2)[0:36, :], ACT.Identity, bias=vec[0:36, V_RB:V_RB + 1]).then_inc(sem("lgT"), 1)
                for t in range(TT):
                    act.wait_ge(*after("hrow_mm", L, t + 1))
                    if t >= 2:
                        act.wait_ge(*after(f"hrow{t % 2}", L, 16 * (t // 2)))
                    act.activation(hstg[t % 2], pair(4 + 2 * (t % 2)), ACT.Copy).then_inc(sem("hstg"), 1)
                act.wait_ge(*after("gd", L, 2))
                act.activation(ro[:, 0:TT * 4], ro[:, 0:TT * 4], ACT.Exp).then_inc(sem("gx"), 1)
                act.activation(ro[:, 32:32 + TT], ro[:, 32:32 + TT], ACT.Exp).then_inc(sem("gx"), 1)
                act.wait_ge(*after("plan", L, 1))
                npairs = act.value_load(ebi[0:1, NBMAX:NBMAX + 1], min_val=NE // 2, max_val=NBMAX // 2)

                def blocks(i):
                    first = isinstance(i, int)
                    for b in range(2):
                        j = 2 * i + b
                        if not first:
                            reg_wait(act, sem(f"g_mm{L}"), j - 1)
                        reg_wait(act, sem(f"xt_mm{L}"), j + 1)
                        act.activation(XT[b][:, 0:4, :], ps[:, 0, :].rearrange("p (k t) -> p k t", k=4), ACT.Copy).then_inc(sem(f"xt_a{L}"), 1)
                    for b in range(2):
                        j = 2 * i + b
                        if not first:
                            reg_wait(act, sem(f"hid{L}"), j - 1)
                        reg_wait(act, sem(f"g_mm{L}"), j + 1)
                        act.activation(sg[b], ps[:, 2 + b, 0:DE], ACT.Silu).then_inc(sem(f"sg{L}"), 1)
                    for b in range(2):
                        j = 2 * i + b
                        if not first:
                            reg_wait(act, sem(f"yst{b}_{L}"), 16 * i, 16)
                        reg_wait(act, sem(f"d_mm{L}"), j + 1)
                        act.activation(YB[b][:, 0:512], ps[:, 5, :], ACT.Copy).then_inc(sem(f"yev_a{L}"), 1)

                blocks(0)
                with act.Fori(1, npairs) as i:
                    blocks(i)
            act.wait_ge(*after("x_end", DEPTH - 1, KD * TT))
            norm_squares("_fin", 0)
            norm_rstd("_fin", 0)
            for t in range(LAT // P):
                act.wait_ge(sem("o_mm"), t + 1)
                if t >= 2:
                    act.wait_ge(sem(f"o_st{t % 2}"), 16 * (t // 2))
                act.activation(hstg[t % 2], pair(4 + 2 * (t % 2)), ACT.Copy).then_inc(sem("o_ev"), 1)

        @block.vector
        def _(dve):
            chain = [0]

            def link(ins):
                chain[0] += 1
                ins.then_inc(sem("dve_chain"), 1)
                dve.wait_ge(sem("dve_chain"), chain[0])

            def norm_scale(tag, L, w):
                dve.wait_ge(*after(f"rstd{tag}", L, 1))
                for m in range(KD):
                    for s0, s1, s in SEG:
                        dve.scalar_tensor_tensor(out=hT[:, m, s0:s1], in0=xT[:, m, s0:s1], scalar=w(m, s),
                                                 in1=rstd[:, s0:s1], op0=ALU.mult, op1=ALU.mult).then_inc(sem(f"hm{tag}"), 1)

            dve.memset(eps[:], EPS).then_inc(sem("dve_chain"), 1)
            chain[0] += 1
            link(dve.memset(gg, 0.0))
            dve.memset(vrow[:], 0.0).then_inc(sem("init"), 1)
            for m in range(KD):
                dve.wait_ge(sem("x_mm"), m + 1)
                dve.tensor_copy(xT[:, m, :], tokens(2 * (m % 2))).then_inc(sem("x_cp"), 1)

            for L in range(DEPTH):
                dve.wait_ge(*after("vec_mm", L, 1))
                link(dve.tensor_copy(vec[:], ps[:, 7, 0:V_N]))
                lg = vec[:, V_LB:V_LB + 16].rearrange("p (d l h) -> p l d h", d=2, l=2)
                l0, l1, mx, t1 = [lbm[:, i, :].rearrange("p (d h) -> p d h", d=2) for i in range(4)]
                link(dve.tensor_tensor(mx, lg[:, 0], lg[:, 1], ALU.max))
                dve.tensor_tensor(l0, lg[:, 0], mx, ALU.subtract).then_inc(sem("pre"), 1)
                dve.tensor_tensor(l1, lg[:, 1], mx, ALU.subtract).then_inc(sem("pre"), 1)
                link(dve.tensor_scalar(dec[:, 2, :], dec[:, 0, :], -1.0, None, ALU.mult))
                dve.tensor_tensor(dec[:, 1, :], dec[:, 0, :], dec[:, 2, :], ALU.max).then_inc(sem("pre"), 1)
                dve.wait_ge(*after("pre_a", L, 3))
                l0, l1, lb, om = lbm[:, 0, :], lbm[:, 1, :], lbm[:, 2, :], lbm[:, 3, :]
                link(dve.tensor_tensor(lb, l0, l1, ALU.add))
                link(dve.reciprocal(om, lb))
                if L == 0:
                    link(dve.memset(lb, 0.0))
                else:
                    link(dve.tensor_tensor(l0, l0, om, ALU.mult))
                    link(dve.tensor_tensor(l1, l1, om, ALU.mult))
                    link(dve.tensor_tensor(lb, l0, l1, ALU.add))
                    link(dve.tensor_tensor(lb, lb, l0, ALU.subtract))
                    link(dve.tensor_scalar(lb, lb, 0.0, 1.0 - 1e-6, ALU.max, ALU.min))
                link(dve.tensor_scalar(om, lb, -1.0, 1.0, ALU.mult, ALU.add))
                link(dve.tensor_scalar(dec[:, 2, :], dec[:, 0, :], 0.0, None, ALU.min))
                link(dve.tensor_tensor(dec[:, 3, :], dec[:, 2, :], dec[:, 1, :], ALU.subtract))
                link(dve.tensor_scalar(dec[:, 4, 0:4], dec[:, 3, 0:4], float(CTX), None, ALU.mult))
                link(dve.tensor_scalar(dec[:, 4, 4:8], dec[:, 3, 4:8], float(LAT), None, ALU.mult))
                link(dve.tensor_scalar(dec[:, 5, :], dec[:, 3, :], -1.0, None, ALU.mult))
                dve.wait_ge(*after("modT_mm", L, 1))
                link(dve.tensor_tensor(modT[:], ps[:, 6, 0:96].rearrange("p (j s) -> p j s", s=2),
                                       vec[:, V_BMOD:V_BMOD + 48].unsqueeze(2).to_broadcast([P, 48, 2]), ALU.add))
                for i, (v0, sc) in enumerate(((V_MIX, 1), (V_FFN, 4))):
                    link(dve.tensor_scalar(amod[:, i], modT[:, sc * 8:sc * 8 + 8, :], 1.0, None, ALU.add))
                    ins = dve.tensor_tensor(amod[:, i], amod[:, i], vec[:, v0:v0 + 8].unsqueeze(2).to_broadcast([P, 8, 2]), ALU.mult)
                    if i == 0:
                        link(ins)
                    else:
                        ins.then_inc(sem("amod"), 1)
                dve.wait_ge(*after("amod", L, 1))
                norm_scale("_mix", L, lambda m, s: amod[:, 0, m, s:s + 1])

                link(dve.memset(keep, 1.0))
                link(dve.memset(gg, 0.0))
                link(dve.memset(keep[:, :, 0:1], 0.0))

                def forget(u):
                    h, d, n, part = unit(u)
                    x = sig[d][:, h, part * PART:(part + 1) * PART]
                    lb, om = lbm[:, 2, d * 4 + h:d * 4 + h + 1], lbm[:, 3, d * 4 + h:d * 4 + h + 1]
                    dve.tensor_scalar(kk, x, -1.0, 1.0, ALU.mult, ALU.add).then_inc(sem("k1"), 1)
                    link(dve.tensor_scalar(ff, x, om, lb, ALU.mult, ALU.add))
                    dve.tensor_scalar(ff, ff, F_MIN, None, ALU.max).then_inc(sem("f"), 1)
                    dve.wait_ge(*after("k1", L, u + 1))
                    dve.tensor_scalar(kk, kk, om, None, ALU.mult).then_inc(sem("k"), 1)

                def differences(u):
                    h, d, n, part = unit(u)
                    off = 1 - d
                    dve.wait_ge(*after("lnf", L, u + 1))
                    link(dve.tensor_tensor_scan(Pc.rearrange("p c t -> p (c t)"), keep.rearrange("p c t -> p (c t)"),
                                                gg.rearrange("p c t -> p (c t)"), 0.0, ALU.mult, ALU.add))
                    if u:
                        dve.wait_ge(*after("kl", L, u))
                    for l in range(LEVELS):
                        w = C >> l
                        n_ = C // w
                        x = Pc[:, :, off:off + C].rearrange("p c (n w) -> p c n w", w=w)
                        mid = Pc[:, :, w // 2:C:w].unsqueeze(3).to_broadcast([P, 4, n_, w // 2])
                        e = E[:, 1 + l, :].rearrange("p (c n w) -> p c n w", c=4, w=w)
                        dve.tensor_tensor(e[:, :, :, w // 2:w], x[:, :, :, w // 2:w], mid, ALU.subtract)
                        dve.tensor_tensor(e[:, :, :, 0:w // 2], mid, x[:, :, :, 0:w // 2], ALU.subtract)
                    last = Pc[:, :, C:C + 1].to_broadcast([P, 4, C])
                    e = [E[:, i, :].rearrange("p (c t) -> p c t", t=C) for i in (0, 7)]
                    dve.tensor_copy(e[0], Pc[:, :, off:off + C])
                    dve.tensor_tensor(e[1], last, Pc[:, :, off:off + C], ALU.subtract).then_inc(sem("dd"), 1)

                def queries(u):
                    h, d, n, part = unit(u)
                    dve.wait_ge(*after("ee", L, u + 1))
                    q = hq[:, h, part * PART:(part + 1) * PART].unsqueeze(1).to_broadcast([P, 7, PART])
                    dve.scalar_tensor_tensor(out=QL, in0=E[:, d:d + 7, :], scalar=QSCALE, in1=q, op0=ALU.mult,
                                             op1=ALU.mult).then_inc(sem("ql"), 1)

                def outputs(u):
                    h, d, n, part = unit(u)
                    s0 = 12 * (2 * h + d) + 2 * h + d
                    if n == 0:
                        if u:
                            dve.wait_ge(*after("S", L, 13 * (2 * h + d)))
                        dve.memset(S[:, 0, :], 0.0).then_inc(sem("S"), 1)
                    for p_ in range(2):
                        p = p_ if d == 0 else 1 - p_
                        tt = part * 2 + p
                        q = 2 * u + p_
                        dve.wait_ge(*after("sc_mm", L, q + 1))
                        dve.tensor_tensor(msk, ps[:, 4, 0:7 * C].rearrange("p (l t) -> p l t", l=7), masks[d],
                                          ALU.mult).then_inc(sem("sc_ev"), 1)
                        dve.wait_ge(*after("kT_mm", L, q + 1))
                        dve.tensor_copy(kTs, ps[:, 6, 0:P]).then_inc(sem("kT"), 1)
                        dve.wait_ge(*after("sc_ev", L, q + 1))
                        dve.tensor_reduce(scT, msk.rearrange("p l t -> p t l"), AX.X, ALU.add).then_inc(sem("scT"), 1)
                        dve.wait_ge(*after("pS_mm", L, q + 1))
                        for j_ in range(2):
                            j = j_ if d == 0 else 1 - j_
                            c = n * 4 + 2 * p_ + j_
                            c0 = p * P + j * C
                            x = E[:, 0, c0 + C - 1:c0 + C] if d == 0 else E[:, 7, c0:c0 + 1]
                            dve.wait_ge(*after("S", L, HEADS_S(u, 2 * p_ + j_)))
                            dve.scalar_tensor_tensor(out=S[:, (c + 1) % 3, :], in0=S[:, c % 3, :], scalar=x,
                                                     in1=ps[:, 7 - j, P:2 * P], op0=ALU.mult, op1=ALU.add).then_inc(sem("S"), 1)
                        dve.wait_ge(*after("o_mmh", L, q + 1))
                        if d == 0:
                            dve.tensor_copy(oacc[:, tt, :], ps[:, 5, 0:P]).then_inc(sem("o_evh"), 1)
                        else:
                            dve.tensor_tensor(oacc[:, tt, :], ps[:, 5, 0:P], oacc[:, tt, :], ALU.add).then_inc(sem("o_evh"), 1)

                dve.wait_ge(*after("proj_ev", L, TILES_HG))
                forget(0)
                differences(0)
                for k, (g, m) in enumerate(TILES):
                    st = k - TILES_HG
                    if st not in UNIT_AT:
                        continue
                    u = UNIT_AT[st]
                    queries(u)
                    if u and u % 6 == 0:
                        head_gate(dve, L, u // 6 - 1)
                    outputs(u)
                    if u + 1 < UNITS:
                        forget(u + 1)
                        differences(u + 1)
                    if u % 6 == 5:
                        dve.wait_ge(*after("hr", L, u // 6 + 1))
                        for t in range(TT):
                            dve.tensor_scalar(oacc[:, t, :], oacc[:, t, :], ss[:, 8 + t:9 + t], None, ALU.mult).then_inc(sem("on"), 1)
                head_gate(dve, L, HEADS - 1)

                for h in range(HEADS):
                    dve.wait_ge(*after(f"rqkv{h % 2}", L, 48 * (h // 2 + 1)))
                    dve.wait_ge(*after("rc_ld", L, 32))
                    for i in range(2):
                        x = rqk[h % 2][:, i, CTX:TOK]
                        dve.wait_ge(*after("rot_mm", L, 2 * h + i + 1))
                        if i or h or L:
                            dve.wait_ge(*after("rot", L, 2 * h + i))
                        link(dve.tensor_tensor(rtmp, ps[:, i, :], sinT, ALU.mult))
                        link(dve.tensor_tensor(x, x, cosT, ALU.mult))
                        dve.tensor_tensor(x, x, rtmp, ALU.add).then_inc(sem("rot"), 1)
                    dve.wait_ge(*after("rot", L, 2 * h + 2))
                    dve.wait_ge(*after("dt", L, 4 * (h + 1)))
                    link(dve.tensor_tensor(Wd, Wd, wtmp, ALU.mult))
                    link(dve.tensor_tensor(Wd[:, 384:512], Wd[:, 384:512], ident, ALU.add))
                    link(dve.tensor_tensor(Dc, Dc, dtmp, ALU.add))

                    def scores(n):
                        s0, q0, q1 = SCORES[n]
                        i = 8 * h + n
                        dve.wait_ge(*after("rsc_mm", L, i + 1))
                        cross = s0 < CTX <= q0
                        tab = Dc if cross else Wd
                        y = (q0 - CTX if cross else q0) - s0 + 384
                        if h:
                            dve.wait_ge(*after("pv_mm", L, TT * h))
                        dve.tensor_tensor(PT[:, PT_AT[n]:PT_AT[n] + q1 - q0], ps[:, n % 4, 0:q1 - q0], tab[:, y:y + q1 - q0],
                                          ALU.mult).then_inc(sem("rsc_ev"), 1)

                    def ret_norm(i):
                        b = 4 + i % 2
                        st6 = rst[:, 6 * (i % 2):6 * (i % 2) + 6]
                        mv = rst[:, 16 + 4 * (i % 2):18 + 4 * (i % 2)]
                        dve.wait_ge(*after("pv_mm", L, i + 1))
                        link(dve.bn_stats(st6, ps[:, b, 0:DV]))
                        dve.bn_aggr(mv, st6).then_inc(sem("rvar"), 1)
                        dve.wait_ge(*after("rr", L, i + 1))
                        if i >= 2:
                            dve.wait_ge(*after("roT_mm", L, i - 1))
                        dve.tensor_scalar(on[:, i % 2, :], ps[:, b, 0:DV], mv[:, 0:1], rst[:, 32 + 4 * (i % 2):33 + 4 * (i % 2)],
                                          ALU.subtract, ALU.mult).then_inc(sem("ro_ev"), 1)

                    for n in range(8):
                        scores(n)
                    for t in range(TT):
                        ret_norm(TT * h + t)
                        if TT * h + t:
                            ret_gate(dve, L, TT * h + t - 1)
                ret_gate(dve, L, HEADS * TT - 1)

                for m in range(KD):
                    b = 4 * (m % 2)
                    dve.wait_ge(*after("y_mm", L, m + 1))
                    dve.wait_ge(*after(f"gab{m % 2}", L, 32 * (m // 2 + 1)))
                    if m or L:
                        dve.wait_ge(*after("y_ev", L, m))
                    link(dve.tensor_tensor(ytmp, tokens(b), gab[m % 2][:, 0], ALU.mult))
                    link(dve.tensor_tensor(merged[:, m, :], tokens(b + 2), gab[m % 2][:, 1], ALU.mult))
                    dve.tensor_tensor(merged[:, m, :], merged[:, m, :], ytmp, ALU.add).then_inc(sem("y_ev"), 1)
                for m in range(KD):
                    dve.wait_ge(*after("out_mm", L, m + 1))
                    for s0, s1, s in SEG:
                        dve.scalar_tensor_tensor(out=xT[:, m, s0:s1], in0=tokens(2 * (m % 2))[:, s0:s1], scalar=modT[:, 16 + m, s:s + 1],
                                                 in1=xT[:, m, s0:s1], op0=ALU.mult, op1=ALU.add).then_inc(sem("x_mid"), 1)

                norm_scale("_ffn", L, lambda m, s: amod[:, 1, m, s:s + 1])
                dve.wait_ge(*after("mc_ld", L, 16))
                dve.wait_ge(*after("Lg_mm", L, 1))
                link(dve.tensor_copy(Lg, ps[:, 1, 0:TT * 36].rearrange("p (t e) -> p t e", e=36)))

                def r_(off, n, **kw):
                    v = ro[:, off:off + n]
                    return v.rearrange("p (a b) -> p a b", **kw) if kw else v

                gx, d21 = r_(0, 24, a=TT), r_(32, TT)
                pad, mx8, mx8e = r_(64, 48, a=TT), r_(112, 48, a=TT), r_(160, 48, a=TT)
                ein, idf = r_(208, 48, a=TT), r_(256, 96, a=2 * TT)
                gs, grp, e12, w12 = r_(352, TT), r_(360, TT), r_(368, 2 * TT, a=2), r_(380, 2 * TT, a=2)
                tmp4 = r_(400, TT * NE)
                O1, O2 = r_(600, TT * NE, a=TT), r_(800, TT * NE, a=TT)
                rank, cnt = r_(1000, TT * NE, a=TT), r_(1192, NE)
                nb, inc, bs = r_(1224, NE), r_(1256, NE), r_(1288, NE)
                rk, bb, rj, t6 = r_(1320, 2 * TT, a=2), r_(1332, 2 * TT, a=2), r_(1344, 2 * TT, a=2), r_(1356, 2 * TT, a=2)
                one32 = r_(1370, NE)
                sl = r_(1410, 4 * TT, a=4)
                ebf = r_(1440, NBMAX + 2)
                link(dve.memset(pad, -3.0e38))
                link(dve.tensor_copy(pad[:, :, 0:NG], Lg[:, :, 0:NG]))
                for t in range(TT):
                    ins = dve.max(mx8[:, t, :], pad[:, t, :])
                    ins.then_inc(sem("m8"), 1)
                dve.wait_ge(*after("m8", L, TT))
                for t in range(TT):
                    dve.max_index(u8[:, t, :], mx8[:, t, :], pad[:, t, :]).then_inc(sem("m8"), 1)
                dve.tensor_tensor(gx, Lg[:, :, 0:NG], mx8[:, :, 0:1].to_broadcast([P, TT, NG]), ALU.subtract).then_inc(sem("gd"), 1)
                dve.wait_ge(*after("m8", L, 2 * TT))
                link(dve.tensor_copy(grp, u8[:, 0:TT, 0]))
                link(dve.tensor_tensor(r_(400, TT * NG, a=TT), io[:, 0:NG].unsqueeze(1).to_broadcast([P, TT, NG]),
                                       grp.unsqueeze(2).to_broadcast([P, TT, NG]), ALU.is_equal))
                for g in range(NG):
                    oh = r_(400, TT * NG, a=TT)[:, :, g:g + 1].to_broadcast([P, TT, NPG])
                    dst = ein if g == 0 else r_(440, TT * NPG, a=TT)
                    link(dve.tensor_tensor(dst, Lg[:, :, NG + g * NPG:NG + (g + 1) * NPG], oh, ALU.mult))
                    if g:
                        link(dve.tensor_tensor(ein, ein, r_(440, TT * NPG, a=TT), ALU.add))
                for t in range(TT):
                    dve.max(mx8e[:, t, :], ein[:, t, :]).then_inc(sem("m8"), 1)
                dve.wait_ge(*after("m8", L, 3 * TT))
                for t in range(TT):
                    dve.max_index(u8[:, TT + t, :], mx8e[:, t, :], ein[:, t, :]).then_inc(sem("m8"), 1)
                dve.tensor_tensor(d21, mx8e[:, :, 1], mx8e[:, :, 0], ALU.subtract).then_inc(sem("gd"), 1)
                dve.wait_ge(*after("m8", L, 4 * TT))
                link(dve.tensor_copy(e12, u8[:, TT:2 * TT, 0:2].rearrange("p t k -> p k t")))
                link(dve.tensor_scalar(t6[:, 0, :], grp, float(NPG), None, ALU.mult))
                link(dve.tensor_tensor(e12, e12, t6[:, 0:1, :].to_broadcast([P, 2, TT]), ALU.add))
                for i, O in enumerate((O1, O2)):
                    link(dve.tensor_tensor(O, io.unsqueeze(1).to_broadcast([P, TT, NE]),
                                           e12[:, i, :].unsqueeze(2).to_broadcast([P, TT, NE]), ALU.is_equal))
                dve.tensor_tensor(Mb[:], O1, O2, ALU.add).then_inc(sem("Mb"), 1)
                link(dve.tensor_copy(trib[:, 0:P], tri))
                dve.memset(trib[:, P:2 * P], 1.0).then_inc(sem("Mb"), 1)
                dve.wait_ge(*after("gx", L, 2))
                link(dve.tensor_reduce(gs, gx, AX.X, ALU.add))
                link(dve.tensor_scalar(w12[:, 0, :], d21, 1.0, None, ALU.add))
                link(dve.tensor_tensor(gs, gs, w12[:, 0, :], ALU.mult))
                link(dve.reciprocal(w12[:, 0, :], gs))
                link(dve.tensor_tensor(w12[:, 1, :], w12[:, 0, :], d21, ALU.mult))
                dve.wait_ge(*after("rank_mm", L, 1))
                link(dve.tensor_copy(rank, ps[:, 2, 0:TT * NE].rearrange("p (t e) -> p t e", e=NE)))
                link(dve.tensor_copy(cnt, ps[:, 2, TT * NE:(TT + 1) * NE]))
                link(dve.memset(nb, 1.0))
                link(dve.memset(one32, 1.0))
                for n in range(1, TT):
                    link(dve.tensor_scalar(bs, cnt, float(n * BLK), None, ALU.is_gt))
                    link(dve.tensor_tensor(nb, nb, bs, ALU.add))
                link(dve.tensor_tensor_scan(inc, one32, nb, 0.0, ALU.mult, ALU.add))
                link(dve.tensor_tensor(bs, inc, nb, ALU.subtract))
                for c0 in range(0, NBMAX, NBMAX // 2):
                    n2 = NBMAX // 2
                    jt = r_(1500, n2 * NE, a=n2)
                    link(dve.tensor_tensor(jt, jm[:, c0:c0 + n2, :], inc.unsqueeze(1).to_broadcast([P, n2, NE]), ALU.is_ge))
                    link(dve.tensor_reduce(ebf[:, c0:c0 + n2], jt, AX.X, ALU.add))
                link(dve.tensor_scalar(ebf[:, 0:NBMAX], ebf[:, 0:NBMAX], float(NE - 1), None, ALU.min))
                hb = mc[:, P + NBMAX * NE + NE:P + NBMAX * NE + NE + NBMAX]
                link(dve.tensor_tensor(hb, hb, inc[:, NE - 1:NE].to_broadcast([P, NBMAX]), ALU.is_lt))
                link(dve.tensor_reduce(ebf[:, NBMAX:NBMAX + 1], hb[:, 0:NBMAX:2], AX.X, ALU.add))
                link(dve.tensor_scalar(ebf[:, NBMAX + 1:NBMAX + 2], ebf[:, NBMAX:NBMAX + 1], 2.0, -2.0, ALU.mult, ALU.add))
                dve.tensor_copy(ebi[0:1, :], ebf[0:1, :]).then_inc(sem("plan"), 1)
                for i, O in enumerate((O1, O2)):
                    for dst, tab in ((rk, rank), (bb, bs.unsqueeze(1).to_broadcast([P, TT, NE]))):
                        t4 = tmp4.rearrange("p (a b) -> p a b", a=TT)
                        link(dve.tensor_tensor(t4, O, tab, ALU.mult))
                        link(dve.tensor_reduce(dst[:, i, :], t4, AX.X, ALU.add))
                link(dve.tensor_scalar(rj, rk, float(BLK), None, ALU.is_ge))
                for n in range(2, TT):
                    link(dve.tensor_scalar(t6, rk, float(n * BLK), None, ALU.is_ge))
                    link(dve.tensor_tensor(rj, rj, t6, ALU.add))
                link(dve.tensor_tensor(bb, bb, rj, ALU.add))
                link(dve.tensor_scalar(rj, rj, float(-BLK), None, ALU.mult))
                link(dve.tensor_tensor(rk, rk, rj, ALU.add))
                link(dve.tensor_scalar(t6, bb, float(BLK), None, ALU.mult))
                link(dve.tensor_tensor(sl[:, 0:2, :], t6, rk, ALU.add))
                link(dve.tensor_scalar(t6, rk, float(NBMAX), None, ALU.mult))
                link(dve.tensor_tensor(sl[:, 2:4, :], t6, bb, ALU.add))
                dve.tensor_copy(slots[:], sl).then_inc(sem("slots"), 1)
                npairs = dve.value_load(ebi[0:1, NBMAX:NBMAX + 1], min_val=NE // 2, max_val=NBMAX // 2)

                def blocks(i):
                    first = isinstance(i, int)
                    for b in range(2):
                        j = 2 * i + b
                        if not first:
                            reg_wait(dve, sem(f"g_mm{L}"), j - 1)
                        reg_wait(dve, sem(f"xt_mm{L}"), j + 1)
                        dve.tensor_copy(XT[b][:, 4:8, :], ps[:, 1, :].rearrange("p (k t) -> p k t", k=4)).then_inc(sem(f"xt_v{L}"), 1)
                    for b in range(2):
                        j = 2 * i + b
                        reg_wait(dve, sem(f"sg{L}"), j + 1)
                        if not first:
                            reg_wait(dve, sem(f"ht_mm{L}"), j - 1)
                        dve.tensor_tensor(hid[b], ps[:, 2 + b, DE:2 * DE], sg[b], ALU.mult).then_inc(sem(f"hid{L}"), 1)
                    for b in range(2):
                        j = 2 * i + b
                        reg_wait(dve, sem(f"ht_mm{L}"), j + 1)
                        dve.tensor_copy(hidT[b], ps[:, 4, 0:256].rearrange("p (k t) -> p k t", k=2)).then_inc(sem(f"hidT{L}"), 1)
                        if not first:
                            reg_wait(dve, sem(f"yst{b}_{L}"), 16 * i, 16)
                        reg_wait(dve, sem(f"d_mm{L}"), j + 1)
                        dve.tensor_copy(YB[b][:, 512:1024], ps[:, 6, :]).then_inc(sem(f"yev_v{L}"), 1)

                blocks(0)
                with dve.Fori(1, npairs) as i:
                    blocks(i)
                for t in range(TT):
                    s = 1 if t < CTX // P else 0
                    dve.wait_ge(*after(f"yg{t % 2}", L, 32 * (t // 2 + 1)))
                    if t >= 2:
                        dve.wait_ge(*after("yc_mm", L, t - 1))
                    y = WE[t % 2]
                    dve.tensor_scalar(XB[t % 2], y[:, 0:D], w12[:, 0, t:t + 1], None, ALU.mult).then_inc(sem("yc"), 1)
                    dve.wait_ge(*after("yc", L, 2 * t + 1))
                    dve.scalar_tensor_tensor(out=XB[t % 2], in0=y[:, D:2 * D], scalar=w12[:, 1, t:t + 1], in1=XB[t % 2],
                                             op0=ALU.mult, op1=ALU.add).then_inc(sem("yc"), 1)
                    dve.wait_ge(*after("yc_mm", L, t + 1))
                    for m in range(KD):
                        x = xT[:, m, t * P:(t + 1) * P]
                        dve.scalar_tensor_tensor(out=x, in0=pair(2 * (t % 2))[:, m * P:(m + 1) * P], scalar=modT[:, 40 + m, s:s + 1],
                                                 in1=x, op0=ALU.mult, op1=ALU.add).then_inc(sem("x_end"), 1)
                dve.wait_ge(*after("x_end", L, KD * TT))
                dve.memset(gg[:, 0, 0:1], 0.0).then_inc(sem("final_vec"), 1)
                dve.wait_ge(*after("final_vec", L, 1))

            dve.wait_ge(sem("rstd_fin"), 1)
            for m in range(KD):
                for s0, s1, s in SEG:
                    dve.scalar_tensor_tensor(out=hT[:, m, s0:s1], in0=xT[:, m, s0:s1], scalar=vec[:, V_FIN + m:V_FIN + m + 1],
                                             in1=rstd[:, s0:s1], op0=ALU.mult, op1=ALU.mult).then_inc(sem("h_fin"), 1)


        @block.gpsimd
        def _(pool):
            def after_wait(s, v, c=1):
                pool.wait_ge(s, v)
                pool.tensor_tensor(nil[:, c:c + 1], nil[:, 0:1], nil[:, 0:1], ALU.add)

            pool.memset(nil[:], 0.0).then_inc(sem("clr"), 1)
            pool.memset(stage[0], 0.0).then_inc(sem("clr"), 1)
            pool.wait_ge(sem("clr"), 2)
            for j in range(NE, NBMAX):
                pool.dma_start(yrow[j * BLK:(j + 1) * BLK, :], stage[0]).then_inc(sem("yclr"), 16)
            pool.iota(tokid[:], pattern=[[P, TT]], base=0, channel_multiplier=1).then_inc(sem("tokid"), 1)
            for L in range(DEPTH):
                pool.memset(idx0[:], 0).then_inc(sem("idx0"), 1)
                for u in range(UNITS):
                    h, d, n, part = unit(u)
                    pool.wait_ge(*after("ee", L, u + 1))
                    pool.wait_ge(*after("k", L, u + 1))
                    if u:
                        pool.wait_ge(*after("o_mmh", L, 2 * u))
                    pool.tensor_tensor(KL, E[:, 1 - d:8 - d, :], kk.unsqueeze(1).to_broadcast([P, 7, PART]),
                                       ALU.mult).then_inc(sem("kl"), 1)
                pool.wait_ge(*after("slots", L, 1))
                pool.wait_ge(*after("idx_clr", L, 16))
                pool.wait_ge(sem("tokid"), 1)
                for t in range(TT):
                    for i in range(2):
                        pool.indirect_dma_start(
                            out=idxd[L], out_offset=bass.IndirectOffsetOnAxis(ap=slots[:, 2 + i, t:t + 1], axis=0),
                            in_=tokid[:, t:t + 1], in_offset=None).then_inc(sem("idx_sc"), 16)
                pool.wait_ge(*after("idxs", L, 16))
                for i in range(2):
                    pool.wait_ge(*after(f"hrow{i}", L, 16 * (TT // 2)))
                npairs = pool.value_load(ebi[0:1, NBMAX:NBMAX + 1], min_val=NE // 2, max_val=NBMAX // 2)

                def blocks(i):
                    for b in range(2):
                        j = 2 * i + b
                        if not isinstance(i, int):
                            reg_wait(pool, sem(f"xt_mm{L}"), j - 1)
                        pool.tensor_copy(idxc[:, b:b + 1], idxs[:, bass.ds(j, 1)]).then_inc(sem(f"idxc{L}"), 1)
                        after_wait(sem(f"idxc{L}"), j + 1)
                        pool.indirect_dma_start(
                            out=XB[b], out_offset=None, in_=hrow,
                            in_offset=bass.IndirectOffsetOnAxis(ap=idxc[:, b:b + 1].bitcast(U32), axis=0)).then_inc(sem(f"xg{b}_{L}"), 16)

                blocks(0)
                with pool.Fori(1, npairs) as i:
                    blocks(i)
                for b in range(2):
                    after_wait(sem(f"yst{b}_{L}"), 16 * npairs, 2 + b)
                for t in range(TT):
                    if t >= 2:
                        pool.wait_ge(*after("yc", L, 2 * (t - 1)))
                    for i in range(2):
                        pool.indirect_dma_start(
                            out=WE[t % 2][:, i * D:(i + 1) * D], out_offset=None, in_=yrow,
                            in_offset=bass.IndirectOffsetOnAxis(ap=slots[:, i, t:t + 1], axis=0)).then_inc(sem(f"yg{t % 2}"), 16)


def HEADS_S(u, n):
    scan, part = divmod(u, NPART)
    return 13 * scan + 1 + 4 * part + n


SCORES = [(s, CTX, TOK) for s in range(0, TOK, P)] + [(s, 0, CTX) for s in range(0, CTX, P)]
PT_AT = [sum(q1 - q0 for _, q0, q1 in SCORES[:n]) for n in range(len(SCORES))]


_INS = ["x", "c", "ctx", "c_ctx", "w_mod", "b_mod", "norm_mix_w", "norm_ffn_w", "w_in", "hgrn_lb_logits", "hgrn_norm_w",
        "ret_decay_logit", "ret_gn_w", "w_o_hgrn", "w_o_ret", "w_out", "router_group_w", "router_group_b",
        "router_expert_w", "router_expert_b", "expert_w_gate", "expert_w_up", "expert_w_down", "final_norm_w"]


def tables():
    import numpy as np
    f = np.float32
    cst = np.zeros((P, 2 * P + 2 * 7 * C), f)
    cst[:, 0:P] = np.eye(P)
    cst[:, P:2 * P] = 1.0 / D
    s, t = np.meshgrid(np.arange(C), np.arange(C), indexing="ij")
    for d in range(2):
        m = np.zeros((C, 7, C), f)
        for l in range(LEVELS):
            w = C >> l
            same = s // w == t // w
            first, second = (s, t) if d == 0 else (t, s)
            m[:, l, :] = same & (first % w < w // 2) & (second % w >= w // 2)
        m[:, 6, :] = np.eye(C) * QSCALE
        cst[:, 2 * P + d * 7 * C:2 * P + (d + 1) * 7 * C] = np.tile(m.reshape(C, -1), (2, 1))
    rc = np.zeros((P, 2 * LAT + P + 3 * XW), f)
    pos = np.arange(LAT)
    inv = (10000.0 ** (-np.arange(0, 64, 2, dtype=f) / f(64))).astype(f)
    for half, x in enumerate((pos // 64, pos % 64)):
        ang = (inv[:, None] * x[None, :].astype(f)).astype(f)
        for i, sign in ((0, -1.0), (1, 1.0)):
            r = slice(64 * half + 32 * i, 64 * half + 32 * (i + 1))
            rc[r, 0:512] = np.cos(ang)
            rc[r, 512:1024] = sign * np.sin(ang)
    for i in range(P):
        rc[i ^ 32, 1024 + i] = 1.0
    xx = np.arange(XW)[None, :] - 384 - np.arange(P)[:, None]
    rc[:, 1152:1152 + XW] = xx
    rc[:, 1152 + XW:1152 + 2 * XW] = np.maximum(xx, 0)
    rc[:, 1152 + 2 * XW:] = np.maximum(-xx, 0)
    mc = np.zeros((P, P + NBMAX * NE + NE + NBMAX), f)
    mc[:, 0:P] = np.triu(np.ones((P, P)), 1)
    mc[:, P:P + NBMAX * NE] = np.repeat(np.arange(NBMAX), NE)[None, :]
    mc[:, P + NBMAX * NE:P + NBMAX * NE + NE] = np.arange(NE)[None, :]
    mc[:, P + NBMAX * NE + NE:] = np.arange(NBMAX)[None, :]
    return {"cst": cst, "rc": rc, "mc": mc}


def kernel(**inputs):
    import numpy as _np
    import concourse.bacc as _bacc
    from concourse import mybir as _mybir
    from concourse.bass_utils import run_bass_kernel_spmd as _run

    nc = _bacc.Bacc("TRN2", target_bir_lowering=False, num_devices=1)
    arrays, aps = {}, {}
    data = {n: _np.ascontiguousarray(inputs[n]) for n in _INS}
    data.update(tables())
    for name, x in data.items():
        arrays[f"in_{name}"] = x
        aps[name] = nc.dram_tensor(f"in_{name}", x.shape, _mybir.dt.from_np(x.dtype), kind="ExternalInput").ap()
    aps["out"] = nc.dram_tensor("out_0", (1, LAT, D), _mybir.dt.float32, kind="ExternalOutput").ap()
    build(nc, aps)
    r = _run(nc, [arrays], core_ids=[0])
    return r.results[0]["out_0"]
```

```python
from contextlib import ExitStack

import concourse.bass as bass
from concourse import mybir

F32 = mybir.dt.float32
F32R = mybir.dt.float32r
BF16 = mybir.dt.bfloat16
I32 = mybir.dt.int32
U32 = mybir.dt.uint32
ALU = mybir.AluOpType
ACT = mybir.ActivationFunctionType
AX = mybir.AxisListType

P = 128
D = 1024
KD = D // P
LAT, CTX = 512, 256
TOK = CTX + LAT
TT = TOK // P
DEPTH = 2
SEG = ((0, CTX, 1), (CTX, TOK, 0))
HEADS = 4
DV = 256
C = 64
LEVELS = 6
PART = 256
NPART = TOK // PART
UNITS = HEADS * 2 * NPART
EPS = 1e-6
F_MIN = 1e-30
QSCALE = float(P) ** -0.5
NG, NPG = 4, 8
NE = NG * NPG
DE = 256
BLK = 128
TOPK = 2
NBMAX = NE + TOPK * TOK // BLK
NBMAX += NBMAX % 2
CAP = NBMAX * BLK
XW = TOK + P

GROUPS = [("ff", 512, 0), ("fb", 1024, 0), ("q", 0, 0), ("v", 1536, 1), ("g", 2048, 0),
          ("rq", 2560, 0), ("rk", 3072, 0), ("rv0", 3584, 1), ("rv1", 4096, 1), ("rg0", 4608, 0), ("rg1", 5120, 0),
          ("ga0", 5632, 0), ("ga1", 6144, 0), ("gb0", 6656, 0), ("gb1", 7168, 0)]
NHG = 5
TILES = [(g, m) for g, (_, _, tm) in enumerate(GROUPS) for m in range(4)]
TILES_HG = sum(1 for g, _ in TILES if g < NHG)
STEPS = len(TILES) - TILES_HG
SCR = {"rq": 0, "rk": 4, "rg0": 8, "rg1": 12, "ga0": 16, "ga1": 20, "gb0": 24, "gb1": 28}
LAST_USE = {}
for _g in range(1, len(GROUPS)):
    for _m in range(4):
        LAST_USE.setdefault(4 * (_g - 1) + (2 * (_m // 2) + 1 if GROUPS[_g - 1][2] else _m), []).append(4 * _g + _m)
EARLY = STEPS * 5 // 8
UNIT_AT = {u * (STEPS - 1) // UNITS: u for u in range(UNITS)}
NMOD = 6 * D // 512
USES = NMOD + len(GROUPS) + 4

V_BMOD, V_MIX, V_FFN, V_HGN, V_GN, V_FIN, V_RB, V_LB, V_N = 0, 48, 56, 64, 68, 76, 84, 85, 101


PER_LAYER = {}
for _n, _names in (
        (NMOD, "mod_mm mod_ev"), (len(TILES), "proj_mm proj_ev whi wlo"), (KD, "y_mm y_ev out_mm sq_mix sq_ffn"),
        (16 * 12, "vec_ld"), (1, "final_vec idx0 plan slots vec_mm modT_mm ms_mix ms_ffn rstd_mix rstd_ffn lg_mm lgT Lg_mm rank_mm amod"),
        (16 * STEPS // 2, "spill0 spill1"), (16, "rot_ld x_spill x_back wohg mc_ld idx_clr idxs"), (HEADS, "hgate oT_mm hr"), (16, "rg_ld dist_ld"),
        (HEADS * TT, "pv_mm rg_done on ro_ev roT_mm rvar rr"), (48 * HEADS // 2, "rqkv0 rqkv1"), (32 * KD // 2, "gab0 gab1"),
        (2 * KD, "x_mid hlo h_mix h_ffn hm_mix hm_ffn"), (TT, "hstg hrow_mm yc_mm"), (16 * TT // 2, "hrow0 hrow1"),
        (32 * TT, "idx_sc"), (KD * TT, "x_end"), (UNITS, "ql kl dcy f k k1 lnf dd ee"),
        (2 * UNITS, "sc_ev sc_mm kT kT_mm pS_mm scT o_mmh o_evh"), (13 * 2 * HEADS, "S"), (8 * HEADS, "rsc_ev rsc_mm"),
        (2 * HEADS, "rot_mm rot"), (2, "Mb gd gx"), (2 * TT, "yc"), (3, "pre pre_a"), (4 * HEADS, "dt"), (4 * TT, "m8"),
        (32 * TT // 2, "yg0 yg1")):
    for _name in _names.split():
        PER_LAYER[_name] = _n


def first_tile(L):
    return 0 if L < DEPTH - 1 else CTX // P


def tiles(L):
    return range(first_tile(L), TT)


def ntile(L):
    return len(tiles(L))


def segs(L):
    return SEG if L < DEPTH - 1 else SEG[1:]


def silent(L, u):
    return L == DEPTH - 1 and u % NPART == 0


def spoken(L, u):
    return sum(not silent(L, v) for v in range(u))


def unit(u):
    h, r = divmod(u, 2 * NPART)
    d, n = divmod(r, NPART)
    part = n if d == 0 or n == 0 else NPART - n
    return h, d, n, part


def build(nc, a):
    with ExitStack() as ctx:
        def sb(name, shape, dt=F32):
            return ctx.enter_context(nc.sbuf_tensor(name, shape, dt))

        sems = {}

        def sem(name):
            if name not in sems:
                sems[name] = ctx.enter_context(nc.semaphore(name))
            return sems[name]

        def after(name, L, n):
            return sem(name), L * PER_LAYER.get(name, 0) + n

        at = -(-nc.sbuf_base // 32) * 32
        xT = sb("xT", [P, KD, TOK])
        hT = sb("hT", [P, KD, TOK])
        ring = sb("ring", [P, 2, KD, 512])
        hhi = nc.alloc_sbuf_tensor_at("hhi", [P, KD, TOK], F32R, offset=at)
        hlo = nc.alloc_sbuf_tensor_at("hlo", [P, KD, TOK], F32R, offset=at + 4 * KD * TOK)
        wlo = nc.alloc_sbuf_tensor_at("wlo", [P, 2, KD, 512], F32R, offset=at + 8 * KD * TOK)
        cst = sb("cst", [P, 2 * P + 2 * 7 * C])
        ident, meanw = cst[:, 0:P], cst[:, P:2 * P]
        masks = [cst[:, 2 * P + i * 7 * C:2 * P + (i + 1) * 7 * C].rearrange("p (l t) -> p l t", l=7) for i in range(2)]
        eps = sb("eps", [P, 1])
        cT = sb("cT", [P, 16])
        vrow = sb("vrow", [V_N, P])
        vec = sb("vec", [P, V_N])
        modT = sb("modT", [P, 48, 2])
        amod = sb("amod", [P, 2, KD, 2])
        lbm = sb("lbm", [P, 4, 8])
        dec = sb("dec", [P, 6, 8])
        wrt = sb("wrt", [P, KD, NG + NE])
        AR = 29856
        at = -(-nc.sbuf_base // 32) * 32
        arena = sb("arena", [P, AR])
        whi = nc.alloc_sbuf_tensor_at("whi", [P, KD, 512], F32R, offset=at + 4 * 25760)

        def ar(off, n, **kw):
            assert off + n <= AR
            v = arena[:, off:off + n]
            return v.rearrange("p (a b) -> p a b", **kw) if kw else v

        xrow = ar(0, TT * D, a=TT)
        ccrow = ar(28000, P)[0:16]
        rstd = ar(28200, TOK)
        mrow = ar(6144, 6 * D)
        hq = ar(0, 3072, a=4)
        sig = [ar(3072, 3072, a=4), ar(6144, 3072, a=4)]
        hv = ar(9216, 3072, a=TT)
        hgate = ar(12288, 3072, a=4)
        E = ar(15360, 8 * PART, a=8)
        QL = ar(17408, 7 * PART, a=7)
        KL = ar(19200, 7 * PART, a=7)
        Pc = ar(20992, 4 * (C + 1), a=4)
        ff = ar(21252, PART)
        kk = sb("kk", [P, 2, PART])
        dcy = sb("dcy", [P, 4])
        gg = ar(21764, 4 * (C + 1), a=4)
        keep = ar(22024, 4 * (C + 1), a=4)
        msk = ar(22284, 7 * C, a=7)
        scT = ar(22732, C)
        kTs = ar(22796, P)
        S = ar(22924, 3 * P, a=3)
        oacc = ar(23308, TT * P, a=TT)
        stage = [ar(24076, TOK), ar(24844, TOK)]
        zeros = ar(24076, D)
        junk = ar(25612, P)
        ss = ar(25740, 16)
        rgate = ar(15360, 6144, a=8)
        rqk = [ar(0, 1536, a=2), ar(1536, 1536, a=2)]
        rv = [ar(3072, 1536, a=TT), ar(4608, 1536, a=TT)]
        NROT = 2 * LAT + P
        rot = ar(6144, NROT)
        cosT, sinT, perm = rot[:, 0:LAT], rot[:, LAT:2 * LAT], rot[:, 2 * LAT:NROT]
        rtmp = ar(7296, LAT)
        PT = ar(7808, 3584)
        Wd = ar(11392, XW)
        Dc = ar(21504, XW)
        wtmp = ar(22400, XW)
        dtmp = ar(28448, XW)
        on = ar(24192, 512, a=2)
        rst = ar(24704, 64)
        dist = ar(25760, 3 * XW)
        XX, XP, XN = [dist[:, i * XW:(i + 1) * XW] for i in range(3)]
        merged = ar(0, 6144, a=8)
        gab = [ar(6144, 1536, a=2), ar(7680, 1536, a=2)]
        ytmp = ar(9216, TOK)
        WE = [ar(i * 6144, 6144) for i in range(2)]
        XB = [ar(12288 + i * 1024, 1024) for i in range(2)]
        XT = [ar(14336 + i * 1024, 1024, a=8) for i in range(2)]
        sg = [ar(16384 + i * 256, 256) for i in range(2)]
        hid = [ar(16896 + i * 256, 256) for i in range(2)]
        hidT = [ar(17408 + i * 256, 256, a=2) for i in range(2)]
        YB = [ar(17920 + i * 1024, 1024) for i in range(2)]
        mc = ar(20000, P + NBMAX * NE + NE + NBMAX)
        tri, jm = mc[:, 0:P], mc[:, P:P + NBMAX * NE].rearrange("p (j e) -> p j e", e=NE)
        io = mc[:, P + NBMAX * NE:P + NBMAX * NE + NE]
        lgT = ar(21700, TOK)
        Lg = ar(22470, TT * 36, a=TT)
        ro = ar(22700, 2300)
        hstg = [ar(25000, 1024), ar(26024, 1024)]
        nil = sb("nil", [P, 4])
        trib = ar(27100, P).bitcast(BF16)
        Mb = sb("Mb", [P, TT, NE], BF16)
        u8 = sb("u8", [P, 2 * TT, 8], U32)
        slots = sb("slots", [P, 4, TT], U32)
        tokid = sb("tokid", [P, TT], I32)
        idx0 = sb("idx0", [P, NBMAX], I32)
        idxs = sb("idxs", [P, NBMAX], I32)
        idxc = sb("idxc", [P, 2], I32)
        ebi = sb("ebi", [1, NBMAX + 2], I32)

        ps = ctx.enter_context(nc.psum_tensor("ps", [P, 8, 512], F32))

        def pair(b):
            return ps[:, b:b + 2, :].rearrange("p b n -> p (b n)")

        def tokens(b):
            return pair(b)[:, 256:1024]

        def dram(name, shape, dt=F32):
            return nc.dram_tensor(name, shape, dt, kind="Internal").ap()

        xsp = dram("xsp", (P, KD, TOK))
        scr = dram("scr", (32, P, TOK))
        scrv = dram("scrv", (TOK, 1024))
        hrow = dram("hrow", (TOK, D))
        yrow = dram("yrow", (CAP, D))
        idxd = [dram(f"idxd{i}", (CAP, 1), I32) for i in range(DEPTH)]

        def uses(L):
            out = [a["w_mod"][L][:, g * 512:(g + 1) * 512] for g in range(NMOD)]
            out += [a["w_in"][L][:, c:c + 512] for _, c, _ in GROUPS]
            out += [a[n][L][:, c:c + 512] for n in ("w_o_ret", "w_out") for c in (0, 512)]
            return [x.rearrange("(k p) n -> p k n", p=P) for x in out]

        def used(L, n):
            if n < NMOD:
                return after("mod_mm", L, n + 1)
            n -= NMOD
            if n < len(GROUPS):
                return after("proj_mm", L, 1 + max(i for i, (g, _) in enumerate(TILES) if g == n))
            n -= len(GROUPS)
            return after("y_mm", L, 4 * (n + 1)) if n < 2 else after("out_mm", L, 4 * (n - 1))

        stream = [(L, n, x) for L in range(DEPTH) for n, x in enumerate(uses(L))]

        def ring_ready(eng, L, n):
            i = L * USES + n
            eng.wait_ge(sem(f"ring{i % 2}"), 16 * (i // 2 + 1))

        def reg_wait(eng, s, v, least=1):
            eng.wait_ge(s, v)
            if not isinstance(v, int):
                eng.wait_ge(s, least)

        def ret_transposes(pe, L, i):
            pe.wait_ge(*after("ro_ev", L, i + 1))
            if i >= 2:
                pe.wait_ge(*after("rg_done", L, i - 1))
            for e in range(2):
                mm = pe.transpose(ps[:, 6 + i % 2, e * P:(e + 1) * P], on[:, i % 2, e * P:(e + 1) * P], ident)
            mm.then_inc(sem("roT_mm"), 1)

        def head_gate(dve, L, h):
            dve.wait_ge(*after("oT_mm", L, h + 1))
            s0 = first_tile(L) * P
            dve.scalar_tensor_tensor(out=hgate[:, h, s0:TOK], in0=pair(6)[:, s0:TOK], scalar=vec[:, V_HGN + h:V_HGN + h + 1],
                                     in1=hgate[:, h, s0:TOK], op0=ALU.mult, op1=ALU.mult).then_inc(sem("hgate"), 1)

        def ret_gate(dve, L, i):
            h, t = divmod(i, ntile(L))
            t += first_tile(L)
            dve.wait_ge(*after("roT_mm", L, i + 1))
            for e in range(2):
                x = rgate[:, 2 * h + e, t * P:(t + 1) * P]
                ins = dve.scalar_tensor_tensor(out=x, in0=ps[:, 6 + i % 2, e * P:(e + 1) * P], scalar=vec[:, V_GN + 2 * h + e:V_GN + 2 * h + e + 1],
                                               in1=x, op0=ALU.mult, op1=ALU.mult)
            ins.then_inc(sem("rg_done"), 1)

        block = ctx.enter_context(nc.Block())

        @block.sync
        def _(sp):
            def fill(i):
                if i >= len(stream):
                    return
                if i >= 2:
                    sp.wait_ge(*used(*stream[i - 2][:2]))
                sp.dma_start(ring[:, i % 2], stream[i][2]).then_inc(sem(f"ring{i % 2}"), 16)

            def head_load(L, h):
                s0 = first_tile(L) * P
                ld = sem(f"rqkv{h % 2}")
                sp.dma_start(rqk[h % 2][:, 0, s0:TOK], scr[h][:, s0:TOK]).then_inc(ld, 16)
                sp.dma_start(rqk[h % 2][:, 1], scr[4 + h]).then_inc(ld, 16)
                sp.dma_start(rv[h % 2], scrv[:, h * DV:(h + 1) * DV].rearrange("(t p) n -> p t n", p=P)).then_inc(ld, 16)

            sp.dma_start(cst[:], a["cst"]).then_inc(sem("cst_ld"), 16)
            sp.dma_start(ccrow[0:8, :], a["c"].rearrange("a (k p) -> (a k) p", p=P)).then_inc(sem("cst_ld"), 16)
            sp.dma_start(ccrow[8:16, :], a["c_ctx"].rearrange("(k p) -> k p", p=P)).then_inc(sem("cst_ld"), 16)
            sp.dma_start(xrow[:, 0:2, :], a["ctx"][0].rearrange("(t p) d -> p t d", p=P)).then_inc(sem("x_ld"), 16)
            sp.dma_start(xrow[:, 2:6, :], a["x"][0].rearrange("(t p) d -> p t d", p=P)).then_inc(sem("x_ld"), 16)
            fill(0)
            fill(1)
            for L in range(DEPTH):
                base = L * USES
                if L:
                    sp.wait_ge(*after("final_vec", L - 1, 1))
                else:
                    sp.wait_ge(sem("init"), 1)
                vl = sem("vec_ld")
                for r, x in ((V_BMOD, a["b_mod"][L]), (V_MIX, a["norm_mix_w"][L]), (V_FFN, a["norm_ffn_w"][L]),
                             (V_HGN, a["hgrn_norm_w"][L]), (V_GN, a["ret_gn_w"][L]), (V_FIN, a["final_norm_w"])):
                    x = x.rearrange("(k p) -> k p", p=P)
                    sp.dma_start(vrow[r:r + x.shape[0], :], x).then_inc(vl, 16)
                sp.dma_start(vrow[V_LB:V_LB + 16, :], a["hgrn_lb_logits"].rearrange("d l (h p) -> (d l h) p", p=P)).then_inc(vl, 16)
                sp.dma_start(vrow[V_RB:V_RB + 1, 0:NG], a["router_group_b"][L:L + 1, :]).then_inc(vl, 16)
                sp.dma_start(vrow[V_RB:V_RB + 1, NG:NG + NE], a["router_expert_b"][L:L + 1, :]).then_inc(vl, 16)
                sp.dma_start(dec[:, 0, :], a["ret_decay_logit"][L].rearrange("d h -> (d h)").partition_broadcast(P)).then_inc(vl, 16)
                sp.dma_start(wrt[:, :, 0:NG], a["router_group_w"][L].rearrange("(k p) n -> p k n", p=P)).then_inc(vl, 16)
                sp.dma_start(wrt[:, :, NG:NG + NE], a["router_expert_w"][L].rearrange("(k p) n -> p k n", p=P)).then_inc(vl, 16)
                if L:
                    sp.wait_ge(*after("x_end", L - 1, KD * ntile(L - 1)))
                else:
                    sp.wait_ge(sem("x_cp"), KD)
                sp.dma_start(xsp, xT[:]).then_inc(sem("x_spill"), 16)
                for n in range(NMOD):
                    fill(base + n + 2)
                for k, (g, m) in enumerate(TILES):
                    i = k - TILES_HG
                    if i >= 0:
                        sp.wait_ge(*after("proj_ev", L, k + 1))
                        name, _, tm = GROUPS[g]
                        if tm:
                            c0 = (512 if name == "rv1" else 0) + 256 * (m // 2)
                            t0 = 3 * (m % 2)
                            dst = scrv[t0 * P:(t0 + 3) * P, c0:c0 + 256].rearrange("(b p) n -> p b n", p=P)
                            src = stage[i % 2].rearrange("p (b n) -> p b n", b=3)
                        else:
                            s0 = tile_start(L, name)
                            dst, src = scr[SCR[name] + m][:, s0:TOK], stage[i % 2][:, s0:TOK]
                        sp.dma_start(dst, src).then_inc(sem(f"spill{i % 2}"), 16)
                    if k + 1 == len(TILES) or TILES[k + 1][0] != g:
                        fill(base + NMOD + g + 2)
                    if i == EARLY:
                        sp.wait_ge(*after("o_evh", L, 2 * spoken(L, UNITS // 2)))
                        for j in range(2):
                            sp.wait_ge(*after(f"spill{j}", L, 16 * 8))
                        sp.dma_start(rot, a["rc"][:, 0:NROT]).then_inc(sem("rot_ld"), 16)
                        head_load(L, 0)

                sp.wait_ge(*after("proj_mm", L, len(TILES)))
                sp.dma_start(dist, a["rc"][:, NROT:NROT + 3 * XW]).then_inc(sem("dist_ld"), 16)
                for i in range(2):
                    sp.wait_ge(*after(f"spill{i}", L, 16 * (STEPS // 2)))
                s0 = first_tile(L) * P
                sp.wait_ge(*after("o_evh", L, 2 * spoken(L, UNITS)))
                head_load(L, 1)
                sp.dma_start(rgate[:, :, s0:TOK], scr[8:16, :, s0:TOK].rearrange("m p t -> p m t")).then_inc(sem("rg_ld"), 16)
                sp.dma_start(xT[:], xsp).then_inc(sem("x_back"), 16)
                wohg = hT[:].rearrange("p k t -> p (k t)")[:, 0:4096].rearrange("p (k n) -> p k n", k=4)
                sp.dma_start(wohg, a["w_o_hgrn"][L].rearrange("(k p) n -> p k n", p=P)).then_inc(sem("wohg"), 16)
                for h in range(2, HEADS):
                    sp.wait_ge(*after("pv_mm", L, ntile(L) * (h - 1)))
                    head_load(L, h)
                sp.wait_ge(*after("rg_done", L, HEADS * ntile(L)))
                for m in range(KD):
                    if m >= 2:
                        sp.wait_ge(*after("y_ev", L, m - 1))
                    sp.dma_start(gab[m % 2][:, 0, s0:TOK], scr[16 + m][:, s0:TOK]).then_inc(sem(f"gab{m % 2}"), 16)
                    sp.dma_start(gab[m % 2][:, 1, s0:TOK], scr[24 + m][:, s0:TOK]).then_inc(sem(f"gab{m % 2}"), 16)
                    if m in (3, 7):
                        fill(base + NMOD + len(GROUPS) + (0 if m == 3 else 1) + 2)
                fill(base + NMOD + len(GROUPS) + 2 + 2)
                fill(base + NMOD + len(GROUPS) + 3 + 2)

                sp.wait_ge(*after("x_mid", L, len(segs(L)) * KD))
                sp.dma_start(mc, a["mc"]).then_inc(sem("mc_ld"), 16)
                sp.wait_ge(*after("idx0", L, 1))
                sp.dma_start(idxd[L].rearrange("(p j) o -> p (j o)", p=P), idx0[:]).then_inc(sem("idx_clr"), 16)
                for t in tiles(L):
                    sp.wait_ge(*after("hstg", L, t - first_tile(L) + 1))
                    sp.dma_start(hrow[t * P:(t + 1) * P, :], hstg[t % 2]).then_inc(sem(f"hrow{t % 2}"), 16)
                sp.wait_ge(*after("idx_sc", L, 16 * 2 * ntile(L)))
                sp.dma_start(idxs[:], idxd[L].rearrange("(p j) o -> p (j o)", p=P)).then_inc(sem("idxs"), 16)
                sp.wait_ge(*after("plan", L, 1))
                npairs = sp.value_load(ebi[0:1, NBMAX:NBMAX + 1], min_val=NE // 2, max_val=NBMAX // 2)

                last = sp.value_load(ebi[0:1, NBMAX + 1:NBMAX + 2], min_val=NE - 2, max_val=NBMAX - 2)

                def weights(i, b, which):
                    e = sp.value_load(ebi[0:1, bass.ds(2 * i + b, 1)], min_val=0, max_val=NE - 1)
                    w = WE[b]
                    if not isinstance(i, int):
                        sp.wait_ge(sem(f"d_mm{L}" if which else f"g_mm{L}"), 2 * i + b - 1)
                    if which == 0:
                        for n, o in (("expert_w_gate", 0), ("expert_w_up", 256)):
                            dst = w[:, 0:4096].rearrange("p (k n) -> p k n", k=8)[:, :, o:o + 256]
                            src = a[n][L].rearrange("e (p k) n -> e p k n", k=8)[bass.ds(e, 1)].rearrange("e p k n -> (e p) k n")
                            sp.dma_start(dst, src).then_inc(sem(f"wgu{b}_{L}"), 16)
                    else:
                        src = a["expert_w_down"][L].rearrange("e (p k) n -> e p (k n)", k=2)[bass.ds(e, 1)].rearrange("e p n -> (e p) n")
                        sp.dma_start(w[:, 4096:6144], src).then_inc(sem(f"wd{b}_{L}"), 16)

                def stores(i, b, j):
                    reg_wait(sp, sem(f"yev_a{L}"), 2 * i + b + 1)
                    reg_wait(sp, sem(f"yev_v{L}"), 2 * i + b + 1)
                    dst = yrow[bass.ds(j * BLK, BLK), :]
                    sp.dma_start(dst, YB[b]).then_inc(sem(f"yst{b}_{L}"), 16)

                for b in range(2):
                    weights(0, b, 0)
                    weights(0, b, 1)
                with sp.Fori(1, npairs) as i:
                    for b in range(2):
                        weights(i, b, 0)
                    for b in range(2):
                        weights(i, b, 1)
                        stores(i - 1, b, 2 * i + b - 2)
                for b in range(2):
                    sp.wait_ge(sem(f"yev_a{L}"), last + b + 1)
                    sp.wait_ge(sem(f"yev_v{L}"), last + b + 1)
                    sp.dma_start(yrow[bass.ds((last + b) * BLK, BLK), :], YB[b]).then_inc(sem(f"yst{b}_{L}"), 16)

            for t in range(LAT // P):
                sp.wait_ge(sem("o_ev"), t + 1)
                sp.dma_start(a["out"][0, t * P:(t + 1) * P, :], hstg[t % 2]).then_inc(sem(f"o_st{t % 2}"), 16)
            for i in range(2):
                sp.wait_ge(sem(f"o_st{i}"), 16 * (LAT // P // 2))


        @block.tensor
        def _(pe):
            def seg_mm(bank, lhsT, rhs, first, last, T=SEG):
                for s0, s1, _ in T:
                    b, c = (bank, 256) if s0 == 0 else (bank + 1, 0)
                    mm = pe.matmul(ps[0:lhsT.shape[1], b, c:c + s1 - s0], lhsT, rhs[:, s0:s1], start=first, stop=last)
                return mm

            def norm_sum(tag, L, T=SEG):
                for m in range(KD):
                    pe.wait_ge(*after(f"sq{tag}", L, m + 1))
                    mm = seg_mm(0, meanw, hT[:, m, :], m == 0, m == KD - 1, T)
                mm.then_inc(sem(f"ms{tag}"), 1)

            pe.wait_ge(sem("cst_ld"), 48)
            pe.transpose(ps[:, 7, 0:16], ccrow, ident[0:16, 0:16]).then_inc(sem("cc_mm"), 1)
            pe.wait_ge(sem("x_ld"), 32)
            for m in range(KD):
                b = 2 * (m % 2)
                if m >= 2:
                    pe.wait_ge(sem("x_cp"), m - 1)
                for t in range(TT):
                    mm = pe.transpose(tokens(b)[:, t * P:(t + 1) * P], xrow[:, t, m * P:(m + 1) * P], ident)
                mm.then_inc(sem("cc_mm"), 1)

            for L in range(DEPTH):
                pe.wait_ge(*after("vec_ld", L, 16 * 12))
                if L == 0:
                    pe.wait_ge(sem("cT"), 2)
                pe.transpose(ps[:, 7, 0:V_N], vrow[:], ident[0:V_N, 0:V_N]).then_inc(sem("vec_mm"), 1)
                if L:
                    pe.wait_ge(*after("x_end", L - 1, KD * ntile(L - 1)))
                for g in range(NMOD):
                    ring_ready(pe, L, g)
                    if g >= 2:
                        pe.wait_ge(*after("mod_ev", L, g - 1))
                    r = ring[:, (L * USES + g) % 2]
                    for k in range(KD):
                        mm = pe.matmul(ps[0:2, 4 + g % 2, :], cT[:, k:16:8], r[:, k, :], start=k == 0, stop=k == KD - 1)
                    mm.then_inc(sem("mod_mm"), 1)
                pe.wait_ge(*after("mod_ev", L, NMOD))
                for j in range(48):
                    mm = pe.transpose(ps[:, 6, 2 * j:2 * j + 2], mrow[0:2, j * P:(j + 1) * P], ident[0:2, 0:2])
                mm.then_inc(sem("modT_mm"), 1)
                norm_sum("_mix", L)

                def head_transposes(h):
                    pe.wait_ge(*after("on", L, ntile(L) * (h + 1)))
                    for t in tiles(L):
                        mm = pe.transpose(pair(6)[:, t * P:(t + 1) * P], oacc[:, t, :], ident)
                    mm.then_inc(sem("oT_mm"), 1)

                def unit_products(u):
                    h, d, n, part = unit(u)
                    quiet = silent(L, u)
                    if u and u % 6 == 0:
                        head_transposes(h - 1)
                        yield
                        pe.wait_ge(*after("hgate", L, h))
                    if not quiet:
                        pe.wait_ge(*after("ql", L, spoken(L, u) + 1))
                    pe.wait_ge(*after("kl", L, u + 1))
                    kslot, qslot = (6, 0) if d == 0 else (0, 6)
                    lk, lq = (0, 1) if d == 0 else (1, 0)
                    for p_ in range(2):
                        p = p_ if d == 0 else 1 - p_
                        tt = part * 2 + p
                        q = 2 * u + p_
                        qo = 2 * spoken(L, u) + p_
                        if q:
                            pe.wait_ge(*after("S", L, HEADS_S(u, 2 * p_)))
                        pe.transpose(ps[:, 6, 0:P], KL[:, kslot, p * P:(p + 1) * P], ident).then_inc(sem("kT_mm"), 1)
                        if not quiet:
                            if qo:
                                pe.wait_ge(*after("sc_ev", L, qo))
                            for j in range(2):
                                c0 = p * P + j * C
                                for l in range(LEVELS):
                                    pe.matmul(ps[j * C:(j + 1) * C, 4, l * C:(l + 1) * C], KL[:, lk + l, c0:c0 + C],
                                              QL[:, lq + l, c0:c0 + C], start=True, stop=True)
                                mm = pe.matmul(ps[j * C:(j + 1) * C, 4, 6 * C:7 * C], kk[:, u % 2, c0:c0 + C],
                                               hq[:, h, tt * P + j * C:tt * P + (j + 1) * C], start=True, stop=True)
                            mm.then_inc(sem("sc_mm"), 1)
                        yield
                        pe.wait_ge(*after("kT", L, q + 1))
                        for j in range(2):
                            mm = pe.matmul(ps[:, 7 - j, P:2 * P], kTs[j * C:(j + 1) * C, :],
                                           hv[j * C:(j + 1) * C, tt, h * P:(h + 1) * P], start=True, stop=True)
                        mm.then_inc(sem("pS_mm"), 1)
                        yield
                        if quiet:
                            continue
                        pe.wait_ge(*after("scT", L, qo + 1))
                        if qo:
                            pe.wait_ge(*after("o_evh", L, qo))
                        for j_ in range(2):
                            j = j_ if d == 0 else 1 - j_
                            c = n * 4 + 2 * p_ + j_
                            pe.matmul(ps[j * C:(j + 1) * C, 5, 0:P], scT[j * C:(j + 1) * C, :],
                                      hv[j * C:(j + 1) * C, tt, h * P:(h + 1) * P], start=True, stop=False)
                            pe.wait_ge(*after("S", L, HEADS_S(u, 2 * p_ + j_)))
                            mm = pe.matmul(ps[j * C:(j + 1) * C, 5, 0:P], QL[:, qslot, p * P + j * C:p * P + (j + 1) * C],
                                           S[:, c % 3, :], start=False, stop=True)
                        mm.then_inc(sem("o_mmh"), 1)

                pieces = iter(())
                for k, (g, m) in enumerate(TILES):
                    name, _, tm = GROUPS[g]
                    pe.wait_ge(*after("wlo", L, 4 * g + (2 * (m // 2) + 2 if tm else m + 1)))
                    b = 2 * (k % 2)
                    if k >= 2:
                        pe.wait_ge(*after("proj_ev", L, k - 1))
                    wl, wh = wlo[:, (L * USES + NMOD + g) % 2], whi
                    if tm:
                        cols = slice(256 * (m // 2), 256 * (m // 2) + 256)
                        for t in range(3):
                            rows = slice((3 * (m % 2) + t) * P, (3 * (m % 2) + t + 1) * P)
                            out = tokens(b)[:, t * 256:(t + 1) * 256]
                            for k8 in range(KD):
                                if t * KD + k8 in (3, 7, 11, 15, 19):
                                    next(pieces, None)
                                pe.matmul(out, hhi[:, k8, rows], wh[:, k8, cols], start=k8 == 0, stop=False)
                                pe.matmul(out, hhi[:, k8, rows], wl[:, k8, cols], start=False, stop=False)
                                mm = pe.matmul(out, hlo[:, k8, rows], wh[:, k8, cols], start=False, stop=k8 == KD - 1)
                    else:
                        cols = slice(m * P, (m + 1) * P)
                        T = SEG[bool(tile_start(L, name)):]
                        for k8 in range(KD):
                            if k == 0:
                                pe.wait_ge(*after("hlo", L, 2 * (k8 + 1)))
                            if k8 in (1, 3, 4, 5, 7):
                                next(pieces, None)
                            seg_mm(b, wh[:, k8, cols], hhi[:, k8, :], k8 == 0, False, T)
                            seg_mm(b, wh[:, k8, cols], hlo[:, k8, :], False, False, T)
                            mm = seg_mm(b, wl[:, k8, cols], hhi[:, k8, :], False, k8 == KD - 1, T)
                    mm.then_inc(sem("proj_mm"), 1)
                    st = k - TILES_HG
                    if st in UNIT_AT:
                        for _piece in pieces:
                            pass
                        pieces = unit_products(UNIT_AT[st])
                        next(pieces)
                for _piece in pieces:
                    pass

                pe.wait_ge(*after("rot_ld", L, 16))
                pe.wait_ge(*after("proj_ev", L, len(TILES)))
                for h in range(HEADS):
                    pe.wait_ge(*after(f"rqkv{h % 2}", L, 48 * (h // 2 + 1)))
                    qk = rqk[h % 2]
                    if h:
                        pe.wait_ge(*after("rsc_ev", L, nscore(L) * h))
                    for i in range(2):
                        pe.matmul(ps[:, i, :], perm, qk[:, i, CTX:TOK], start=True, stop=True).then_inc(sem("rot_mm"), 1)
                    if h == 0:
                        head_transposes(HEADS - 1)
                    pe.wait_ge(*after("rot", L, 2 * (h + 1)))
                    for n, (s0, q0, q1) in enumerate(SCORES[:nscore(L)]):
                        i = nscore(L) * h + n
                        if n >= 4 or h:
                            pe.wait_ge(*after("rsc_ev", L, i - 3))
                        pe.matmul(ps[:, n % 4, 0:q1 - q0], qk[:, 1, s0:s0 + P], qk[:, 0, q0:q1],
                                  start=True, stop=True).then_inc(sem("rsc_mm"), 1)
                    for t in tiles(L):
                        i = ntile(L) * h + t - first_tile(L)
                        b = 4 + i % 2
                        terms = [n for n, (s0, q0, q1) in enumerate(SCORES) if q0 <= t * P < q1]
                        if i >= 2:
                            pe.wait_ge(*after("ro_ev", L, i - 1))
                        pe.wait_ge(*after("rsc_ev", L, nscore(L) * h + max(terms) + 1))
                        for n in terms:
                            s0, q0, q1 = SCORES[n]
                            o = PT_AT[n] + t * P - q0
                            mm = pe.matmul(ps[:, b, 0:DV], PT[:, o:o + P], rv[h % 2][:, s0 // P, :], start=n == terms[0],
                                           stop=n == terms[-1])
                        mm.then_inc(sem("pv_mm"), 1)
                        if i == 1:
                            pe.wait_ge(*after("hgate", L, HEADS))
                        if i:
                            ret_transposes(pe, L, i - 1)
                ret_transposes(pe, L, HEADS * ntile(L) - 1)

                wohg = hT[:].rearrange("p k t -> p (k t)")[:, 0:4096].rearrange("p (k n) -> p k n", k=4)
                pe.wait_ge(*after("wohg", L, 16))
                pe.wait_ge(*after("rg_done", L, HEADS * ntile(L)))
                for m in range(KD):
                    if m % 4 == 0:
                        ring_ready(pe, L, NMOD + len(GROUPS) + m // 4)
                    r = ring[:, (L * USES + NMOD + len(GROUPS) + m // 4) % 2]
                    b = 4 * (m % 2)
                    if m >= 2:
                        pe.wait_ge(*after("y_ev", L, m - 1))
                    for k in range(4):
                        seg_mm(b, wohg[:, k, m * P:(m + 1) * P], hgate[:, k, :], k == 0, k == 3, segs(L))
                    for k in range(KD):
                        mm = seg_mm(b + 2, r[:, k, (m % 4) * P:(m % 4 + 1) * P], rgate[:, k, :], k == 0, k == KD - 1, segs(L))
                    mm.then_inc(sem("y_mm"), 1)
                pe.wait_ge(*after("y_ev", L, KD))
                for m in range(KD):
                    if m % 4 == 0:
                        ring_ready(pe, L, NMOD + len(GROUPS) + 2 + m // 4)
                    r = ring[:, (L * USES + NMOD + len(GROUPS) + 2 + m // 4) % 2]
                    b = 2 * (m % 2)
                    if m >= 2:
                        pe.wait_ge(*after("x_mid", L, len(segs(L)) * (m - 1)))
                    for k in range(KD):
                        mm = seg_mm(b, r[:, k, (m % 4) * P:(m % 4 + 1) * P], merged[:, k, :], k == 0, k == KD - 1, segs(L))
                    mm.then_inc(sem("out_mm"), 1)

                norm_sum("_ffn", L, segs(L))
                pe.wait_ge(*after("h_ffn", L, len(segs(L)) * KD))
                for k in range(KD):
                    mm = seg_mm(2, wrt[:, k, :], hT[:, k, :], k == 0, k == KD - 1, segs(L))
                mm.then_inc(sem("lg_mm"), 1)
                pe.wait_ge(*after("lgT", L, 1))
                for t in tiles(L):
                    i = t - first_tile(L)
                    mm = pe.transpose(ps[:, 1, i * 36:(i + 1) * 36], lgT[0:36, t * P:(t + 1) * P], ident[0:36, 0:36])
                mm.then_inc(sem("Lg_mm"), 1)
                for t in tiles(L):
                    b = 4 + 2 * (t % 2)
                    if t - first_tile(L) >= 2:
                        pe.wait_ge(*after("hstg", L, t - first_tile(L) - 1))
                    for k in range(KD):
                        mm = pe.transpose(pair(b)[:, k * P:(k + 1) * P], hT[:, k, t * P:(t + 1) * P], ident)
                    mm.then_inc(sem("hrow_mm"), 1)
                pe.wait_ge(*after("Mb", L, 2))
                nt = ntile(L)
                for t in range(nt):
                    for t2 in range(t + 1):
                        pe.matmul(ps[:, 2, t * NE:(t + 1) * NE], trib[:, 0:P] if t2 == t else trib[:, P:2 * P], Mb[:, t2, :],
                                  start=t2 == 0, stop=t2 == t)
                for t in range(nt):
                    mm = pe.matmul(ps[:, 2, nt * NE:(nt + 1) * NE], trib[:, P:2 * P], Mb[:, t, :], start=t == 0, stop=t == nt - 1)
                mm.then_inc(sem("rank_mm"), 1)
                pe.wait_ge(*after("plan", L, 1))
                pe.wait_ge(*after("hstg", L, ntile(L)))
                npairs = pe.value_load(ebi[0:1, NBMAX:NBMAX + 1], min_val=NE // 2, max_val=NBMAX // 2)

                def blocks(i):
                    first = isinstance(i, int)
                    for b in range(2):
                        j = 2 * i + b
                        reg_wait(pe, sem(f"xg{b}_{L}"), 16 * i + 16, 16)
                        if not first or b:
                            reg_wait(pe, sem(f"xt_a{L}"), j)
                            reg_wait(pe, sem(f"xt_v{L}"), j)
                        for k in range(KD):
                            mm = pe.transpose(pair(0)[:, k * P:(k + 1) * P], XB[b][:, k:D:KD], ident)
                        mm.then_inc(sem(f"xt_mm{L}"), 1)
                    for b in range(2):
                        j = 2 * i + b
                        reg_wait(pe, sem(f"wgu{b}_{L}"), 32 * i + 32, 32)
                        reg_wait(pe, sem(f"xt_a{L}"), j + 1)
                        reg_wait(pe, sem(f"xt_v{L}"), j + 1)
                        for k in range(KD):
                            mm = pe.matmul(ps[:, 2 + b, :], XT[b][:, k, :], WE[b][:, k * 512:(k + 1) * 512], start=k == 0,
                                           stop=k == KD - 1)
                        mm.then_inc(sem(f"g_mm{L}"), 1)
                    for b in range(2):
                        j = 2 * i + b
                        reg_wait(pe, sem(f"hid{L}"), j + 1)
                        for k in range(2):
                            mm = pe.transpose(ps[:, 4, k * P:(k + 1) * P], hid[b][:, k:DE:2], ident)
                        mm.then_inc(sem(f"ht_mm{L}"), 1)
                        reg_wait(pe, sem(f"hidT{L}"), j + 1)
                        reg_wait(pe, sem(f"wd{b}_{L}"), 16 * i + 16, 16)
                        if not first or b:
                            reg_wait(pe, sem(f"yev_a{L}"), j)
                            reg_wait(pe, sem(f"yev_v{L}"), j)
                        for n in range(2):
                            for k in range(2):
                                mm = pe.matmul(ps[:, 5 + n, :], hidT[b][:, k, :],
                                               WE[b][:, 4096 + k * 1024 + n * 512:4096 + k * 1024 + (n + 1) * 512],
                                               start=k == 0, stop=k == 1)
                        mm.then_inc(sem(f"d_mm{L}"), 1)

                blocks(0)
                with pe.Fori(1, npairs) as i:
                    blocks(i)
                for t in tiles(L):
                    b = 2 * (t % 2)
                    i = t - first_tile(L)
                    pe.wait_ge(*after("yc", L, 2 * (i + 1)))
                    if i >= 2:
                        pe.wait_ge(*after("x_end", L, KD * (i - 1)))
                    for m in range(KD):
                        mm = pe.transpose(pair(b)[:, m * P:(m + 1) * P], XB[t % 2][:, m * P:(m + 1) * P], ident)
                    mm.then_inc(sem("yc_mm"), 1)

            norm_sum("_fin", 0, SEG[1:])
            pe.wait_ge(sem("h_fin"), KD)
            for t in range(LAT // P):
                b = 4 + 2 * (t % 2)
                if t >= 2:
                    pe.wait_ge(sem("o_ev"), t - 1)
                for m in range(KD):
                    mm = pe.transpose(pair(b)[:, m * P:(m + 1) * P], hT[:, m, CTX + t * P:CTX + (t + 1) * P], ident)
                mm.then_inc(sem("o_mm"), 1)


        @block.scalar
        def _(act):
            chain = [0]

            def link(ins):
                chain[0] += 1
                ins.then_inc(sem("act_chain"), 1)
                act.wait_ge(sem("act_chain"), chain[0])

            table = [""]

            def log_exp():
                if table[0] != "log_exp":
                    act.preload_act_table_set("natural_log_exp_and_others")
                    table[0] = "log_exp"

            def norm_squares(tag, L, s0=0):
                for m in range(KD):
                    act.activation(hT[:, m, s0:TOK], xT[:, m, s0:TOK], ACT.Square).then_inc(sem(f"sq{tag}"), 1)

            def norm_rstd(tag, L, s0=0):
                log_exp()
                act.wait_ge(*after(f"ms{tag}", L, 1))
                link(act.activation(rstd[:, s0:TOK], tokens(0)[:, s0:TOK], ACT.Ln, bias=eps[:]))
                act.activation(rstd[:, s0:TOK], rstd[:, s0:TOK], ACT.Exp, scale=-0.5).then_inc(sem(f"rstd{tag}"), 1)

            def norm_shift(tag, L, shift, T=SEG):
                n = 0
                for m in range(KD):
                    for s0, s1, s in T:
                        n += 1
                        act.wait_ge(*after(f"hm{tag}", L, n))
                        act.activation(hT[:, m, s0:s1], hT[:, m, s0:s1], ACT.Identity,
                                       bias=modT[:, shift * 8 + m, s:s + 1]).then_inc(sem(f"h{tag}"), 1)

            act.wait_ge(sem("init"), 1)
            act.wait_ge(sem("cc_mm"), 1)
            act.activation(cT[:], ps[:, 7, 0:16], ACT.Silu).then_inc(sem("cT"), 1)
            act.wait_ge(sem("cT"), 1)
            act.activation(eps[:], eps[:], ACT.Copy).then_inc(sem("cT"), 1)

            for L in range(DEPTH):
                for g in range(NMOD):
                    act.wait_ge(*after("mod_mm", L, g + 1))
                    act.activation(mrow[0:2, g * 512:(g + 1) * 512], ps[0:2, 4 + g % 2, :], ACT.Copy).then_inc(sem("mod_ev"), 1)
                log_exp()
                act.wait_ge(*after("pre", L, 3))
                act.activation(lbm[:, 0, :], lbm[:, 0, :], ACT.Exp).then_inc(sem("pre_a"), 1)
                act.activation(lbm[:, 1, :], lbm[:, 1, :], ACT.Exp).then_inc(sem("pre_a"), 1)
                link(act.activation(dec[:, 1, :], dec[:, 1, :], ACT.Exp, scale=-1.0))
                act.activation(dec[:, 1, :], dec[:, 1, :], ACT.Ln, bias=1.0).then_inc(sem("pre_a"), 1)
                act.wait_ge(sem("x_cp"), KD)
                if L:
                    act.wait_ge(*after("x_end", L - 1, KD * ntile(L - 1)))
                norm_squares("_mix", L)
                norm_rstd("_mix", L)
                act.wait_ge(*after("amod", L, 1))
                act.wait_ge(*after("x_spill", L, 16))
                n = 0
                for m in range(KD):
                    for s0, s1, s in SEG:
                        n += 1
                        act.wait_ge(*after("hm_mix", L, n))
                        act.activation(hhi[:, m, s0:s1], hT[:, m, s0:s1], ACT.Identity,
                                       bias=modT[:, m, s:s + 1]).then_inc(sem("h_mix"), 1)

                def weights_high(q):
                    g, m = divmod(q, 4)
                    if m == 0:
                        ring_ready(act, L, NMOD + g)
                    w = ring[:, (L * USES + NMOD + g) % 2, :, m * P:(m + 1) * P]
                    act.activation(whi[:, :, m * P:(m + 1) * P], w, ACT.Copy).then_inc(sem("whi"), 1)

                for q in range(4):
                    weights_high(q)

                def unit_log(u):
                    log_exp()
                    act.wait_ge(*after("f", L, u + 1))
                    act.activation(gg[:, :, 1:C + 1], ff.rearrange("p (c t) -> p c t", t=C), ACT.Ln).then_inc(sem("lnf"), 1)

                def unit_exp(u):
                    act.wait_ge(*after("dd", L, u + 1))
                    e = E[:, 0:8:7, :] if silent(L, u) else E
                    act.activation(e, e, ACT.Exp).then_inc(sem("ee"), 1)

                def head_norm(h):
                    log_exp()
                    act.wait_ge(*after("o_evh", L, 2 * spoken(L, 6 * (h + 1))))
                    for t in tiles(L):
                        link(act.activation(junk, oacc[:, t, :], ACT.Square, accum_out=ss[:, t:t + 1]))
                    t0 = first_tile(L)
                    link(act.activation(ss[:, 8 + t0:8 + TT], ss[:, t0:TT], ACT.Ln, scale=1.0 / P, bias=eps[:]))
                    act.activation(ss[:, 8 + t0:8 + TT], ss[:, 8 + t0:8 + TT], ACT.Exp, scale=-0.5).then_inc(sem("hr"), 1)

                for k, (g, m) in enumerate(TILES):
                    name, _, tm = GROUPS[g]
                    b = 2 * (k % 2)
                    st = k - TILES_HG
                    if st == 0:
                        if L == 0:
                            act.wait_ge(sem("yclr"), 16 * (NBMAX - NE))
                        unit_log(0)
                        unit_exp(0)
                    act.wait_ge(*after("proj_mm", L, k + 1))
                    s0 = tile_start(L, name)
                    src = tokens(b)[:, s0:TOK]
                    if name in ("ff", "fb"):
                        ins = act.activation(sig[name == "fb"][:, m, :], src, ACT.Sigmoid)
                    elif name == "q":
                        ins = act.activation(hq[:, m, s0:TOK], src, ACT.Silu)
                    elif name == "g":
                        ins = act.activation(hgate[:, m, s0:TOK], src, ACT.Silu)
                    elif name == "v":
                        ins = act.activation(hv[:, 3 * (m % 2):3 * (m % 2) + 3, 256 * (m // 2):256 * (m // 2) + 256],
                                             src.rearrange("p (t n) -> p t n", t=3), ACT.Copy)
                    else:
                        if st >= 2:
                            act.wait_ge(*after(f"spill{st % 2}", L, 16 * (st // 2)))
                        fn = {"rg": ACT.Silu, "ga": ACT.Sigmoid, "gb": ACT.Sigmoid}.get(name[:2], ACT.Copy)
                        ins = act.activation(stage[st % 2][:, s0:TOK], src, fn, scale=QSCALE if name == "rq" else 1.0)
                    if name[:2] in ("ff", "fb", "q", "g", "rg", "ga", "gb"):
                        table[0] = "other"
                    ins.then_inc(sem("proj_ev"), 1)
                    for q in LAST_USE.get(k, ()):
                        weights_high(q)
                    if st in UNIT_AT:
                        u = UNIT_AT[st]
                        if u + 1 < UNITS:
                            unit_log(u + 1)
                            unit_exp(u + 1)
                        if u % 6 == 5:
                            head_norm(u // 6)

                log_exp()
                act.wait_ge(*after("dist_ld", L, 16))
                for h in range(HEADS):
                    lf, lb = dec[:, 3, h:h + 1], dec[:, 3, 4 + h:5 + h]
                    if h:
                        act.wait_ge(*after("rsc_ev", L, nscore(L) * h))
                    act.activation(Wd, XP, ACT.Exp, scale=lf).then_inc(sem("dt"), 1)
                    act.activation(wtmp, XN, ACT.Exp, scale=lb).then_inc(sem("dt"), 1)
                    act.activation(Dc, XX, ACT.Exp, scale=lf, bias=dec[:, 4, h:h + 1]).then_inc(sem("dt"), 1)
                    act.activation(dtmp, XX, ACT.Exp, scale=dec[:, 5, 4 + h:5 + h], bias=dec[:, 4, 4 + h:5 + h]).then_inc(sem("dt"), 1)
                    for i in range(ntile(L) * h, ntile(L) * (h + 1)):
                        act.wait_ge(*after("rvar", L, i + 1))
                        r = rst[:, 32 + 4 * (i % 2):33 + 4 * (i % 2)]
                        link(act.activation(r, rst[:, 17 + 4 * (i % 2):18 + 4 * (i % 2)], ACT.Ln, bias=eps[:]))
                        act.activation(r, r, ACT.Exp, scale=-0.5).then_inc(sem("rr"), 1)

                act.wait_ge(*after("x_mid", L, len(segs(L)) * KD))
                s0 = first_tile(L) * P
                norm_squares("_ffn", L, s0)
                norm_rstd("_ffn", L, s0)
                norm_shift("_ffn", L, 3, segs(L))
                act.wait_ge(*after("lg_mm", L, 1))
                act.activation(lgT[0:36, s0:TOK], tokens(2)[0:36, s0:TOK], ACT.Identity, bias=vec[0:36, V_RB:V_RB + 1]).then_inc(sem("lgT"), 1)
                for t in tiles(L):
                    i = t - first_tile(L)
                    act.wait_ge(*after("hrow_mm", L, i + 1))
                    if i >= 2:
                        act.wait_ge(*after(f"hrow{t % 2}", L, 16 * (i // 2)))
                    act.activation(hstg[t % 2], pair(4 + 2 * (t % 2)), ACT.Copy).then_inc(sem("hstg"), 1)
                log_exp()
                act.wait_ge(*after("gd", L, 2))
                act.activation(ro[:, 0:ntile(L) * 4], ro[:, 0:ntile(L) * 4], ACT.Exp).then_inc(sem("gx"), 1)
                act.activation(ro[:, 32:32 + ntile(L)], ro[:, 32:32 + ntile(L)], ACT.Exp).then_inc(sem("gx"), 1)
                act.wait_ge(*after("plan", L, 1))
                npairs = act.value_load(ebi[0:1, NBMAX:NBMAX + 1], min_val=NE // 2, max_val=NBMAX // 2)

                def blocks(i):
                    first = isinstance(i, int)
                    for b in range(2):
                        j = 2 * i + b
                        if not first:
                            reg_wait(act, sem(f"g_mm{L}"), j - 1)
                        reg_wait(act, sem(f"xt_mm{L}"), j + 1)
                        act.activation(XT[b][:, 0:4, :], ps[:, 0, :].rearrange("p (k t) -> p k t", k=4), ACT.Copy).then_inc(sem(f"xt_a{L}"), 1)
                    for b in range(2):
                        j = 2 * i + b
                        if not first:
                            reg_wait(act, sem(f"hid{L}"), j - 1)
                        reg_wait(act, sem(f"g_mm{L}"), j + 1)
                        act.activation(sg[b], ps[:, 2 + b, 0:DE], ACT.Silu).then_inc(sem(f"sg{L}"), 1)
                    for b in range(2):
                        j = 2 * i + b
                        if not first:
                            reg_wait(act, sem(f"yst{b}_{L}"), 16 * i, 16)
                        reg_wait(act, sem(f"d_mm{L}"), j + 1)
                        act.activation(YB[b][:, 0:512], ps[:, 5, :], ACT.Copy).then_inc(sem(f"yev_a{L}"), 1)

                blocks(0)
                with act.Fori(1, npairs) as i:
                    blocks(i)
                table[0] = "silu"
            act.wait_ge(*after("x_end", DEPTH - 1, KD * ntile(DEPTH - 1)))
            norm_squares("_fin", 0, CTX)
            norm_rstd("_fin", 0, CTX)
            for t in range(LAT // P):
                act.wait_ge(sem("o_mm"), t + 1)
                if t >= 2:
                    act.wait_ge(sem(f"o_st{t % 2}"), 16 * (t // 2))
                act.activation(hstg[t % 2], pair(4 + 2 * (t % 2)), ACT.Copy).then_inc(sem("o_ev"), 1)

        @block.vector
        def _(dve):
            chain = [0]

            def link(ins):
                chain[0] += 1
                ins.then_inc(sem("dve_chain"), 1)
                dve.wait_ge(sem("dve_chain"), chain[0])

            def norm_scale(tag, L, w, T=SEG):
                dve.wait_ge(*after(f"rstd{tag}", L, 1))
                for m in range(KD):
                    for s0, s1, s in T:
                        dve.scalar_tensor_tensor(out=hT[:, m, s0:s1], in0=xT[:, m, s0:s1], scalar=w(m, s),
                                                 in1=rstd[:, s0:s1], op0=ALU.mult, op1=ALU.mult).then_inc(sem(f"hm{tag}"), 1)

            dve.memset(eps[:], EPS).then_inc(sem("dve_chain"), 1)
            chain[0] += 1
            link(dve.memset(gg, 0.0))
            dve.memset(vrow[:], 0.0).then_inc(sem("init"), 1)
            for m in range(KD):
                dve.wait_ge(sem("cc_mm"), m + 2)
                dve.tensor_copy(xT[:, m, :], tokens(2 * (m % 2))).then_inc(sem("x_cp"), 1)

            for L in range(DEPTH):
                dve.wait_ge(*after("vec_mm", L, 1))
                link(dve.tensor_copy(vec[:], ps[:, 7, 0:V_N]))
                lg = vec[:, V_LB:V_LB + 16].rearrange("p (d l h) -> p l d h", d=2, l=2)
                l0, l1, mx, t1 = [lbm[:, i, :].rearrange("p (d h) -> p d h", d=2) for i in range(4)]
                link(dve.tensor_tensor(mx, lg[:, 0], lg[:, 1], ALU.max))
                dve.tensor_tensor(l0, lg[:, 0], mx, ALU.subtract).then_inc(sem("pre"), 1)
                dve.tensor_tensor(l1, lg[:, 1], mx, ALU.subtract).then_inc(sem("pre"), 1)
                link(dve.tensor_scalar(dec[:, 2, :], dec[:, 0, :], -1.0, None, ALU.mult))
                dve.tensor_tensor(dec[:, 1, :], dec[:, 0, :], dec[:, 2, :], ALU.max).then_inc(sem("pre"), 1)
                dve.wait_ge(*after("pre_a", L, 3))
                l0, l1, lb, om = lbm[:, 0, :], lbm[:, 1, :], lbm[:, 2, :], lbm[:, 3, :]
                link(dve.tensor_tensor(lb, l0, l1, ALU.add))
                link(dve.reciprocal(om, lb))
                if L == 0:
                    link(dve.memset(lb, 0.0))
                else:
                    link(dve.tensor_tensor(l0, l0, om, ALU.mult))
                    link(dve.tensor_tensor(l1, l1, om, ALU.mult))
                    link(dve.tensor_tensor(lb, l0, l1, ALU.add))
                    link(dve.tensor_tensor(lb, lb, l0, ALU.subtract))
                    link(dve.tensor_scalar(lb, lb, 0.0, 1.0 - 1e-6, ALU.max, ALU.min))
                link(dve.tensor_scalar(om, lb, -1.0, 1.0, ALU.mult, ALU.add))
                link(dve.tensor_scalar(dec[:, 2, :], dec[:, 0, :], 0.0, None, ALU.min))
                link(dve.tensor_tensor(dec[:, 3, :], dec[:, 2, :], dec[:, 1, :], ALU.subtract))
                link(dve.tensor_scalar(dec[:, 4, 0:4], dec[:, 3, 0:4], float(CTX), None, ALU.mult))
                link(dve.tensor_scalar(dec[:, 4, 4:8], dec[:, 3, 4:8], float(LAT), None, ALU.mult))
                link(dve.tensor_scalar(dec[:, 5, :], dec[:, 3, :], -1.0, None, ALU.mult))
                dve.wait_ge(*after("modT_mm", L, 1))
                link(dve.tensor_tensor(modT[:], ps[:, 6, 0:96].rearrange("p (j s) -> p j s", s=2),
                                       vec[:, V_BMOD:V_BMOD + 48].unsqueeze(2).to_broadcast([P, 48, 2]), ALU.add))
                for i, (v0, sc) in enumerate(((V_MIX, 1), (V_FFN, 4))):
                    link(dve.tensor_scalar(amod[:, i], modT[:, sc * 8:sc * 8 + 8, :], 1.0, None, ALU.add))
                    ins = dve.tensor_tensor(amod[:, i], amod[:, i], vec[:, v0:v0 + 8].unsqueeze(2).to_broadcast([P, 8, 2]), ALU.mult)
                    if i == 0:
                        link(ins)
                    else:
                        ins.then_inc(sem("amod"), 1)
                dve.wait_ge(*after("amod", L, 1))
                norm_scale("_mix", L, lambda m, s: amod[:, 0, m, s:s + 1])
                n = 0
                for m in range(KD):
                    for s0, s1, s in SEG:
                        n += 1
                        dve.wait_ge(*after("h_mix", L, n))
                        dve.scalar_tensor_tensor(out=hlo[:, m, s0:s1], in0=hT[:, m, s0:s1], scalar=modT[:, m, s:s + 1],
                                                 in1=hhi[:, m, s0:s1].bitcast(F32), op0=ALU.add, op1=ALU.subtract).then_inc(sem("hlo"), 1)

                def weights_low(q):
                    g, m = divmod(q, 4)
                    slot, cols = (L * USES + NMOD + g) % 2, slice(m * P, (m + 1) * P)
                    dve.wait_ge(*after("whi", L, q + 1))
                    dve.tensor_tensor(wlo[:, slot, :, cols], ring[:, slot, :, cols], whi[:, :, cols].bitcast(F32), ALU.subtract).then_inc(sem("wlo"), 1)

                for q in range(4):
                    weights_low(q)

                link(dve.memset(keep, 1.0))
                link(dve.memset(gg, 0.0))
                link(dve.memset(keep[:, :, 0:1], 0.0))

                def forget(u):
                    h, d, n, part = unit(u)
                    x = sig[d][:, h, part * PART:(part + 1) * PART]
                    lb, om = lbm[:, 2, d * 4 + h:d * 4 + h + 1], lbm[:, 3, d * 4 + h:d * 4 + h + 1]
                    k_ = kk[:, u % 2, :]
                    dve.tensor_scalar(k_, x, -1.0, 1.0, ALU.mult, ALU.add).then_inc(sem("k1"), 1)
                    link(dve.tensor_scalar(ff, x, om, lb, ALU.mult, ALU.add))
                    dve.tensor_scalar(ff, ff, F_MIN, None, ALU.max).then_inc(sem("f"), 1)
                    dve.wait_ge(*after("k1", L, u + 1))
                    dve.tensor_scalar(k_, k_, om, None, ALU.mult).then_inc(sem("k"), 1)

                def differences(u):
                    h, d, n, part = unit(u)
                    off = 1 - d
                    dve.wait_ge(*after("lnf", L, u + 1))
                    link(dve.tensor_tensor_scan(Pc.rearrange("p c t -> p (c t)"), keep.rearrange("p c t -> p (c t)"),
                                                gg.rearrange("p c t -> p (c t)"), 0.0, ALU.mult, ALU.add))
                    if u:
                        dve.wait_ge(*after("kl", L, u))
                        dve.wait_ge(*after("dcy", L, u))
                    for l in range(0 if silent(L, u) else LEVELS):
                        w = C >> l
                        n_ = C // w
                        x = Pc[:, :, off:off + C].rearrange("p c (n w) -> p c n w", w=w)
                        mid = Pc[:, :, w // 2:C:w].unsqueeze(3).to_broadcast([P, 4, n_, w // 2])
                        e = E[:, 1 + l, :].rearrange("p (c n w) -> p c n w", c=4, w=w)
                        dve.tensor_tensor(e[:, :, :, w // 2:w], x[:, :, :, w // 2:w], mid, ALU.subtract)
                        dve.tensor_tensor(e[:, :, :, 0:w // 2], mid, x[:, :, :, 0:w // 2], ALU.subtract)
                    last = Pc[:, :, C:C + 1].to_broadcast([P, 4, C])
                    e = [E[:, i, :].rearrange("p (c t) -> p c t", t=C) for i in (0, 7)]
                    dve.tensor_copy(e[0], Pc[:, :, off:off + C])
                    dve.tensor_tensor(e[1], last, Pc[:, :, off:off + C], ALU.subtract).then_inc(sem("dd"), 1)

                def queries(u):
                    h, d, n, part = unit(u)
                    dve.wait_ge(*after("ee", L, u + 1))
                    x = E[:, 0, C - 1:PART:C] if d == 0 else E[:, 7, 0:PART:C]
                    if u:
                        dve.wait_ge(*after("S", L, HEADS_S(u - 1, 4)))
                    dve.tensor_copy(dcy[:], x).then_inc(sem("dcy"), 1)
                    if silent(L, u):
                        return
                    q = hq[:, h, part * PART:(part + 1) * PART].unsqueeze(1).to_broadcast([P, 7, PART])
                    dve.scalar_tensor_tensor(out=QL, in0=E[:, d:d + 7, :], scalar=QSCALE, in1=q, op0=ALU.mult,
                                             op1=ALU.mult).then_inc(sem("ql"), 1)

                def outputs(u, p_):
                    h, d, n, part = unit(u)
                    quiet = silent(L, u)
                    if n == 0 and p_ == 0:
                        if u:
                            dve.wait_ge(*after("S", L, 13 * (2 * h + d)))
                        dve.memset(S[:, 0, :], 0.0).then_inc(sem("S"), 1)
                    p = p_ if d == 0 else 1 - p_
                    tt = part * 2 + p
                    q = 2 * u + p_
                    qo = 2 * spoken(L, u) + p_
                    dve.wait_ge(*after("kT_mm", L, q + 1))
                    dve.tensor_copy(kTs, ps[:, 6, 0:P]).then_inc(sem("kT"), 1)
                    if not quiet:
                        dve.wait_ge(*after("sc_mm", L, qo + 1))
                        dve.tensor_tensor(msk, ps[:, 4, 0:7 * C].rearrange("p (l t) -> p l t", l=7), masks[d],
                                          ALU.mult).then_inc(sem("sc_ev"), 1)
                        dve.wait_ge(*after("sc_ev", L, qo + 1))
                        dve.tensor_reduce(scT, msk.rearrange("p l t -> p t l"), AX.X, ALU.add).then_inc(sem("scT"), 1)
                    dve.wait_ge(*after("dcy", L, u + 1))
                    dve.wait_ge(*after("pS_mm", L, q + 1))
                    for j_ in range(2):
                        j = j_ if d == 0 else 1 - j_
                        c = n * 4 + 2 * p_ + j_
                        dve.wait_ge(*after("S", L, HEADS_S(u, 2 * p_ + j_)))
                        dve.scalar_tensor_tensor(out=S[:, (c + 1) % 3, :], in0=S[:, c % 3, :], scalar=dcy[:, 2 * p + j:2 * p + j + 1],
                                                 in1=ps[:, 7 - j, P:2 * P], op0=ALU.mult, op1=ALU.add).then_inc(sem("S"), 1)
                    if quiet:
                        return
                    dve.wait_ge(*after("o_mmh", L, qo + 1))
                    if d == 0:
                        dve.tensor_copy(oacc[:, tt, :], ps[:, 5, 0:P]).then_inc(sem("o_evh"), 1)
                    else:
                        dve.tensor_tensor(oacc[:, tt, :], ps[:, 5, 0:P], oacc[:, tt, :], ALU.add).then_inc(sem("o_evh"), 1)

                def rotate(h):
                    dve.wait_ge(*after(f"rqkv{h % 2}", L, 48 * (h // 2 + 1)))
                    dve.wait_ge(*after("rot_ld", L, 16))
                    for i in range(2):
                        x = rqk[h % 2][:, i, CTX:TOK]
                        dve.wait_ge(*after("rot_mm", L, 2 * h + i + 1))
                        if i or h or L:
                            dve.wait_ge(*after("rot", L, 2 * h + i))
                        link(dve.tensor_tensor(rtmp, ps[:, i, :], sinT, ALU.mult))
                        link(dve.tensor_tensor(x, x, cosT, ALU.mult))
                        dve.tensor_tensor(x, x, rtmp, ALU.add).then_inc(sem("rot"), 1)

                for k in range(TILES_HG):
                    for q in LAST_USE.get(k, ()):
                        weights_low(q)
                dve.wait_ge(*after("proj_ev", L, TILES_HG))
                forget(0)
                differences(0)
                for k, (g, m) in enumerate(TILES):
                    st = k - TILES_HG
                    if st < 0:
                        continue
                    if st not in UNIT_AT:
                        for q in LAST_USE.get(k, ()):
                            weights_low(q)
                        continue
                    u = UNIT_AT[st]
                    queries(u)
                    if u and u % 6 == 0:
                        head_gate(dve, L, u // 6 - 1)
                    if u + 1 < UNITS:
                        forget(u + 1)
                    outputs(u, 0)
                    if u + 1 < UNITS:
                        differences(u + 1)
                    outputs(u, 1)
                    for q in LAST_USE.get(k, ()):
                        weights_low(q)
                    if u % 6 == 5:
                        dve.wait_ge(*after("hr", L, u // 6 + 1))
                        for t in tiles(L):
                            dve.tensor_scalar(oacc[:, t, :], oacc[:, t, :], ss[:, 8 + t:9 + t], None, ALU.mult).then_inc(sem("on"), 1)

                for h in range(HEADS):
                    rotate(h)
                    if h == 0:
                        head_gate(dve, L, HEADS - 1)
                    dve.wait_ge(*after("rot", L, 2 * h + 2))
                    dve.wait_ge(*after("dt", L, 4 * (h + 1)))
                    link(dve.tensor_tensor(Wd, Wd, wtmp, ALU.mult))
                    link(dve.tensor_tensor(Wd[:, 384:512], Wd[:, 384:512], ident, ALU.add))
                    link(dve.tensor_tensor(Dc, Dc, dtmp, ALU.add))

                    def scores(n):
                        s0, q0, q1 = SCORES[n]
                        i = nscore(L) * h + n
                        dve.wait_ge(*after("rsc_mm", L, i + 1))
                        cross = s0 < CTX <= q0
                        tab = Dc if cross else Wd
                        y = (q0 - CTX if cross else q0) - s0 + 384
                        if h:
                            dve.wait_ge(*after("pv_mm", L, ntile(L) * h))
                        dve.tensor_tensor(PT[:, PT_AT[n]:PT_AT[n] + q1 - q0], ps[:, n % 4, 0:q1 - q0], tab[:, y:y + q1 - q0],
                                          ALU.mult).then_inc(sem("rsc_ev"), 1)

                    def ret_norm(i):
                        b = 4 + i % 2
                        st6 = rst[:, 6 * (i % 2):6 * (i % 2) + 6]
                        mv = rst[:, 16 + 4 * (i % 2):18 + 4 * (i % 2)]
                        dve.wait_ge(*after("pv_mm", L, i + 1))
                        link(dve.bn_stats(st6, ps[:, b, 0:DV]))
                        dve.bn_aggr(mv, st6).then_inc(sem("rvar"), 1)
                        dve.wait_ge(*after("rr", L, i + 1))
                        if i >= 2:
                            dve.wait_ge(*after("roT_mm", L, i - 1))
                        dve.tensor_scalar(on[:, i % 2, :], ps[:, b, 0:DV], mv[:, 0:1], rst[:, 32 + 4 * (i % 2):33 + 4 * (i % 2)],
                                          ALU.subtract, ALU.mult).then_inc(sem("ro_ev"), 1)

                    for n in range(nscore(L)):
                        scores(n)
                    for i in range(ntile(L) * h, ntile(L) * (h + 1)):
                        ret_norm(i)
                        if i == 1:
                            dve.wait_ge(*after("rg_ld", L, 16))
                        if i:
                            ret_gate(dve, L, i - 1)
                ret_gate(dve, L, HEADS * ntile(L) - 1)

                dve.wait_ge(*after("x_back", L, 16))
                t0 = first_tile(L) * P
                for m in range(KD):
                    b = 4 * (m % 2)
                    dve.wait_ge(*after("y_mm", L, m + 1))
                    dve.wait_ge(*after(f"gab{m % 2}", L, 32 * (m // 2 + 1)))
                    if m or L:
                        dve.wait_ge(*after("y_ev", L, m))
                    y = merged[:, m, t0:TOK]
                    link(dve.tensor_tensor(ytmp[:, t0:TOK], tokens(b)[:, t0:TOK], gab[m % 2][:, 0, t0:TOK], ALU.mult))
                    link(dve.tensor_tensor(y, tokens(b + 2)[:, t0:TOK], gab[m % 2][:, 1, t0:TOK], ALU.mult))
                    dve.tensor_tensor(y, y, ytmp[:, t0:TOK], ALU.add).then_inc(sem("y_ev"), 1)
                for m in range(KD):
                    dve.wait_ge(*after("out_mm", L, m + 1))
                    for s0, s1, s in segs(L):
                        dve.scalar_tensor_tensor(out=xT[:, m, s0:s1], in0=tokens(2 * (m % 2))[:, s0:s1], scalar=modT[:, 16 + m, s:s + 1],
                                                 in1=xT[:, m, s0:s1], op0=ALU.mult, op1=ALU.add).then_inc(sem("x_mid"), 1)

                norm_scale("_ffn", L, lambda m, s: amod[:, 1, m, s:s + 1], segs(L))
                dve.wait_ge(*after("mc_ld", L, 16))
                dve.wait_ge(*after("Lg_mm", L, 1))
                nt = ntile(L)
                link(dve.tensor_copy(Lg[:, 0:nt], ps[:, 1, 0:nt * 36].rearrange("p (t e) -> p t e", e=36)))

                def r_(off, n, **kw):
                    v = ro[:, off:off + n]
                    return v.rearrange("p (a b) -> p a b", **kw) if kw else v

                gx, d21 = r_(0, NG * nt, a=nt), r_(32, nt)
                pad, mx8, mx8e = r_(64, 8 * nt, a=nt), r_(112, 8 * nt, a=nt), r_(160, 8 * nt, a=nt)
                ein = r_(208, NPG * nt, a=nt)
                gs, grp, e12, w12 = r_(352, nt), r_(360, nt), r_(368, 2 * nt, a=2), r_(380, 2 * nt, a=2)
                tmp4 = r_(400, nt * NE)
                O1, O2 = r_(600, nt * NE, a=nt), r_(800, nt * NE, a=nt)
                rank, cnt = r_(1000, nt * NE, a=nt), r_(1192, NE)
                nb, inc, bs = r_(1224, NE), r_(1256, NE), r_(1288, NE)
                rk, bb, rj, t6 = r_(1320, 2 * nt, a=2), r_(1332, 2 * nt, a=2), r_(1344, 2 * nt, a=2), r_(1356, 2 * nt, a=2)
                one32 = r_(1370, NE)
                sl = r_(1410, 4 * nt, a=4)
                ebf = r_(1440, NBMAX + 2)
                link(dve.memset(pad, -3.0e38))
                link(dve.tensor_copy(pad[:, :, 0:NG], Lg[:, 0:nt, 0:NG]))
                for t in range(nt):
                    ins = dve.max(mx8[:, t, :], pad[:, t, :])
                    ins.then_inc(sem("m8"), 1)
                dve.wait_ge(*after("m8", L, nt))
                for t in range(nt):
                    dve.max_index(u8[:, t, :], mx8[:, t, :], pad[:, t, :]).then_inc(sem("m8"), 1)
                dve.tensor_tensor(gx, Lg[:, 0:nt, 0:NG], mx8[:, :, 0:1].to_broadcast([P, nt, NG]), ALU.subtract).then_inc(sem("gd"), 1)
                dve.wait_ge(*after("m8", L, 2 * nt))
                link(dve.tensor_copy(grp, u8[:, 0:nt, 0]))
                link(dve.tensor_tensor(r_(400, nt * NG, a=nt), io[:, 0:NG].unsqueeze(1).to_broadcast([P, nt, NG]),
                                       grp.unsqueeze(2).to_broadcast([P, nt, NG]), ALU.is_equal))
                for g in range(NG):
                    oh = r_(400, nt * NG, a=nt)[:, :, g:g + 1].to_broadcast([P, nt, NPG])
                    dst = ein if g == 0 else r_(440, nt * NPG, a=nt)
                    link(dve.tensor_tensor(dst, Lg[:, 0:nt, NG + g * NPG:NG + (g + 1) * NPG], oh, ALU.mult))
                    if g:
                        link(dve.tensor_tensor(ein, ein, r_(440, nt * NPG, a=nt), ALU.add))
                for t in range(nt):
                    dve.max(mx8e[:, t, :], ein[:, t, :]).then_inc(sem("m8"), 1)
                dve.wait_ge(*after("m8", L, 3 * nt))
                for t in range(nt):
                    dve.max_index(u8[:, nt + t, :], mx8e[:, t, :], ein[:, t, :]).then_inc(sem("m8"), 1)
                dve.tensor_tensor(d21, mx8e[:, :, 1], mx8e[:, :, 0], ALU.subtract).then_inc(sem("gd"), 1)
                dve.wait_ge(*after("m8", L, 4 * nt))
                link(dve.tensor_copy(e12, u8[:, nt:2 * nt, 0:2].rearrange("p t k -> p k t")))
                link(dve.tensor_scalar(t6[:, 0, :], grp, float(NPG), None, ALU.mult))
                link(dve.tensor_tensor(e12, e12, t6[:, 0:1, :].to_broadcast([P, 2, nt]), ALU.add))
                for i, O in enumerate((O1, O2)):
                    link(dve.tensor_tensor(O, io.unsqueeze(1).to_broadcast([P, nt, NE]),
                                           e12[:, i, :].unsqueeze(2).to_broadcast([P, nt, NE]), ALU.is_equal))
                dve.tensor_tensor(Mb[:, 0:nt], O1, O2, ALU.add).then_inc(sem("Mb"), 1)
                link(dve.tensor_copy(trib[:, 0:P], tri))
                dve.memset(trib[:, P:2 * P], 1.0).then_inc(sem("Mb"), 1)
                dve.wait_ge(*after("gx", L, 2))
                link(dve.tensor_reduce(gs, gx, AX.X, ALU.add))
                link(dve.tensor_scalar(w12[:, 0, :], d21, 1.0, None, ALU.add))
                link(dve.tensor_tensor(gs, gs, w12[:, 0, :], ALU.mult))
                link(dve.reciprocal(w12[:, 0, :], gs))
                link(dve.tensor_tensor(w12[:, 1, :], w12[:, 0, :], d21, ALU.mult))
                dve.wait_ge(*after("rank_mm", L, 1))
                link(dve.tensor_copy(rank, ps[:, 2, 0:nt * NE].rearrange("p (t e) -> p t e", e=NE)))
                link(dve.tensor_copy(cnt, ps[:, 2, nt * NE:(nt + 1) * NE]))
                link(dve.memset(nb, 1.0))
                link(dve.memset(one32, 1.0))
                for n in range(1, nt):
                    link(dve.tensor_scalar(bs, cnt, float(n * BLK), None, ALU.is_gt))
                    link(dve.tensor_tensor(nb, nb, bs, ALU.add))
                link(dve.tensor_tensor_scan(inc, one32, nb, 0.0, ALU.mult, ALU.add))
                link(dve.tensor_tensor(bs, inc, nb, ALU.subtract))
                for c0 in range(0, NBMAX, NBMAX // 2):
                    n2 = NBMAX // 2
                    jt = r_(1500, n2 * NE, a=n2)
                    link(dve.tensor_tensor(jt, jm[:, c0:c0 + n2, :], inc.unsqueeze(1).to_broadcast([P, n2, NE]), ALU.is_ge))
                    link(dve.tensor_reduce(ebf[:, c0:c0 + n2], jt, AX.X, ALU.add))
                link(dve.tensor_scalar(ebf[:, 0:NBMAX], ebf[:, 0:NBMAX], float(NE - 1), None, ALU.min))
                hb = mc[:, P + NBMAX * NE + NE:P + NBMAX * NE + NE + NBMAX]
                link(dve.tensor_tensor(hb, hb, inc[:, NE - 1:NE].to_broadcast([P, NBMAX]), ALU.is_lt))
                link(dve.tensor_reduce(ebf[:, NBMAX:NBMAX + 1], hb[:, 0:NBMAX:2], AX.X, ALU.add))
                link(dve.tensor_scalar(ebf[:, NBMAX + 1:NBMAX + 2], ebf[:, NBMAX:NBMAX + 1], 2.0, -2.0, ALU.mult, ALU.add))
                dve.tensor_copy(ebi[0:1, :], ebf[0:1, :]).then_inc(sem("plan"), 1)
                for i, O in enumerate((O1, O2)):
                    for dst, tab in ((rk, rank), (bb, bs.unsqueeze(1).to_broadcast([P, nt, NE]))):
                        t4 = tmp4.rearrange("p (a b) -> p a b", a=nt)
                        link(dve.tensor_tensor(t4, O, tab, ALU.mult))
                        link(dve.tensor_reduce(dst[:, i, :], t4, AX.X, ALU.add))
                link(dve.tensor_scalar(rj, rk, float(BLK), None, ALU.is_ge))
                for n in range(2, nt):
                    link(dve.tensor_scalar(t6, rk, float(n * BLK), None, ALU.is_ge))
                    link(dve.tensor_tensor(rj, rj, t6, ALU.add))
                link(dve.tensor_tensor(bb, bb, rj, ALU.add))
                link(dve.tensor_scalar(rj, rj, float(-BLK), None, ALU.mult))
                link(dve.tensor_tensor(rk, rk, rj, ALU.add))
                link(dve.tensor_scalar(t6, bb, float(BLK), None, ALU.mult))
                link(dve.tensor_tensor(sl[:, 0:2, :], t6, rk, ALU.add))
                link(dve.tensor_scalar(t6, rk, float(NBMAX), None, ALU.mult))
                link(dve.tensor_tensor(sl[:, 2:4, :], t6, bb, ALU.add))
                dve.tensor_copy(slots[:, :, 0:nt], sl).then_inc(sem("slots"), 1)
                npairs = dve.value_load(ebi[0:1, NBMAX:NBMAX + 1], min_val=NE // 2, max_val=NBMAX // 2)

                def blocks(i):
                    first = isinstance(i, int)
                    for b in range(2):
                        j = 2 * i + b
                        if not first:
                            reg_wait(dve, sem(f"g_mm{L}"), j - 1)
                        reg_wait(dve, sem(f"xt_mm{L}"), j + 1)
                        dve.tensor_copy(XT[b][:, 4:8, :], ps[:, 1, :].rearrange("p (k t) -> p k t", k=4)).then_inc(sem(f"xt_v{L}"), 1)
                    for b in range(2):
                        j = 2 * i + b
                        reg_wait(dve, sem(f"sg{L}"), j + 1)
                        if not first:
                            reg_wait(dve, sem(f"ht_mm{L}"), j - 1)
                        dve.tensor_tensor(hid[b], ps[:, 2 + b, DE:2 * DE], sg[b], ALU.mult).then_inc(sem(f"hid{L}"), 1)
                    for b in range(2):
                        j = 2 * i + b
                        reg_wait(dve, sem(f"ht_mm{L}"), j + 1)
                        dve.tensor_copy(hidT[b], ps[:, 4, 0:256].rearrange("p (k t) -> p k t", k=2)).then_inc(sem(f"hidT{L}"), 1)
                        if not first:
                            reg_wait(dve, sem(f"yst{b}_{L}"), 16 * i, 16)
                        reg_wait(dve, sem(f"d_mm{L}"), j + 1)
                        dve.tensor_copy(YB[b][:, 512:1024], ps[:, 6, :]).then_inc(sem(f"yev_v{L}"), 1)

                blocks(0)
                with dve.Fori(1, npairs) as i:
                    blocks(i)
                for t in tiles(L):
                    s = 1 if t < CTX // P else 0
                    i = t - first_tile(L)
                    dve.wait_ge(*after(f"yg{t % 2}", L, 32 * (i // 2 + 1)))
                    if i >= 2:
                        dve.wait_ge(*after("yc_mm", L, i - 1))
                    y = WE[t % 2]
                    dve.tensor_scalar(XB[t % 2], y[:, 0:D], w12[:, 0, i:i + 1], None, ALU.mult).then_inc(sem("yc"), 1)
                    dve.wait_ge(*after("yc", L, 2 * i + 1))
                    dve.scalar_tensor_tensor(out=XB[t % 2], in0=y[:, D:2 * D], scalar=w12[:, 1, i:i + 1], in1=XB[t % 2],
                                             op0=ALU.mult, op1=ALU.add).then_inc(sem("yc"), 1)
                    dve.wait_ge(*after("yc_mm", L, i + 1))
                    for m in range(KD):
                        x = xT[:, m, t * P:(t + 1) * P]
                        dve.scalar_tensor_tensor(out=x, in0=pair(2 * (t % 2))[:, m * P:(m + 1) * P], scalar=modT[:, 40 + m, s:s + 1],
                                                 in1=x, op0=ALU.mult, op1=ALU.add).then_inc(sem("x_end"), 1)
                dve.wait_ge(*after("x_end", L, KD * ntile(L)))
                dve.memset(gg[:, 0, 0:1], 0.0).then_inc(sem("final_vec"), 1)
                dve.wait_ge(*after("final_vec", L, 1))

            dve.wait_ge(sem("rstd_fin"), 1)
            for m in range(KD):
                for s0, s1, s in SEG[1:]:
                    dve.scalar_tensor_tensor(out=hT[:, m, s0:s1], in0=xT[:, m, s0:s1], scalar=vec[:, V_FIN + m:V_FIN + m + 1],
                                             in1=rstd[:, s0:s1], op0=ALU.mult, op1=ALU.mult).then_inc(sem("h_fin"), 1)


        @block.gpsimd
        def _(pool):
            def after_wait(s, v, c=1):
                pool.wait_ge(s, v)
                pool.tensor_tensor(nil[:, c:c + 1], nil[:, 0:1], nil[:, 0:1], ALU.add)

            pool.memset(nil[:], 0.0).then_inc(sem("clr"), 1)
            pool.memset(zeros, 0.0).then_inc(sem("clr"), 1)
            pool.wait_ge(sem("clr"), 2)
            for j in range(NE, NBMAX):
                pool.dma_start(yrow[j * BLK:(j + 1) * BLK, :], zeros).then_inc(sem("yclr"), 16)
            pool.iota(tokid[:], pattern=[[P, TT]], base=0, channel_multiplier=1).then_inc(sem("clr"), 1)
            for L in range(DEPTH):
                pool.memset(idx0[:], 0).then_inc(sem("idx0"), 1)
                for u in range(UNITS):
                    h, d, n, part = unit(u)
                    pool.wait_ge(*after("ee", L, u + 1))
                    pool.wait_ge(*after("k", L, u + 1))
                    if u:
                        pool.wait_ge(*(after("pS_mm", L, 2 * u) if silent(L, u - 1) else after("o_mmh", L, 2 * spoken(L, u))))
                    i0, i1 = (0, 7) if not silent(L, u) else (6, 7) if d == 0 else (0, 1)
                    pool.tensor_tensor(KL[:, i0:i1, :], E[:, 1 - d + i0:1 - d + i1, :], kk[:, u % 2, :].unsqueeze(1).to_broadcast([P, i1 - i0, PART]),
                                       ALU.mult).then_inc(sem("kl"), 1)
                pool.wait_ge(*after("slots", L, 1))
                pool.wait_ge(*after("idx_clr", L, 16))
                pool.wait_ge(sem("clr"), 3)
                for t in tiles(L):
                    n = t - first_tile(L)
                    for i in range(2):
                        pool.indirect_dma_start(
                            out=idxd[L], out_offset=bass.IndirectOffsetOnAxis(ap=slots[:, 2 + i, n:n + 1], axis=0),
                            in_=tokid[:, t:t + 1], in_offset=None).then_inc(sem("idx_sc"), 16)
                pool.wait_ge(*after("idxs", L, 16))
                for i in range(2):
                    pool.wait_ge(*after(f"hrow{i}", L, 16 * (ntile(L) // 2)))
                npairs = pool.value_load(ebi[0:1, NBMAX:NBMAX + 1], min_val=NE // 2, max_val=NBMAX // 2)

                def blocks(i):
                    for b in range(2):
                        j = 2 * i + b
                        if not isinstance(i, int):
                            reg_wait(pool, sem(f"xt_mm{L}"), j - 1)
                        pool.tensor_copy(idxc[:, b:b + 1], idxs[:, bass.ds(j, 1)]).then_inc(sem(f"idxc{L}"), 1)
                        after_wait(sem(f"idxc{L}"), j + 1)
                        pool.indirect_dma_start(
                            out=XB[b], out_offset=None, in_=hrow,
                            in_offset=bass.IndirectOffsetOnAxis(ap=idxc[:, b:b + 1].bitcast(U32), axis=0)).then_inc(sem(f"xg{b}_{L}"), 16)

                blocks(0)
                with pool.Fori(1, npairs) as i:
                    blocks(i)
                for b in range(2):
                    after_wait(sem(f"yst{b}_{L}"), 16 * npairs, 2 + b)
                for t in tiles(L):
                    n = t - first_tile(L)
                    if n >= 2:
                        pool.wait_ge(*after("yc", L, 2 * (n - 1)))
                    for i in range(2):
                        pool.indirect_dma_start(
                            out=WE[t % 2][:, i * D:(i + 1) * D], out_offset=None, in_=yrow,
                            in_offset=bass.IndirectOffsetOnAxis(ap=slots[:, i, n:n + 1], axis=0)).then_inc(sem(f"yg{t % 2}"), 16)


def HEADS_S(u, n):
    scan, part = divmod(u, NPART)
    return 13 * scan + 1 + 4 * part + n


SCORES = [(s, CTX, TOK) for s in range(0, TOK, P)] + [(s, 0, CTX) for s in range(0, CTX, P)]
PT_AT = [sum(q1 - q0 for _, q0, q1 in SCORES[:n]) for n in range(len(SCORES))]




def nscore(L):
    return len(SCORES) if L < DEPTH - 1 else len(SCORES) - CTX // P


def tile_start(L, name):
    return 0 if name in ("ff", "fb", "rk", "v", "rv0", "rv1") else first_tile(L) * P


_INS = ["x", "c", "ctx", "c_ctx", "w_mod", "b_mod", "norm_mix_w", "norm_ffn_w", "w_in", "hgrn_lb_logits", "hgrn_norm_w",
        "ret_decay_logit", "ret_gn_w", "w_o_hgrn", "w_o_ret", "w_out", "router_group_w", "router_group_b",
        "router_expert_w", "router_expert_b", "expert_w_gate", "expert_w_up", "expert_w_down", "final_norm_w"]


def tables():
    import numpy as np
    f = np.float32
    cst = np.zeros((P, 2 * P + 2 * 7 * C), f)
    cst[:, 0:P] = np.eye(P)
    cst[:, P:2 * P] = 1.0 / D
    s, t = np.meshgrid(np.arange(C), np.arange(C), indexing="ij")
    for d in range(2):
        m = np.zeros((C, 7, C), f)
        for l in range(LEVELS):
            w = C >> l
            same = s // w == t // w
            first, second = (s, t) if d == 0 else (t, s)
            m[:, l, :] = same & (first % w < w // 2) & (second % w >= w // 2)
        m[:, 6, :] = np.eye(C) * QSCALE
        cst[:, 2 * P + d * 7 * C:2 * P + (d + 1) * 7 * C] = np.tile(m.reshape(C, -1), (2, 1))
    rc = np.zeros((P, 2 * LAT + P + 3 * XW), f)
    pos = np.arange(LAT)
    inv = (10000.0 ** (-np.arange(0, 64, 2, dtype=f) / f(64))).astype(f)
    for half, x in enumerate((pos // 64, pos % 64)):
        ang = (inv[:, None] * x[None, :].astype(f)).astype(f)
        for i, sign in ((0, -1.0), (1, 1.0)):
            r = slice(64 * half + 32 * i, 64 * half + 32 * (i + 1))
            rc[r, 0:512] = np.cos(ang)
            rc[r, 512:1024] = sign * np.sin(ang)
    for i in range(P):
        rc[i ^ 32, 1024 + i] = 1.0
    xx = np.arange(XW)[None, :] - 384 - np.arange(P)[:, None]
    rc[:, 1152:1152 + XW] = xx
    rc[:, 1152 + XW:1152 + 2 * XW] = np.maximum(xx, 0)
    rc[:, 1152 + 2 * XW:] = np.maximum(-xx, 0)
    mc = np.zeros((P, P + NBMAX * NE + NE + NBMAX), f)
    mc[:, 0:P] = np.triu(np.ones((P, P)), 1)
    mc[:, P:P + NBMAX * NE] = np.repeat(np.arange(NBMAX), NE)[None, :]
    mc[:, P + NBMAX * NE:P + NBMAX * NE + NE] = np.arange(NE)[None, :]
    mc[:, P + NBMAX * NE + NE:] = np.arange(NBMAX)[None, :]
    return {"cst": cst, "rc": rc, "mc": mc}


def kernel(**inputs):
    import numpy as _np
    import concourse.bacc as _bacc
    from concourse import mybir as _mybir
    from concourse.bass_utils import run_bass_kernel_spmd as _run

    nc = _bacc.Bacc("TRN2", target_bir_lowering=False, num_devices=1)
    arrays, aps = {}, {}
    data = {n: _np.ascontiguousarray(inputs[n]) for n in _INS}
    data.update(tables())
    for name, x in data.items():
        arrays[f"in_{name}"] = x
        aps[name] = nc.dram_tensor(f"in_{name}", x.shape, _mybir.dt.from_np(x.dtype), kind="ExternalInput").ap()
    aps["out"] = nc.dram_tensor("out_0", (1, LAT, D), _mybir.dt.float32, kind="ExternalOutput").ap()
    build(nc, aps)
    r = _run(nc, [arrays], core_ids=[0])
    return r.results[0]["out_0"]
```

```python
from contextlib import ExitStack

import concourse.bass as bass
from concourse import mybir

F32 = mybir.dt.float32
F32R = mybir.dt.float32r
BF16 = mybir.dt.bfloat16
I32 = mybir.dt.int32
U32 = mybir.dt.uint32
ALU = mybir.AluOpType
ACT = mybir.ActivationFunctionType
AX = mybir.AxisListType

P = 128
D = 1024
KD = D // P
LAT, CTX = 512, 256
TOK = CTX + LAT
TT = TOK // P
DEPTH = 2
SEG = ((0, CTX, 1), (CTX, TOK, 0))
HEADS = 4
DV = 256
C = 64
LEVELS = 6
KPOOL = 4
PART = 256
NPART = TOK // PART
UNITS = HEADS * 2 * NPART
EPS = 1e-6
F_MIN = 1e-30
QSCALE = float(P) ** -0.5
NG, NPG = 4, 8
NE = NG * NPG
DE = 256
BLK = 128
TOPK = 2
NBMAX = NE + TOPK * TOK // BLK
NBMAX += NBMAX % 2
CAP = NBMAX * BLK
MC = P + NBMAX * NE + NE + NBMAX + P + TT + 1
XW = TOK + P

GROUPS = [("ff", 512, 0), ("fb", 1024, 0), ("q", 0, 0), ("v", 1536, 1), ("g", 2048, 0),
          ("rq", 2560, 0), ("rk", 3072, 0), ("rv0", 3584, 1), ("rv1", 4096, 1), ("rg0", 4608, 0), ("rg1", 5120, 0),
          ("ga0", 5632, 0), ("ga1", 6144, 0), ("gb0", 6656, 0), ("gb1", 7168, 0)]
NHG = 5
TILES = [(g, m) for g, (_, _, tm) in enumerate(GROUPS) for m in range(4)]
TILES_HG = sum(1 for g, _ in TILES if g < NHG)
STEPS = len(TILES) - TILES_HG
SCR = {"rq": 0, "rk": 4, "rg0": 8, "rg1": 12, "ga0": 16, "ga1": 20, "gb0": 24, "gb1": 28}
LAST_USE = {}
for _g in range(1, len(GROUPS)):
    for _m in range(4):
        LAST_USE.setdefault(4 * (_g - 1) + (2 * (_m // 2) + 1 if GROUPS[_g - 1][2] else _m), []).append(4 * _g + _m)
EARLY = STEPS * 5 // 8
AHEAD = 4
UNIT_AT = {u * (STEPS + AHEAD - 1) // UNITS - AHEAD: u for u in range(UNITS)}
NMOD = 6 * D // 512
USES = NMOD + len(GROUPS) + 4

V_BMOD, V_MIX, V_FFN, V_HGN, V_GN, V_FIN, V_RB, V_LB, V_N = 0, 48, 56, 64, 68, 76, 84, 85, 101


PER_LAYER = {}
for _n, _names in (
        (NMOD, "mod_mm mod_ev"), (len(TILES), "proj_mm proj_ev"), (len(TILES) + 16, "whi wlo"), (HEADS * TT, "rghi rglo"), (KD, "mhi mlo"), (KD, "y_mm y_ev out_mm sq_mix sq_ffn"),
        (16 * 12, "vec_ld"), (1, "final_vec idx0 plan slots vec_mm modT_mm ms_mix ms_ffn rstd_mix rstd_ffn lg_mm lgT Lg_mm rank_mm amod"),
        (16 * STEPS // 2, "spill0 spill1"), (16, "rot_ld x_spill x_back wohg mc_ld idx_clr idxs"), (HEADS, "hgate oT_mm hr"), (16, "rg_ld dist_ld"),
        (HEADS * TT, "pv_mm rg_done on ro_ev roT_mm rvar rr"), (48 * HEADS // 2, "rqkv0 rqkv1"), (32 * KD // 2, "gab0 gab1"),
        (2 * KD, "x_mid hlo h_mix h_ffn hm_mix hm_ffn"), (TT, "hstg hrow_mm yc_mm"), (16 * TT // 2, "hrow0 hrow1"),
        (32 * TT, "idx_sc"), (KD * TT, "x_end"), (UNITS, "ql kl dcy f k k1 lnf dd ee"),
        (2 * UNITS, "sc_ev sc_mm kT kT_mm pS_mm scT o_mmh o_evh"), (13 * 2 * HEADS, "S"), (8 * HEADS, "rsc_ev rsc_mm"),
        (2 * HEADS, "rot_mm rot"), (2, "Mb gd"), (3, "gx"), (1, "onehot idx_mm idxs"), (TT, "yc yp"), (3, "pre pre_a"), (4 * HEADS, "dt"), (4 * TT, "m8"),
        (32 * TT // 2, "yg0 yg1")):
    for _name in _names.split():
        PER_LAYER[_name] = _n


def first_tile(L):
    return 0 if L < DEPTH - 1 else CTX // P


def tiles(L):
    return range(first_tile(L), TT)


def ntile(L):
    return len(tiles(L))


def segs(L):
    return SEG if L < DEPTH - 1 else SEG[1:]


def silent(L, u):
    return L == DEPTH - 1 and u % NPART == 0


def spoken(L, u):
    return sum(not silent(L, v) for v in range(u))


def unit(u):
    h, r = divmod(u, 2 * NPART)
    d, n = divmod(r, NPART)
    part = n if d == 0 or n == 0 else NPART - n
    return h, d, n, part


def build(nc, a):
    with ExitStack() as ctx:
        def sb(name, shape, dt=F32):
            return ctx.enter_context(nc.sbuf_tensor(name, shape, dt))

        sems = {}

        def sem(name):
            if name not in sems:
                sems[name] = ctx.enter_context(nc.semaphore(name))
            return sems[name]

        def after(name, L, n):
            return sem(name), L * PER_LAYER.get(name, 0) + n

        at = -(-nc.sbuf_base // 32) * 32
        xT = sb("xT", [P, KD, TOK])
        hT = sb("hT", [P, KD, TOK])
        ring = sb("ring", [P, 2, KD, 512])
        hhi = nc.alloc_sbuf_tensor_at("hhi", [P, KD, TOK], F32R, offset=at)
        hlo = nc.alloc_sbuf_tensor_at("hlo", [P, KD, TOK], F32R, offset=at + 4 * KD * TOK)
        wlo = nc.alloc_sbuf_tensor_at("wlo", [P, 2, KD, 512], F32R, offset=at + 8 * KD * TOK)
        cst = sb("cst", [P, 2 * P + 2 * 7 * C])
        ident, meanw = cst[:, 0:P], cst[:, P:2 * P]
        masks = [cst[:, 2 * P + i * 7 * C:2 * P + (i + 1) * 7 * C].rearrange("p (l t) -> p l t", l=7) for i in range(2)]
        eps = sb("eps", [P, 1])
        cT = sb("cT", [P, 16])
        vrow = sb("vrow", [V_N, P])
        vec = sb("vec", [P, V_N])
        modT = sb("modT", [P, 48, 2])
        amod = sb("amod", [P, 2, KD, 2])
        lbm = sb("lbm", [P, 4, 8])
        dec = sb("dec", [P, 6, 8])
        wrt = sb("wrt", [P, KD, NG + NE])
        AR = 29856
        at = -(-nc.sbuf_base // 32) * 32
        arena = sb("arena", [P, AR])
        whi = nc.alloc_sbuf_tensor_at("whi", [P, KD, 512], F32R, offset=at + 4 * 25760)
        rglo = nc.alloc_sbuf_tensor_at("rglo", [P, KD, TOK], F32R, offset=at + 4 * 15360)
        mlo = nc.alloc_sbuf_tensor_at("mlo", [P, KD, TOK], F32R, offset=at)
        mhi5 = nc.alloc_sbuf_tensor_at("mhi5", [P, 5, TOK], F32R, offset=at + 4 * 21504)
        mhi3 = nc.alloc_sbuf_tensor_at("mhi3", [P, 3, TOK], F32R, offset=at + 4 * 9984)

        def ar(off, n, **kw):
            assert off + n <= AR
            v = arena[:, off:off + n]
            return v.rearrange("p (a b) -> p a b", **kw) if kw else v

        xrow = ar(0, TT * D, a=TT)
        ccrow = ar(28000, P)[0:16]
        rstd = ar(12288, TOK)
        mrow = hT[:].rearrange("p k t -> p (k t)")
        squares = ar(0, 6144, a=KD)
        hq = ar(0, 3072, a=4)
        sig = [ar(3072, 3072, a=4), ar(6144, 3072, a=4)]
        hv = ar(9216, 3072, a=TT)
        hgate = ar(12288, 3072, a=4)
        E = ar(15360, 8 * PART, a=8)
        QL = ar(17408, 7 * PART, a=7)
        KL = ar(19200, 7 * PART, a=7)
        Pc = ar(20992, 4 * (C + 1), a=4)
        ff = ar(21252, PART)
        kk = sb("kk", [P, 2, PART])
        dcy = sb("dcy", [P, 4])
        gg = ar(21764, 4 * (C + 1), a=4)
        keep = ar(22024, 4 * (C + 1), a=4)
        msk = ar(22284, 7 * C, a=7)
        scT = ar(22732, C)
        kTs = ar(22796, P)
        S = ar(22924, 3 * P, a=3)
        oacc = ar(23308, TT * P, a=TT)
        stage = [ar(24076, TOK), ar(24844, TOK)]
        zeros = ar(24076, D)
        junk = ar(25612, P)
        ss = ar(25740, 16)
        rgate = ar(15360, 6144, a=8)
        rqk = [ar(0, 1536, a=2), ar(1536, 1536, a=2)]
        rv = [ar(3072, 1536, a=TT), ar(4608, 1536, a=TT)]
        NROT = 2 * LAT + P
        rot = ar(6144, NROT)
        cosT, sinT, perm = rot[:, 0:LAT], rot[:, LAT:2 * LAT], rot[:, 2 * LAT:NROT]
        rtmp = ar(7296, LAT)
        PT = ar(7808, 3584)
        Wd = ar(11392, XW)
        Dc = ar(21504, XW)
        wtmp = ar(22400, XW)
        dtmp = ar(28448, XW)
        on = ar(24192, 512, a=2)
        rst = ar(24704, 64)
        dist = ar(25760, 3 * XW)
        XX, XP, XN = [dist[:, i * XW:(i + 1) * XW] for i in range(3)]
        merged = ar(0, 6144, a=8)
        gab = [ar(6144, 1536, a=2), ar(7680, 1536, a=2)]
        ytmp = ar(9216, TOK)
        WE = [ar(i * 6144, 6144) for i in range(2)]
        XB = [ar(12288 + i * 1024, 1024) for i in range(2)]
        XT = [ar(14336 + i * 1024, 1024, a=8) for i in range(2)]
        sg = [ar(16384 + i * 256, 256) for i in range(2)]
        hid = [ar(16896 + i * 256, 256) for i in range(2)]
        hidT = [ar(17408 + i * 256, 256, a=2) for i in range(2)]
        YB = [ar(17920 + i * 1024, 1024) for i in range(2)]
        mc = ar(20000, MC)
        tri, jm = mc[:, 0:P], mc[:, P:P + NBMAX * NE].rearrange("p (j e) -> p j e", e=NE)
        io = mc[:, P + NBMAX * NE:P + NBMAX * NE + NE]
        jrow = mc[:, P + NBMAX * NE + NE:MC - P - TT - 1]
        prow, tnum, pcol = mc[:, MC - P - TT - 1:MC - TT - 1], mc[:, MC - TT - 1:MC - 1], mc[:, MC - 1:MC]
        lgT = ar(21752, TOK)
        Lg = ar(22522, TT * 36, a=TT)
        ro = ar(22752, 2248)
        hstg = [ar(25000, 1024), ar(26024, 1024)]
        nil = sb("nil", [P, 4])
        trib = ar(27100, P).bitcast(BF16)
        Mb = sb("Mb", [P, TT, NE], BF16)
        u8 = sb("u8", [P, 2 * TT, 8], U32)
        slots = sb("slots", [P, 2, TT], U32)
        OP = ar(14336, TOPK * TT * P // 2).bitcast(BF16).rearrange("p (a b) -> p a b", a=TOPK * TT)
        OB = ar(15104, 3 * TOPK * TT * NBMAX // 2).bitcast(BF16).rearrange("p (c a b) -> p c a b", c=3, a=TOPK * TT)
        idxs = sb("idxs", [P, NBMAX], I32)
        idxc = sb("idxc", [P, 2], I32)
        ebi = sb("ebi", [1, NBMAX + 2], I32)

        ps = ctx.enter_context(nc.psum_tensor("ps", [P, 8, 512], F32))

        def pair(b):
            return ps[:, b:b + 2, :].rearrange("p b n -> p (b n)")

        def tokens(b):
            return pair(b)[:, 256:1024]

        def dram(name, shape, dt=F32):
            return nc.dram_tensor(name, shape, dt, kind="Internal").ap()

        xsp = dram("xsp", (P, KD, TOK))
        scr = dram("scr", (32, P, TOK))
        scrv = dram("scrv", (TOK, 1024))
        hrow = dram("hrow", (TOK, D))
        yrow = dram("yrow", (CAP, D))

        def uses(L):
            out = [a["w_mod"][L][:, g * 512:(g + 1) * 512] for g in range(NMOD)]
            out += [a["w_in"][L][:, c:c + 512] for _, c, _ in GROUPS]
            out += [a[n][L][:, c:c + 512] for n in ("w_o_ret", "w_out") for c in (0, 512)]
            return [x.rearrange("(k p) n -> p k n", p=P) for x in out]

        def used(L, n):
            if n < NMOD:
                return after("mod_mm", L, n + 1)
            n -= NMOD
            if n < len(GROUPS):
                return after("proj_mm", L, 1 + max(i for i, (g, _) in enumerate(TILES) if g == n))
            n -= len(GROUPS)
            return after("y_mm", L, 4 * (n + 1)) if n < 2 else after("out_mm", L, 4 * (n - 1))

        stream = [(L, n, x) for L in range(DEPTH) for n, x in enumerate(uses(L))]

        def ring_ready(eng, L, n):
            i = L * USES + n
            eng.wait_ge(sem(f"ring{i % 2}"), 16 * (i // 2 + 1))

        def reg_wait(eng, s, v, least=1):
            eng.wait_ge(s, v)
            if not isinstance(v, int):
                eng.wait_ge(s, least)

        def ret_transposes(pe, L, i):
            pe.wait_ge(*after("ro_ev", L, i + 1))
            if i >= 2:
                pe.wait_ge(*after("rg_done", L, i - 1))
            for e in range(2):
                mm = pe.transpose(ps[:, 6 + i % 2, e * P:(e + 1) * P], on[:, i % 2, e * P:(e + 1) * P], ident)
            mm.then_inc(sem("roT_mm"), 1)

        def head_gate(dve, L, h):
            dve.wait_ge(*after("oT_mm", L, h + 1))
            dve.wait_ge(*after("proj_ev", L, TILES_HG))
            s0 = first_tile(L) * P
            dve.scalar_tensor_tensor(out=hgate[:, h, s0:TOK], in0=pair(6)[:, s0:TOK], scalar=vec[:, V_HGN + h:V_HGN + h + 1],
                                     in1=hgate[:, h, s0:TOK], op0=ALU.mult, op1=ALU.mult).then_inc(sem("hgate"), 1)

        def ret_gate(dve, L, i):
            h, t = divmod(i, ntile(L))
            t += first_tile(L)
            dve.wait_ge(*after("roT_mm", L, i + 1))
            for e in range(2):
                x = rgate[:, 2 * h + e, t * P:(t + 1) * P]
                ins = dve.scalar_tensor_tensor(out=x, in0=ps[:, 6 + i % 2, e * P:(e + 1) * P], scalar=vec[:, V_GN + 2 * h + e:V_GN + 2 * h + e + 1],
                                               in1=x, op0=ALU.mult, op1=ALU.mult)
            ins.then_inc(sem("rg_done"), 1)

        def mhi(m):
            return mhi5[:, m, :] if m < 5 else mhi3[:, m - 5, :]

        def mod_bank(L, g):
            return g if L and g < 2 else 4 + g % 2

        def split_weights(L, q):
            return (L * USES + NMOD + len(GROUPS) + q // 4) % 2, slice((q % 4) * P, (q % 4 + 1) * P)

        block = ctx.enter_context(nc.Block())

        @block.sync
        def _(sp):
            def fill(i):
                if i >= len(stream):
                    return
                if i >= 2:
                    sp.wait_ge(*used(*stream[i - 2][:2]))
                sp.dma_start(ring[:, i % 2], stream[i][2]).then_inc(sem(f"ring{i % 2}"), 16)

            def head_load(L, h):
                s0 = first_tile(L) * P
                ld = sem(f"rqkv{h % 2}")
                sp.dma_start(rqk[h % 2][:, 0, s0:TOK], scr[h][:, s0:TOK]).then_inc(ld, 16)
                sp.dma_start(rqk[h % 2][:, 1], scr[4 + h]).then_inc(ld, 16)
                sp.dma_start(rv[h % 2], scrv[:, h * DV:(h + 1) * DV].rearrange("(t p) n -> p t n", p=P)).then_inc(ld, 16)

            def weights(L, i, b, which, e=None):
                if e is None:
                    e = sp.value_load(ebi[0:1, bass.ds(2 * i + b, 1)], min_val=0, max_val=NE - 1)
                w = WE[b]
                if isinstance(e, int):
                    sel = slice(e, e + 1)
                else:
                    sel = bass.ds(e, 1)
                if not isinstance(i, int):
                    sp.wait_ge(sem(f"d_mm{L}" if which else f"g_mm{L}"), 2 * i + b - 1)
                if which == 0:
                    for n, o in (("expert_w_gate", 0), ("expert_w_up", 256)):
                        dst = w[:, 0:4096].rearrange("p (k n) -> p k n", k=8)[:, :, o:o + 256]
                        src = a[n][L].rearrange("e (p k) n -> e p k n", k=8)[sel].rearrange("e p k n -> (e p) k n")
                        sp.dma_start(dst, src).then_inc(sem(f"wgu{b}_{L}"), 16)
                else:
                    src = a["expert_w_down"][L].rearrange("e (p k) n -> e p (k n)", k=2)[sel].rearrange("e p n -> (e p) n")
                    sp.dma_start(w[:, 4096:6144], src).then_inc(sem(f"wd{b}_{L}"), 16)

            def vectors(L):
                vl = sem("vec_ld")
                for r, x in ((V_BMOD, a["b_mod"][L]), (V_MIX, a["norm_mix_w"][L]), (V_FFN, a["norm_ffn_w"][L]),
                             (V_HGN, a["hgrn_norm_w"][L]), (V_GN, a["ret_gn_w"][L]), (V_FIN, a["final_norm_w"])):
                    x = x.rearrange("(k p) -> k p", p=P)
                    sp.dma_start(vrow[r:r + x.shape[0], :], x).then_inc(vl, 16)
                sp.dma_start(vrow[V_LB:V_LB + 16, :], a["hgrn_lb_logits"].rearrange("d l (h p) -> (d l h) p", p=P)).then_inc(vl, 16)
                sp.dma_start(vrow[V_RB:V_RB + 1, 0:NG], a["router_group_b"][L:L + 1, :]).then_inc(vl, 16)
                sp.dma_start(vrow[V_RB:V_RB + 1, NG:NG + NE], a["router_expert_b"][L:L + 1, :]).then_inc(vl, 16)
                sp.dma_start(dec[:, 0, :], a["ret_decay_logit"][L].rearrange("d h -> (d h)").partition_broadcast(P)).then_inc(vl, 16)
                sp.dma_start(wrt[:, :, 0:NG], a["router_group_w"][L].rearrange("(k p) n -> p k n", p=P)).then_inc(vl, 16)
                sp.dma_start(wrt[:, :, NG:NG + NE], a["router_expert_w"][L].rearrange("(k p) n -> p k n", p=P)).then_inc(vl, 16)

            def modulation_weights(L):
                for n in range(2 if L else 0, NMOD):
                    if n == NMOD - 1:
                        if L:
                            sp.wait_ge(*after("x_end", L - 1, KD * ntile(L - 1)))
                        else:
                            sp.wait_ge(sem("x_cp"), KD)
                        sp.dma_start(xsp, xT[:]).then_inc(sem("x_spill"), 16)
                    fill(L * USES + n + 2)

            sp.dma_start(cst[:], a["cst"]).then_inc(sem("cst_ld"), 16)
            sp.dma_start(ccrow[0:8, :], a["c"].rearrange("a (k p) -> (a k) p", p=P)).then_inc(sem("cst_ld"), 16)
            sp.dma_start(ccrow[8:16, :], a["c_ctx"].rearrange("(k p) -> k p", p=P)).then_inc(sem("cst_ld"), 16)
            fill(0)
            sp.dma_start(xrow[:, 0:2, :], a["ctx"][0].rearrange("(t p) d -> p t d", p=P)).then_inc(sem("x_ld"), 16)
            sp.dma_start(xrow[:, 2:6, :], a["x"][0].rearrange("(t p) d -> p t d", p=P)).then_inc(sem("x_ld"), 16)
            fill(1)
            sp.wait_ge(sem("init"), 1)
            vectors(0)
            for L in range(DEPTH):
                base = L * USES
                if L == 0:
                    modulation_weights(0)
                for k, (g, m) in enumerate(TILES):
                    i = k - TILES_HG
                    if i >= 0:
                        sp.wait_ge(*after("proj_ev", L, k + 1))
                        name, _, tm = GROUPS[g]
                        if tm:
                            c0 = (512 if name == "rv1" else 0) + 256 * (m // 2)
                            t0 = 3 * (m % 2)
                            dst = scrv[t0 * P:(t0 + 3) * P, c0:c0 + 256].rearrange("(b p) n -> p b n", p=P)
                            src = stage[i % 2].rearrange("p (b n) -> p b n", b=3)
                        else:
                            s0 = tile_start(L, name)
                            dst, src = scr[SCR[name] + m][:, s0:TOK], stage[i % 2][:, s0:TOK]
                        sp.dma_start(dst, src).then_inc(sem(f"spill{i % 2}"), 16)
                    if k + 1 == len(TILES):
                        sp.wait_ge(*after("proj_mm", L, len(TILES)))
                        sp.dma_start(dist, a["rc"][:, NROT:NROT + 3 * XW]).then_inc(sem("dist_ld"), 16)
                    if k + 1 == len(TILES) or TILES[k + 1][0] != g:
                        fill(base + NMOD + g + 2)
                    if i == EARLY:
                        sp.wait_ge(*after("o_evh", L, 2 * spoken(L, UNITS // 2)))
                        for j in range(2):
                            sp.wait_ge(*after(f"spill{j}", L, 16 * 8))
                        sp.dma_start(rot, a["rc"][:, 0:NROT]).then_inc(sem("rot_ld"), 16)
                        head_load(L, 0)

                for i in range(2):
                    sp.wait_ge(*after(f"spill{i}", L, 16 * (STEPS // 2)))
                s0 = first_tile(L) * P
                sp.wait_ge(*after("o_evh", L, 2 * spoken(L, UNITS)))
                head_load(L, 1)
                sp.dma_start(rgate[:, :, s0:TOK], scr[8:16, :, s0:TOK].rearrange("m p t -> p m t")).then_inc(sem("rg_ld"), 16)
                wohg = hT[:].rearrange("p k t -> p (k t)")[:, 0:4096].rearrange("p (k n) -> p k n", k=4)
                sp.dma_start(wohg, a["w_o_hgrn"][L].rearrange("(k p) n -> p k n", p=P)).then_inc(sem("wohg"), 16)
                for h in range(2, HEADS):
                    sp.wait_ge(*after("pv_mm", L, ntile(L) * (h - 1)))
                    head_load(L, h)
                sp.wait_ge(*after("rg_done", L, HEADS * ntile(L)))
                for m in range(KD):
                    if m >= 2:
                        sp.wait_ge(*after("y_ev", L, m - 1))
                    sp.dma_start(gab[m % 2][:, 0, s0:TOK], scr[16 + m][:, s0:TOK]).then_inc(sem(f"gab{m % 2}"), 16)
                    sp.dma_start(gab[m % 2][:, 1, s0:TOK], scr[24 + m][:, s0:TOK]).then_inc(sem(f"gab{m % 2}"), 16)
                    if m in (3, 7):
                        fill(base + NMOD + len(GROUPS) + (0 if m == 3 else 1) + 2)
                sp.wait_ge(*after("y_mm", L, KD))
                sp.dma_start(xT[:], xsp).then_inc(sem("x_back"), 16)
                fill(base + NMOD + len(GROUPS) + 2 + 2)
                fill(base + NMOD + len(GROUPS) + 3 + 2)

                sp.wait_ge(*after("x_mid", L, len(segs(L)) * KD))
                sp.dma_start(mc, a["mc"]).then_inc(sem("mc_ld"), 16)
                for which in range(2):
                    weights(L, 0, 0, which, 0)
                for t in tiles(L):
                    sp.wait_ge(*after("hstg", L, t - first_tile(L) + 1))
                    sp.dma_start(hrow[t * P:(t + 1) * P, :], hstg[t % 2]).then_inc(sem(f"hrow{t % 2}"), 16)
                sp.wait_ge(*after("plan", L, 1))
                npairs = sp.value_load(ebi[0:1, NBMAX:NBMAX + 1], min_val=NE // 2, max_val=NBMAX // 2)

                last = sp.value_load(ebi[0:1, NBMAX + 1:NBMAX + 2], min_val=NE - 2, max_val=NBMAX - 2)

                def stores(i, b, j):
                    reg_wait(sp, sem(f"yev_a{L}"), 2 * i + b + 1)
                    reg_wait(sp, sem(f"yev_v{L}"), 2 * i + b + 1)
                    dst = yrow[bass.ds(j * BLK, BLK), :]
                    sp.dma_start(dst, YB[b]).then_inc(sem(f"yst{b}_{L}"), 16)

                for which in range(2):
                    weights(L, 0, 1, which)
                if L + 1 < DEPTH:
                    for n in range(2):
                        fill((L + 1) * USES + n + 2)
                with sp.Fori(1, npairs) as i:
                    for b in range(2):
                        weights(L, i, b, 0)
                    for b in range(2):
                        weights(L, i, b, 1)
                        stores(i - 1, b, 2 * i + b - 2)
                for b in range(2):
                    sp.wait_ge(sem(f"yev_a{L}"), last + b + 1)
                    sp.wait_ge(sem(f"yev_v{L}"), last + b + 1)
                    sp.dma_start(yrow[bass.ds((last + b) * BLK, BLK), :], YB[b]).then_inc(sem(f"yst{b}_{L}"), 16)
                if L + 1 < DEPTH:
                    vectors(L + 1)
                    modulation_weights(L + 1)

            for t in range(LAT // P):
                sp.wait_ge(*after("hstg", DEPTH - 1, LAT // P + t + 1))
                sp.dma_start(a["out"][0, t * P:(t + 1) * P, :], hstg[t % 2]).then_inc(sem(f"hrow{t % 2}"), 16)
            for i in range(2):
                sp.wait_ge(*after(f"hrow{i}", DEPTH - 1, 16 * (LAT // P)))


        @block.tensor
        def _(pe):
            def seg_mm(bank, lhsT, rhs, first, last, T=SEG):
                for s0, s1, _ in T:
                    b, c = (bank, 256) if s0 == 0 else (bank + 1, 0)
                    mm = pe.matmul(ps[0:lhsT.shape[1], b, c:c + s1 - s0], lhsT, rhs[:, s0:s1], start=first, stop=last)
                return mm

            def modulation(L, g):
                ring_ready(pe, L, g)
                if g >= 2:
                    pe.wait_ge(*after("mod_ev", L, g - 1))
                r = ring[:, (L * USES + g) % 2]
                for k in range(KD):
                    mm = pe.matmul(ps[0:2, mod_bank(L, g), :], cT[:, k:16:8], r[:, k, :], start=k == 0, stop=k == KD - 1)
                mm.then_inc(sem("mod_mm"), 1)

            def norm_sum(tag, L, T=SEG, sq=hT):
                for m in range(KD):
                    pe.wait_ge(*after(f"sq{tag}", L, m + 1))
                    mm = seg_mm(0, meanw, sq[:, m, :], m == 0, m == KD - 1, T)
                mm.then_inc(sem(f"ms{tag}"), 1)

            pe.wait_ge(sem("cst_ld"), 48)
            pe.transpose(ps[:, 7, 0:16], ccrow, ident[0:16, 0:16]).then_inc(sem("cc_mm"), 1)
            pe.wait_ge(sem("cT"), 1)
            modulation(0, 0)
            pe.wait_ge(sem("x_ld"), 32)
            for m in range(KD):
                b = 2 * (m % 2)
                if m >= 2:
                    pe.wait_ge(sem("x_cp"), m - 1)
                for t in range(TT):
                    mm = pe.transpose(tokens(b)[:, t * P:(t + 1) * P], xrow[:, t, m * P:(m + 1) * P], ident)
                mm.then_inc(sem("cc_mm"), 1)

            for L in range(DEPTH):
                if L == 0:
                    for g in range(1, NMOD):
                        modulation(0, g)
                pe.wait_ge(*after("vec_ld", L, 16 * 12))
                pe.transpose(ps[:, 7, 0:V_N], vrow[:], ident[0:V_N, 0:V_N]).then_inc(sem("vec_mm"), 1)
                pe.wait_ge(*after("mod_ev", L, NMOD))
                for j in range(48):
                    mm = pe.transpose(ps[:, 6, 2 * j:2 * j + 2], mrow[0:2, j * P:(j + 1) * P], ident[0:2, 0:2])
                mm.then_inc(sem("modT_mm"), 1)
                norm_sum("_mix", L, sq=squares)

                def head_transposes(h):
                    pe.wait_ge(*after("on", L, ntile(L) * (h + 1)))
                    for t in tiles(L):
                        mm = pe.transpose(pair(6)[:, t * P:(t + 1) * P], oacc[:, t, :], ident)
                    mm.then_inc(sem("oT_mm"), 1)

                def unit_products(u):
                    h, d, n, part = unit(u)
                    quiet = silent(L, u)
                    if u and u % 6 == 0:
                        head_transposes(h - 1)
                        yield
                        pe.wait_ge(*after("hgate", L, h))
                    if not quiet:
                        pe.wait_ge(*after("ql", L, spoken(L, u) + 1))
                    pe.wait_ge(*after("kl", L, u + 1))
                    kslot, qslot = (6, 0) if d == 0 else (0, 6)
                    lk, lq = (0, 1) if d == 0 else (1, 0)
                    for p_ in range(2):
                        p = p_ if d == 0 else 1 - p_
                        tt = part * 2 + p
                        q = 2 * u + p_
                        qo = 2 * spoken(L, u) + p_
                        if q:
                            pe.wait_ge(*after("S", L, HEADS_S(u, 2 * p_)))
                        pe.transpose(ps[:, 6, 0:P], KL[:, kslot, p * P:(p + 1) * P], ident).then_inc(sem("kT_mm"), 1)
                        if not quiet:
                            if qo:
                                pe.wait_ge(*after("sc_ev", L, qo))
                            for j in range(2):
                                c0 = p * P + j * C
                                for l in range(LEVELS):
                                    pe.matmul(ps[j * C:(j + 1) * C, 4, l * C:(l + 1) * C], KL[:, lk + l, c0:c0 + C],
                                              QL[:, lq + l, c0:c0 + C], start=True, stop=True)
                                mm = pe.matmul(ps[j * C:(j + 1) * C, 4, 6 * C:7 * C], kk[:, u % 2, c0:c0 + C],
                                               hq[:, h, tt * P + j * C:tt * P + (j + 1) * C], start=True, stop=True)
                            mm.then_inc(sem("sc_mm"), 1)
                        yield
                        pe.wait_ge(*after("kT", L, q + 1))
                        for j in range(2):
                            mm = pe.matmul(ps[:, 7 - j, P:2 * P], kTs[j * C:(j + 1) * C, :],
                                           hv[j * C:(j + 1) * C, tt, h * P:(h + 1) * P], start=True, stop=True)
                        mm.then_inc(sem("pS_mm"), 1)
                        yield
                        if quiet:
                            continue
                        pe.wait_ge(*after("scT", L, qo + 1))
                        if qo:
                            pe.wait_ge(*after("o_evh", L, qo))
                        for j_ in range(2):
                            j = j_ if d == 0 else 1 - j_
                            c = n * 4 + 2 * p_ + j_
                            pe.matmul(ps[j * C:(j + 1) * C, 5, 0:P], scT[j * C:(j + 1) * C, :],
                                      hv[j * C:(j + 1) * C, tt, h * P:(h + 1) * P], start=True, stop=False)
                            pe.wait_ge(*after("S", L, HEADS_S(u, 2 * p_ + j_)))
                            mm = pe.matmul(ps[j * C:(j + 1) * C, 5, 0:P], QL[:, qslot, p * P + j * C:p * P + (j + 1) * C],
                                           S[:, c % 3, :], start=False, stop=True)
                        mm.then_inc(sem("o_mmh"), 1)

                pieces = iter(())
                for k, (g, m) in enumerate(TILES):
                    name, _, tm = GROUPS[g]
                    pe.wait_ge(*after("wlo", L, 4 * g + (2 * (m // 2) + 2 if tm else m + 1)))
                    b = 2 * (k % 2)
                    if k >= 2:
                        pe.wait_ge(*after("proj_ev", L, k - 1))
                    wl, wh = wlo[:, (L * USES + NMOD + g) % 2], whi
                    if tm:
                        cols = slice(256 * (m // 2), 256 * (m // 2) + 256)
                        for t in range(3):
                            rows = slice((3 * (m % 2) + t) * P, (3 * (m % 2) + t + 1) * P)
                            out = tokens(b)[:, t * 256:(t + 1) * 256]
                            for k8 in range(KD):
                                if t * KD + k8 in (3, 9, 15, 21):
                                    next(pieces, None)
                                pe.matmul(out, hhi[:, k8, rows], wh[:, k8, cols], start=k8 == 0, stop=False)
                                pe.matmul(out, hhi[:, k8, rows], wl[:, k8, cols], start=False, stop=False)
                                mm = pe.matmul(out, hlo[:, k8, rows], wh[:, k8, cols], start=False, stop=k8 == KD - 1)
                    else:
                        cols = slice(m * P, (m + 1) * P)
                        T = SEG[bool(tile_start(L, name)):]
                        for k8 in range(KD):
                            if k == 0:
                                pe.wait_ge(*after("hlo", L, 2 * (k8 + 1)))
                            if k8 in (1, 3, 5, 7):
                                next(pieces, None)
                            seg_mm(b, wh[:, k8, cols], hhi[:, k8, :], k8 == 0, False, T)
                            seg_mm(b, wh[:, k8, cols], hlo[:, k8, :], False, False, T)
                            mm = seg_mm(b, wl[:, k8, cols], hhi[:, k8, :], False, k8 == KD - 1, T)
                    mm.then_inc(sem("proj_mm"), 1)
                    st = k - TILES_HG
                    if st in UNIT_AT:
                        for _piece in pieces:
                            pass
                        pieces = unit_products(UNIT_AT[st])
                        next(pieces)
                for _piece in pieces:
                    pass

                pe.wait_ge(*after("rot_ld", L, 16))
                pe.wait_ge(*after("proj_ev", L, len(TILES)))
                def swapped(h):
                    pe.wait_ge(*after(f"rqkv{h % 2}", L, 48 * (h // 2 + 1)))
                    if h:
                        pe.wait_ge(*after("rsc_ev", L, nscore(L) * h))
                    for i in range(2):
                        pe.matmul(ps[:, i, :], perm, rqk[h % 2][:, i, CTX:TOK], start=True, stop=True).then_inc(sem("rot_mm"), 1)

                swapped(0)
                head_transposes(HEADS - 1)
                for h in range(HEADS):
                    qk = rqk[h % 2]
                    pe.wait_ge(*after("rot", L, 2 * (h + 1)))
                    for n, (s0, q0, q1) in enumerate(SCORES[:nscore(L)]):
                        i = nscore(L) * h + n
                        if n >= 4 or h:
                            pe.wait_ge(*after("rsc_ev", L, i - 3))
                        pe.matmul(ps[:, n % 4, 0:q1 - q0], qk[:, 1, s0:s0 + P], qk[:, 0, q0:q1],
                                  start=True, stop=True).then_inc(sem("rsc_mm"), 1)
                    for t in tiles(L):
                        i = ntile(L) * h + t - first_tile(L)
                        b = 4 + i % 2
                        terms = [n for n, (s0, q0, q1) in enumerate(SCORES) if q0 <= t * P < q1]
                        if i >= 2:
                            pe.wait_ge(*after("ro_ev", L, i - 1))
                        pe.wait_ge(*after("rsc_ev", L, nscore(L) * h + max(terms) + 1))
                        for n in terms:
                            s0, q0, q1 = SCORES[n]
                            o = PT_AT[n] + t * P - q0
                            mm = pe.matmul(ps[:, b, 0:DV], PT[:, o:o + P], rv[h % 2][:, s0 // P, :], start=n == terms[0],
                                           stop=n == terms[-1])
                        mm.then_inc(sem("pv_mm"), 1)
                        if h + 1 < HEADS and t == first_tile(L) + 2:
                            swapped(h + 1)
                        if i == 1:
                            pe.wait_ge(*after("hgate", L, HEADS))
                        if i:
                            ret_transposes(pe, L, i - 1)
                ret_transposes(pe, L, HEADS * ntile(L) - 1)

                wohg = hT[:].rearrange("p k t -> p (k t)")[:, 0:4096].rearrange("p (k n) -> p k n", k=4)
                pe.wait_ge(*after("wohg", L, 16))
                pe.wait_ge(*after("rg_done", L, HEADS * ntile(L)))
                pe.wait_ge(*after("rglo", L, HEADS * ntile(L)))
                for m in range(KD):
                    slot, cols = split_weights(L, m)
                    b = 4 * (m % 2)
                    if m >= 2:
                        pe.wait_ge(*after("y_ev", L, m - 1))
                    for k in range(4):
                        seg_mm(b, wohg[:, k, m * P:(m + 1) * P], hgate[:, k, :], k == 0, k == 3, segs(L))
                    pe.wait_ge(*after("wlo", L, len(TILES) + m + 1))
                    for k in range(KD):
                        seg_mm(b + 2, whi[:, k, cols], hhi[:, k, :], k == 0, False, segs(L))
                        seg_mm(b + 2, whi[:, k, cols], rglo[:, k, :], False, False, segs(L))
                        mm = seg_mm(b + 2, wlo[:, slot, k, cols], hhi[:, k, :], False, k == KD - 1, segs(L))
                    mm.then_inc(sem("y_mm"), 1)
                pe.wait_ge(*after("y_ev", L, KD))
                for m in range(KD):
                    slot, cols = split_weights(L, KD + m)
                    pe.wait_ge(*after("wlo", L, len(TILES) + KD + m + 1))
                    b = 2 * (m % 2)
                    if m >= 2:
                        pe.wait_ge(*after("x_mid", L, len(segs(L)) * (m - 1)))
                    for k in range(KD):
                        if m == 0:
                            pe.wait_ge(*after("mlo", L, k + 1))
                        seg_mm(b, whi[:, k, cols], mhi(k), k == 0, False, segs(L))
                        seg_mm(b, whi[:, k, cols], mlo[:, k, :], False, False, segs(L))
                        mm = seg_mm(b, wlo[:, slot, k, cols], mhi(k), False, k == KD - 1, segs(L))
                    mm.then_inc(sem("out_mm"), 1)

                norm_sum("_ffn", L, segs(L))
                for k in range(KD):
                    pe.wait_ge(*after("h_ffn", L, len(segs(L)) * (k + 1)))
                    mm = seg_mm(2, wrt[:, k, :], hT[:, k, :], k == 0, k == KD - 1, segs(L))
                mm.then_inc(sem("lg_mm"), 1)
                pe.wait_ge(*after("lgT", L, 1))
                for t in tiles(L):
                    i = t - first_tile(L)
                    mm = pe.transpose(ps[:, 1, i * 36:(i + 1) * 36], lgT[0:36, t * P:(t + 1) * P], ident[0:36, 0:36])
                mm.then_inc(sem("Lg_mm"), 1)
                def rows(t):
                    b = 4 + 2 * (t % 2)
                    if t - first_tile(L) >= 2:
                        pe.wait_ge(*after("hstg", L, t - first_tile(L) - 1))
                    for k in range(KD):
                        mm = pe.transpose(pair(b)[:, k * P:(k + 1) * P], hT[:, k, t * P:(t + 1) * P], ident)
                    mm.then_inc(sem("hrow_mm"), 1)

                for t in tiles(L)[0:3]:
                    rows(t)
                pe.wait_ge(*after("Mb", L, 2))
                nt = ntile(L)
                for t in range(nt):
                    for t2 in range(t + 1):
                        pe.matmul(ps[:, 2, t * NE:(t + 1) * NE], trib[:, 0:P] if t2 == t else trib[:, P:2 * P], Mb[:, t2, :],
                                  start=t2 == 0, stop=t2 == t)
                for t in range(nt):
                    mm = pe.matmul(ps[:, 2, nt * NE:(nt + 1) * NE], trib[:, P:2 * P], Mb[:, t, :], start=t == 0, stop=t == nt - 1)
                mm.then_inc(sem("rank_mm"), 1)
                for t in tiles(L)[3:]:
                    rows(t)
                if L + 1 < DEPTH:
                    modulation(L + 1, 0)
                pe.wait_ge(*after("onehot", L, 1))
                for n in range(TOPK * nt):
                    mm = pe.matmul(ps[:, 3, 0:2 * NBMAX], OP[:, n, :], OB[:, 1:3, n, :], start=n == 0, stop=n == TOPK * nt - 1)
                mm.then_inc(sem("idx_mm"), 1)
                if L + 1 < DEPTH:
                    modulation(L + 1, 1)
                    pe.wait_ge(*after("mod_ev", L + 1, 2))
                pe.wait_ge(*after("plan", L, 1))
                pe.wait_ge(*after("hstg", L, ntile(L)))
                npairs = pe.value_load(ebi[0:1, NBMAX:NBMAX + 1], min_val=NE // 2, max_val=NBMAX // 2)

                last = pe.value_load(ebi[0:1, NBMAX + 1:NBMAX + 2], min_val=NE - 2, max_val=NBMAX - 2)

                def gathered(i, b):
                    j = 2 * i + b
                    reg_wait(pe, sem(f"xg{b}_{L}"), 16 * i + 16, 16)
                    if not isinstance(j, int) or j:
                        reg_wait(pe, sem(f"xt_a{L}"), j)
                        reg_wait(pe, sem(f"xt_v{L}"), j)
                    for k in range(KD):
                        mm = pe.transpose(pair(0)[:, k * P:(k + 1) * P], XB[b][:, k:D:KD], ident)
                    mm.then_inc(sem(f"xt_mm{L}"), 1)

                def blocks(j0, nth, i=None):
                    first = isinstance(j0, int) and j0 == 0
                    for b in range(2):
                        reg_wait(pe, sem(f"wgu{b}_{L}"), nth * 2, 32)
                        reg_wait(pe, sem(f"xt_a{L}"), j0 + b + 1)
                        reg_wait(pe, sem(f"xt_v{L}"), j0 + b + 1)
                        for k in range(KD):
                            mm = pe.matmul(ps[:, 2 + b, :], XT[b][:, k, :], WE[b][:, k * 512:(k + 1) * 512], start=k == 0,
                                           stop=k == KD - 1)
                        mm.then_inc(sem(f"g_mm{L}"), 1)
                    for b in range(2):
                        reg_wait(pe, sem(f"hid{L}"), j0 + b + 1)
                        for k in range(2):
                            mm = pe.transpose(ps[:, 4, k * P:(k + 1) * P], hid[b][:, k:DE:2], ident)
                        mm.then_inc(sem(f"ht_mm{L}"), 1)
                        if i is not None:
                            gathered(i, b)
                        reg_wait(pe, sem(f"hidT{L}"), j0 + b + 1)
                        reg_wait(pe, sem(f"wd{b}_{L}"), nth, 16)
                        if not first or b:
                            reg_wait(pe, sem(f"yev_a{L}"), j0 + b)
                            reg_wait(pe, sem(f"yev_v{L}"), j0 + b)
                        for n in range(2):
                            for k in range(2):
                                mm = pe.matmul(ps[:, 5 + n, :], hidT[b][:, k, :],
                                               WE[b][:, 4096 + k * 1024 + n * 512:4096 + k * 1024 + (n + 1) * 512],
                                               start=k == 0, stop=k == 1)
                        mm.then_inc(sem(f"d_mm{L}"), 1)

                for b in range(2):
                    gathered(0, b)
                blocks(0, 16, 1)
                with pe.Fori(2, npairs) as i:
                    blocks(2 * i - 2, 16 * i, i)
                blocks(last, 16 * npairs)
                if L + 1 < DEPTH:
                    reg_wait(pe, sem(f"yev_a{L}"), 2 * npairs)
                    reg_wait(pe, sem(f"yev_v{L}"), 2 * npairs)
                    for g in range(2, 4):
                        modulation(L + 1, g)
                for t in tiles(L):
                    b = 2 * (t % 2)
                    i = t - first_tile(L)
                    pe.wait_ge(*after("yc", L, i + 1))
                    if i >= 2:
                        pe.wait_ge(*after("x_end", L, KD * (i - 1)))
                    for m in range(KD):
                        mm = pe.transpose(pair(b)[:, m * P:(m + 1) * P], XB[t % 2][:, m * P:(m + 1) * P], ident)
                    mm.then_inc(sem("yc_mm"), 1)
                    if L + 1 < DEPTH:
                        modulation(L + 1, 4 + i)
                if L + 1 < DEPTH:
                    for g in range(4 + ntile(L), NMOD):
                        modulation(L + 1, g)

            norm_sum("_ffn", DEPTH, SEG[1:])
            pe.wait_ge(sem("h_fin"), KD)
            for t in range(LAT // P):
                b = 4 + 2 * (t % 2)
                if t >= 2:
                    pe.wait_ge(*after("hstg", DEPTH - 1, LAT // P + t - 1))
                for m in range(KD):
                    mm = pe.transpose(pair(b)[:, m * P:(m + 1) * P], hT[:, m, CTX + t * P:CTX + (t + 1) * P], ident)
                mm.then_inc(sem("hrow_mm"), 1)


        @block.scalar
        def _(act):
            chain = [0]

            def link(ins):
                chain[0] += 1
                ins.then_inc(sem("act_chain"), 1)
                act.wait_ge(sem("act_chain"), chain[0])

            table = [""]

            def log_exp():
                if table[0] != "log_exp":
                    act.preload_act_table_set("natural_log_exp_and_others")
                    table[0] = "log_exp"

            def norm_squares(tag, L, s0=0, sq=hT):
                for m in range(KD):
                    act.activation(sq[:, m, s0:TOK], xT[:, m, s0:TOK], ACT.Square).then_inc(sem(f"sq{tag}"), 1)

            def norm_rstd(tag, L, s0=0):
                log_exp()
                act.wait_ge(*after(f"ms{tag}", L, 1))
                link(act.activation(rstd[:, s0:TOK], tokens(0)[:, s0:TOK], ACT.Ln, bias=eps[:]))
                act.activation(rstd[:, s0:TOK], rstd[:, s0:TOK], ACT.Exp, scale=-0.5).then_inc(sem(f"rstd{tag}"), 1)

            def norm_shift(tag, L, shift, T=SEG):
                n = 0
                for m in range(KD):
                    for s0, s1, s in T:
                        n += 1
                        act.wait_ge(*after(f"hm{tag}", L, n))
                        act.activation(hT[:, m, s0:s1], hT[:, m, s0:s1], ACT.Identity,
                                       bias=modT[:, shift * 8 + m, s:s + 1]).then_inc(sem(f"h{tag}"), 1)

            def modulation_row(L, g):
                act.wait_ge(*after("mod_mm", L, g + 1))
                act.activation(mrow[0:2, g * 512:(g + 1) * 512], ps[0:2, mod_bank(L, g), :], ACT.Copy).then_inc(sem("mod_ev"), 1)

            act.wait_ge(sem("init"), 1)
            act.wait_ge(sem("cc_mm"), 1)
            act.activation(cT[:], ps[:, 7, 0:16], ACT.Silu).then_inc(sem("cT"), 1)

            for L in range(DEPTH):
                if L == 0:
                    for g in range(NMOD):
                        modulation_row(0, g)
                log_exp()
                act.wait_ge(*after("pre", L, 3))
                act.activation(lbm[:, 0, :], lbm[:, 0, :], ACT.Exp).then_inc(sem("pre_a"), 1)
                act.activation(lbm[:, 1, :], lbm[:, 1, :], ACT.Exp).then_inc(sem("pre_a"), 1)
                link(act.activation(dec[:, 1, :], dec[:, 1, :], ACT.Exp, scale=-1.0))
                act.activation(dec[:, 1, :], dec[:, 1, :], ACT.Ln, bias=1.0).then_inc(sem("pre_a"), 1)
                act.wait_ge(sem("x_cp"), KD)
                if L:
                    act.wait_ge(*after("x_end", L - 1, KD * ntile(L - 1)))
                norm_squares("_mix", L, sq=squares)

                def weights_high(q):
                    g, m = divmod(q, 4)
                    if m == 0:
                        ring_ready(act, L, NMOD + g)
                    w = ring[:, (L * USES + NMOD + g) % 2, :, m * P:(m + 1) * P]
                    act.activation(whi[:, :, m * P:(m + 1) * P], w, ACT.Copy).then_inc(sem("whi"), 1)

                for q in range(4):
                    weights_high(q)
                norm_rstd("_mix", L)
                act.wait_ge(*after("amod", L, 1))
                act.wait_ge(*after("x_spill", L, 16))
                n = 0
                for m in range(KD):
                    for s0, s1, s in SEG:
                        n += 1
                        act.wait_ge(*after("hm_mix", L, n))
                        act.activation(hhi[:, m, s0:s1], hT[:, m, s0:s1], ACT.Identity,
                                       bias=modT[:, m, s:s + 1]).then_inc(sem("h_mix"), 1)


                def unit_log(u):
                    log_exp()
                    act.wait_ge(*after("f", L, u + 1))
                    act.activation(gg[:, :, 1:C + 1], ff.rearrange("p (c t) -> p c t", t=C), ACT.Ln).then_inc(sem("lnf"), 1)

                def unit_exp(u):
                    act.wait_ge(*after("dd", L, u + 1))
                    e = E[:, 0:8:7, :] if silent(L, u) else E
                    act.activation(e, e, ACT.Exp).then_inc(sem("ee"), 1)

                def head_norm(h):
                    log_exp()
                    act.wait_ge(*after("o_evh", L, 2 * spoken(L, 6 * (h + 1))))
                    for t in tiles(L):
                        link(act.activation(junk, oacc[:, t, :], ACT.Square, accum_out=ss[:, t:t + 1]))
                    t0 = first_tile(L)
                    link(act.activation(ss[:, 8 + t0:8 + TT], ss[:, t0:TT], ACT.Ln, scale=1.0 / P, bias=eps[:]))
                    act.activation(ss[:, 8 + t0:8 + TT], ss[:, 8 + t0:8 + TT], ACT.Exp, scale=-0.5).then_inc(sem("hr"), 1)

                for k, (g, m) in enumerate(TILES):
                    name, _, tm = GROUPS[g]
                    b = 2 * (k % 2)
                    st = k - TILES_HG
                    if st == -AHEAD:
                        if L == 0:
                            act.wait_ge(sem("yclr"), 16 * (NBMAX - NE))
                        unit_log(0)
                        unit_exp(0)
                    act.wait_ge(*after("proj_mm", L, k + 1))
                    s0 = tile_start(L, name)
                    src = tokens(b)[:, s0:TOK]
                    if name in ("ff", "fb"):
                        ins = act.activation(sig[name == "fb"][:, m, :], src, ACT.Sigmoid)
                    elif name == "q":
                        ins = act.activation(hq[:, m, s0:TOK], src, ACT.Silu)
                    elif name == "g":
                        ins = act.activation(hgate[:, m, s0:TOK], src, ACT.Silu)
                    elif name == "v":
                        ins = act.activation(hv[:, 3 * (m % 2):3 * (m % 2) + 3, 256 * (m // 2):256 * (m // 2) + 256],
                                             src.rearrange("p (t n) -> p t n", t=3), ACT.Copy)
                    else:
                        if st >= 2:
                            act.wait_ge(*after(f"spill{st % 2}", L, 16 * (st // 2)))
                        fn = {"rg": ACT.Silu, "ga": ACT.Sigmoid, "gb": ACT.Sigmoid}.get(name[:2], ACT.Copy)
                        ins = act.activation(stage[st % 2][:, s0:TOK], src, fn, scale=QSCALE if name == "rq" else 1.0)
                    if name[:2] in ("ff", "fb", "q", "g", "rg", "ga", "gb"):
                        table[0] = "other"
                    ins.then_inc(sem("proj_ev"), 1)
                    for q in LAST_USE.get(k, ()):
                        weights_high(q)
                    if st in UNIT_AT:
                        u = UNIT_AT[st]
                        if u + 1 < UNITS:
                            unit_log(u + 1)
                            unit_exp(u + 1)
                        if u % 6 == 5:
                            head_norm(u // 6)

                def gated_high(i):
                    h, t = divmod(i, ntile(L))
                    t += first_tile(L)
                    act.wait_ge(*after("rg_done", L, i + 1))
                    act.activation(hhi[:, 2 * h:2 * h + 2, t * P:(t + 1) * P], rgate[:, 2 * h:2 * h + 2, t * P:(t + 1) * P],
                                   ACT.Copy).then_inc(sem("rghi"), 1)

                def quarter_high(q):
                    slot, cols = split_weights(L, q)
                    if q % 4 == 0:
                        ring_ready(act, L, NMOD + len(GROUPS) + q // 4)
                    if q < 4:
                        act.wait_ge(*after("rsc_ev", L, nscore(L) * HEADS))
                    else:
                        act.wait_ge(*(after("y_mm", L, q - 3) if q < 12 else after("out_mm", L, q - 11)))
                    act.activation(whi[:, :, cols], ring[:, slot, :, cols], ACT.Copy).then_inc(sem("whi"), 1)

                log_exp()
                act.wait_ge(*after("dist_ld", L, 16))
                def tables_exp(h):
                    lf, lb = dec[:, 3, h:h + 1], dec[:, 3, 4 + h:5 + h]
                    if h:
                        act.wait_ge(*after("rsc_ev", L, nscore(L) * h))
                    act.activation(Wd, XP, ACT.Exp, scale=lf).then_inc(sem("dt"), 1)
                    act.activation(wtmp, XN, ACT.Exp, scale=lb).then_inc(sem("dt"), 1)
                    act.activation(Dc, XX, ACT.Exp, scale=lf, bias=dec[:, 4, h:h + 1]).then_inc(sem("dt"), 1)
                    act.activation(dtmp, XX, ACT.Exp, scale=dec[:, 5, 4 + h:5 + h], bias=dec[:, 4, 4 + h:5 + h]).then_inc(sem("dt"), 1)
                tables_exp(0)
                for h in range(HEADS):
                    for i in range(ntile(L) * h, ntile(L) * (h + 1)):
                        if h + 1 < HEADS and i == ntile(L) * h + 2:
                            tables_exp(h + 1)
                        act.wait_ge(*after("rvar", L, i + 1))
                        r = rst[:, 32 + 4 * (i % 2):33 + 4 * (i % 2)]
                        link(act.activation(r, rst[:, 17 + 4 * (i % 2):18 + 4 * (i % 2)], ACT.Ln, bias=eps[:]))
                        act.activation(r, r, ACT.Exp, scale=-0.5).then_inc(sem("rr"), 1)
                        if i:
                            gated_high(i - 1)
                        if h == HEADS - 1 and i % ntile(L) < 4:
                            quarter_high(i % ntile(L))
                gated_high(HEADS * ntile(L) - 1)

                for m in range(KD):
                    quarter_high(m + 4)
                    act.wait_ge(*after("y_ev", L, m + 1))
                    s0 = first_tile(L) * P
                    act.activation(mhi(m)[:, s0:TOK], merged[:, m, s0:TOK], ACT.Copy).then_inc(sem("mhi"), 1)
                for m in range(4):
                    quarter_high(m + 12)

                act.wait_ge(*after("x_mid", L, len(segs(L)) * KD))
                s0 = first_tile(L) * P
                norm_squares("_ffn", L, s0)
                norm_rstd("_ffn", L, s0)
                norm_shift("_ffn", L, 3, segs(L))
                act.wait_ge(*after("lg_mm", L, 1))
                act.activation(lgT[0:36, s0:TOK], tokens(2)[0:36, s0:TOK], ACT.Identity, bias=vec[0:36, V_RB:V_RB + 1]).then_inc(sem("lgT"), 1)
                for t in tiles(L):
                    i = t - first_tile(L)
                    act.wait_ge(*after("hrow_mm", L, i + 1))
                    if i >= 2:
                        act.wait_ge(*after(f"hrow{t % 2}", L, 16 * (i // 2)))
                    act.activation(hstg[t % 2], pair(4 + 2 * (t % 2)), ACT.Copy).then_inc(sem("hstg"), 1)
                log_exp()
                act.wait_ge(*after("gd", L, 2))
                act.activation(ro[:, 0:ntile(L) * 4], ro[:, 0:ntile(L) * 4], ACT.Exp).then_inc(sem("gx"), 1)
                act.activation(ro[:, 32:32 + ntile(L)], ro[:, 32:32 + ntile(L)], ACT.Exp).then_inc(sem("gx"), 1)
                if L + 1 < DEPTH:
                    for g in range(2):
                        modulation_row(L + 1, g)
                act.wait_ge(*after("plan", L, 1))
                npairs = act.value_load(ebi[0:1, NBMAX:NBMAX + 1], min_val=NE // 2, max_val=NBMAX // 2)

                last = act.value_load(ebi[0:1, NBMAX + 1:NBMAX + 2], min_val=NE - 2, max_val=NBMAX - 2)

                def gathered(i, b):
                    j = 2 * i + b
                    if not isinstance(i, int) or i:
                        reg_wait(act, sem(f"g_mm{L}"), j - 1)
                    reg_wait(act, sem(f"xt_mm{L}"), j + 1)
                    act.activation(XT[b][:, 0:4, :], ps[:, 0, :].rearrange("p (k t) -> p k t", k=4), ACT.Copy).then_inc(sem(f"xt_a{L}"), 1)

                def blocks(j0, nth, i=None):
                    first = isinstance(j0, int) and j0 == 0
                    for b in range(2):
                        if not first:
                            reg_wait(act, sem(f"hid{L}"), j0)
                        reg_wait(act, sem(f"g_mm{L}"), j0 + b + 1)
                        act.activation(sg[b], ps[:, 2 + b, 0:DE], ACT.Silu).then_inc(sem(f"sg{L}"), 1)
                    for b in range(2):
                        if i is not None:
                            gathered(i, b)
                        if not first:
                            reg_wait(act, sem(f"yst{b}_{L}"), nth, 16)
                        reg_wait(act, sem(f"d_mm{L}"), j0 + b + 1)
                        act.activation(YB[b][:, 0:512], ps[:, 5, :], ACT.Copy).then_inc(sem(f"yev_a{L}"), 1)

                for b in range(2):
                    gathered(0, b)
                blocks(0, 0, 1)
                with act.Fori(2, npairs) as i:
                    blocks(2 * i - 2, 16 * i - 16, i)
                blocks(last, last * 8)
                table[0] = "silu"
                if L + 1 < DEPTH:
                    modulation_row(L + 1, 2)
                for i in range(ntile(L)):
                    t = i + first_tile(L)
                    act.wait_ge(*after(f"yg{t % 2}", L, 32 * (i // 2 + 1)))
                    act.wait_ge(*after("gx", L, 3))
                    if i >= 2:
                        act.wait_ge(*after("yc_mm", L, i - 1))
                    act.activation(XB[t % 2], WE[t % 2][:, 0:D], ACT.Identity, scale=ro[:, 380 + i:381 + i]).then_inc(sem("yp"), 1)
                    if L + 1 < DEPTH:
                        modulation_row(L + 1, 3 + i)
                if L + 1 < DEPTH:
                    for g in range(3 + ntile(L), NMOD):
                        modulation_row(L + 1, g)
            act.wait_ge(*after("x_end", DEPTH - 1, KD * ntile(DEPTH - 1)))
            norm_squares("_ffn", DEPTH, CTX)
            norm_rstd("_ffn", DEPTH, CTX)
            for t in range(LAT // P):
                act.wait_ge(*after("hrow_mm", DEPTH - 1, LAT // P + t + 1))
                if t >= 2:
                    act.wait_ge(*after(f"hrow{t % 2}", DEPTH - 1, 16 * (LAT // P // 2 + t // 2)))
                act.activation(hstg[t % 2], pair(4 + 2 * (t % 2)), ACT.Copy).then_inc(sem("hstg"), 1)

        @block.vector
        def _(dve):
            chain = [0]

            def link(ins):
                chain[0] += 1
                ins.then_inc(sem("dve_chain"), 1)
                dve.wait_ge(sem("dve_chain"), chain[0])

            def norm_scale(tag, L, w, T=SEG):
                dve.wait_ge(*after(f"rstd{tag}", L, 1))
                for m in range(KD):
                    for s0, s1, s in T:
                        dve.scalar_tensor_tensor(out=hT[:, m, s0:s1], in0=xT[:, m, s0:s1], scalar=w(m, s),
                                                 in1=rstd[:, s0:s1], op0=ALU.mult, op1=ALU.mult).then_inc(sem(f"hm{tag}"), 1)

            dve.memset(eps[:], EPS).then_inc(sem("dve_chain"), 1)
            chain[0] += 1
            link(dve.memset(gg, 0.0))
            dve.memset(vrow[:], 0.0).then_inc(sem("init"), 1)
            for m in range(KD):
                dve.wait_ge(sem("cc_mm"), m + 2)
                dve.tensor_copy(xT[:, m, :], tokens(2 * (m % 2))).then_inc(sem("x_cp"), 1)

            for L in range(DEPTH):
                dve.wait_ge(*after("vec_mm", L, 1))
                link(dve.tensor_copy(vec[:], ps[:, 7, 0:V_N]))
                lg = vec[:, V_LB:V_LB + 16].rearrange("p (d l h) -> p l d h", d=2, l=2)
                l0, l1, mx, t1 = [lbm[:, i, :].rearrange("p (d h) -> p d h", d=2) for i in range(4)]
                link(dve.tensor_tensor(mx, lg[:, 0], lg[:, 1], ALU.max))
                dve.tensor_tensor(l0, lg[:, 0], mx, ALU.subtract).then_inc(sem("pre"), 1)
                dve.tensor_tensor(l1, lg[:, 1], mx, ALU.subtract).then_inc(sem("pre"), 1)
                link(dve.tensor_scalar(dec[:, 2, :], dec[:, 0, :], -1.0, None, ALU.mult))
                dve.tensor_tensor(dec[:, 1, :], dec[:, 0, :], dec[:, 2, :], ALU.max).then_inc(sem("pre"), 1)
                dve.wait_ge(*after("pre_a", L, 3))
                l0, l1, lb, om = lbm[:, 0, :], lbm[:, 1, :], lbm[:, 2, :], lbm[:, 3, :]
                link(dve.tensor_tensor(lb, l0, l1, ALU.add))
                link(dve.reciprocal(om, lb))
                if L == 0:
                    link(dve.memset(lb, 0.0))
                else:
                    link(dve.tensor_tensor(l0, l0, om, ALU.mult))
                    link(dve.tensor_tensor(l1, l1, om, ALU.mult))
                    link(dve.tensor_tensor(lb, l0, l1, ALU.add))
                    link(dve.tensor_tensor(lb, lb, l0, ALU.subtract))
                    link(dve.tensor_scalar(lb, lb, 0.0, 1.0 - 1e-6, ALU.max, ALU.min))
                link(dve.tensor_scalar(om, lb, -1.0, 1.0, ALU.mult, ALU.add))
                link(dve.tensor_scalar(dec[:, 2, :], dec[:, 0, :], 0.0, None, ALU.min))
                link(dve.tensor_tensor(dec[:, 3, :], dec[:, 2, :], dec[:, 1, :], ALU.subtract))
                link(dve.tensor_scalar(dec[:, 4, 0:4], dec[:, 3, 0:4], float(CTX), None, ALU.mult))
                link(dve.tensor_scalar(dec[:, 4, 4:8], dec[:, 3, 4:8], float(LAT), None, ALU.mult))
                link(dve.tensor_scalar(dec[:, 5, :], dec[:, 3, :], -1.0, None, ALU.mult))
                dve.wait_ge(*after("modT_mm", L, 1))
                link(dve.tensor_tensor(modT[:], ps[:, 6, 0:96].rearrange("p (j s) -> p j s", s=2),
                                       vec[:, V_BMOD:V_BMOD + 48].unsqueeze(2).to_broadcast([P, 48, 2]), ALU.add))
                for i, (v0, sc) in enumerate(((V_MIX, 1), (V_FFN, 4))):
                    link(dve.tensor_scalar(amod[:, i], modT[:, sc * 8:sc * 8 + 8, :], 1.0, None, ALU.add))
                    ins = dve.tensor_tensor(amod[:, i], amod[:, i], vec[:, v0:v0 + 8].unsqueeze(2).to_broadcast([P, 8, 2]), ALU.mult)
                    if i == 0:
                        link(ins)
                    else:
                        ins.then_inc(sem("amod"), 1)
                dve.wait_ge(*after("amod", L, 1))
                def weights_low(q):
                    g, m = divmod(q, 4)
                    slot, cols = (L * USES + NMOD + g) % 2, slice(m * P, (m + 1) * P)
                    dve.wait_ge(*after("whi", L, q + 1))
                    dve.tensor_tensor(wlo[:, slot, :, cols], ring[:, slot, :, cols], whi[:, :, cols].bitcast(F32), ALU.subtract).then_inc(sem("wlo"), 1)

                for q in range(4):
                    weights_low(q)
                dve.wait_ge(*after("rstd_mix", L, 1))
                for m in range(KD + 1):
                    if m < KD:
                        for s0, s1, s in SEG:
                            dve.scalar_tensor_tensor(out=hT[:, m, s0:s1], in0=xT[:, m, s0:s1], scalar=amod[:, 0, m, s:s + 1],
                                                     in1=rstd[:, s0:s1], op0=ALU.mult, op1=ALU.mult).then_inc(sem("hm_mix"), 1)
                    if m:
                        for n, (s0, s1, s) in enumerate(SEG):
                            dve.wait_ge(*after("h_mix", L, 2 * m - 1 + n))
                            dve.scalar_tensor_tensor(out=hlo[:, m - 1, s0:s1], in0=hT[:, m - 1, s0:s1], scalar=modT[:, m - 1, s:s + 1],
                                                     in1=hhi[:, m - 1, s0:s1].bitcast(F32), op0=ALU.add, op1=ALU.subtract).then_inc(sem("hlo"), 1)


                link(dve.memset(keep, 1.0))
                link(dve.memset(gg, 0.0))
                link(dve.memset(keep[:, :, 0:1], 0.0))

                def forget(u):
                    h, d, n, part = unit(u)
                    x = sig[d][:, h, part * PART:(part + 1) * PART]
                    lb, om = lbm[:, 2, d * 4 + h:d * 4 + h + 1], lbm[:, 3, d * 4 + h:d * 4 + h + 1]
                    k_ = kk[:, u % 2, :]
                    dve.tensor_scalar(k_, x, -1.0, 1.0, ALU.mult, ALU.add).then_inc(sem("k1"), 1)
                    link(dve.tensor_scalar(ff, x, om, lb, ALU.mult, ALU.add))
                    dve.tensor_scalar(ff, ff, F_MIN, None, ALU.max).then_inc(sem("f"), 1)
                    dve.wait_ge(*after("k1", L, u + 1))
                    dve.tensor_scalar(k_, k_, om, None, ALU.mult).then_inc(sem("k"), 1)

                def differences(u):
                    h, d, n, part = unit(u)
                    off = 1 - d
                    dve.wait_ge(*after("lnf", L, u + 1))
                    link(dve.tensor_tensor_scan(Pc.rearrange("p c t -> p (c t)"), keep.rearrange("p c t -> p (c t)"),
                                                gg.rearrange("p c t -> p (c t)"), 0.0, ALU.mult, ALU.add))
                    if u:
                        dve.wait_ge(*after("kl", L, u))
                        dve.wait_ge(*after("dcy", L, u))
                    for l in range(0 if silent(L, u) else LEVELS):
                        w = C >> l
                        n_ = C // w
                        x = Pc[:, :, off:off + C].rearrange("p c (n w) -> p c n w", w=w)
                        mid = Pc[:, :, w // 2:C:w].unsqueeze(3).to_broadcast([P, 4, n_, w // 2])
                        e = E[:, 1 + l, :].rearrange("p (c n w) -> p c n w", c=4, w=w)
                        dve.tensor_tensor(e[:, :, :, w // 2:w], x[:, :, :, w // 2:w], mid, ALU.subtract)
                        dve.tensor_tensor(e[:, :, :, 0:w // 2], mid, x[:, :, :, 0:w // 2], ALU.subtract)
                    last = Pc[:, :, C:C + 1].to_broadcast([P, 4, C])
                    e = [E[:, i, :].rearrange("p (c t) -> p c t", t=C) for i in (0, 7)]
                    dve.tensor_copy(e[0], Pc[:, :, off:off + C])
                    dve.tensor_tensor(e[1], last, Pc[:, :, off:off + C], ALU.subtract).then_inc(sem("dd"), 1)

                def queries(u):
                    h, d, n, part = unit(u)
                    dve.wait_ge(*after("ee", L, u + 1))
                    x = E[:, 0, C - 1:PART:C] if d == 0 else E[:, 7, 0:PART:C]
                    if u:
                        dve.wait_ge(*after("S", L, HEADS_S(u - 1, 4)))
                    dve.tensor_copy(dcy[:], x).then_inc(sem("dcy"), 1)
                    if silent(L, u):
                        return
                    dve.wait_ge(*after("k", L, u + 1))
                    dve.tensor_tensor(KL[:, KPOOL:7, :], E[:, 1 - d + KPOOL:8 - d, :],
                                      kk[:, u % 2, :].unsqueeze(1).to_broadcast([P, 7 - KPOOL, PART]), ALU.mult)
                    q = hq[:, h, part * PART:(part + 1) * PART].unsqueeze(1).to_broadcast([P, 7, PART])
                    dve.scalar_tensor_tensor(out=QL, in0=E[:, d:d + 7, :], scalar=QSCALE, in1=q, op0=ALU.mult,
                                             op1=ALU.mult).then_inc(sem("ql"), 1)

                def keys(u, p_):
                    h, d, n, part = unit(u)
                    if n == 0 and p_ == 0:
                        if u:
                            dve.wait_ge(*after("S", L, 13 * (2 * h + d)))
                        dve.memset(S[:, 0, :], 0.0).then_inc(sem("S"), 1)
                    dve.wait_ge(*after("kT_mm", L, 2 * u + p_ + 1))
                    if 2 * u + p_:
                        dve.wait_ge(*after("pS_mm", L, 2 * u + p_))
                    dve.tensor_copy(kTs, ps[:, 6, 0:P]).then_inc(sem("kT"), 1)

                def state(u, p_):
                    h, d, n, part = unit(u)
                    quiet = silent(L, u)
                    p = p_ if d == 0 else 1 - p_
                    q = 2 * u + p_
                    qo = 2 * spoken(L, u) + p_
                    if not quiet:
                        dve.wait_ge(*after("sc_mm", L, qo + 1))
                        dve.tensor_tensor(msk, ps[:, 4, 0:7 * C].rearrange("p (l t) -> p l t", l=7), masks[d],
                                          ALU.mult).then_inc(sem("sc_ev"), 1)
                        dve.wait_ge(*after("sc_ev", L, qo + 1))
                        dve.tensor_reduce(scT, msk.rearrange("p l t -> p t l"), AX.X, ALU.add).then_inc(sem("scT"), 1)
                    dve.wait_ge(*after("dcy", L, u + 1))
                    dve.wait_ge(*after("pS_mm", L, q + 1))
                    for j_ in range(2):
                        j = j_ if d == 0 else 1 - j_
                        c = n * 4 + 2 * p_ + j_
                        dve.wait_ge(*after("S", L, HEADS_S(u, 2 * p_ + j_)))
                        dve.scalar_tensor_tensor(out=S[:, (c + 1) % 3, :], in0=S[:, c % 3, :], scalar=dcy[:, 2 * p + j:2 * p + j + 1],
                                                 in1=ps[:, 7 - j, P:2 * P], op0=ALU.mult, op1=ALU.add).then_inc(sem("S"), 1)

                def outputs(u, p_):
                    h, d, n, part = unit(u)
                    if silent(L, u):
                        return
                    tt = part * 2 + (p_ if d == 0 else 1 - p_)
                    dve.wait_ge(*after("o_mmh", L, 2 * spoken(L, u) + p_ + 1))
                    if d == 0:
                        dve.tensor_copy(oacc[:, tt, :], ps[:, 5, 0:P]).then_inc(sem("o_evh"), 1)
                    else:
                        dve.tensor_tensor(oacc[:, tt, :], ps[:, 5, 0:P], oacc[:, tt, :], ALU.add).then_inc(sem("o_evh"), 1)

                def rotate(h, which=(0, 1)):
                    dve.wait_ge(*after(f"rqkv{h % 2}", L, 48 * (h // 2 + 1)))
                    dve.wait_ge(*after("rot_ld", L, 16))
                    for i in which:
                        x = rqk[h % 2][:, i, CTX:TOK]
                        dve.wait_ge(*after("rot_mm", L, 2 * h + i + 1))
                        if i or h or L:
                            dve.wait_ge(*after("rot", L, 2 * h + i))
                        link(dve.tensor_tensor(rtmp, ps[:, i, :], sinT, ALU.mult))
                        link(dve.tensor_tensor(x, x, cosT, ALU.mult))
                        dve.tensor_tensor(x, x, rtmp, ALU.add).then_inc(sem("rot"), 1)

                for k in range(TILES_HG - AHEAD):
                    for q in LAST_USE.get(k, ()):
                        weights_low(q)
                dve.wait_ge(*after("proj_ev", L, TILES_HG - AHEAD))
                forget(0)
                differences(0)
                later = []
                for k in range(TILES_HG - AHEAD, len(TILES)):
                    st = k - TILES_HG
                    if st not in UNIT_AT:
                        for q in later + LAST_USE.get(k, []):
                            weights_low(q)
                        later = []
                        continue
                    u = UNIT_AT[st]
                    queries(u)
                    if u and u % 6 == 0:
                        head_gate(dve, L, u // 6 - 1)
                    if u + 1 < UNITS:
                        forget(u + 1)
                    for q in later:
                        weights_low(q)
                    later = LAST_USE.get(k, [])
                    keys(u, 0)
                    state(u, 0)
                    if u + 1 < UNITS:
                        differences(u + 1)
                    outputs(u, 0)
                    keys(u, 1)
                    state(u, 1)
                    outputs(u, 1)
                    if u % 6 == 5:
                        dve.wait_ge(*after("hr", L, u // 6 + 1))
                        for t in tiles(L):
                            dve.tensor_scalar(oacc[:, t, :], oacc[:, t, :], ss[:, 8 + t:9 + t], None, ALU.mult).then_inc(sem("on"), 1)

                def quarter_low(q):
                    slot, cols = split_weights(L, q)
                    dve.wait_ge(*after("whi", L, len(TILES) + q + 1))
                    dve.tensor_tensor(wlo[:, slot, :, cols], ring[:, slot, :, cols], whi[:, :, cols].bitcast(F32),
                                      ALU.subtract).then_inc(sem("wlo"), 1)

                def tables(h):
                    dve.wait_ge(*after("dt", L, 4 * (h + 1)))
                    link(dve.tensor_tensor(Wd, Wd, wtmp, ALU.mult))
                    link(dve.tensor_tensor(Wd[:, 384:512], Wd[:, 384:512], ident, ALU.add))
                    link(dve.tensor_tensor(Dc, Dc, dtmp, ALU.add))

                rotate(0)
                head_gate(dve, L, HEADS - 1)
                dve.wait_ge(*after("rot", L, 2))
                tables(0)
                for h in range(HEADS):

                    def scores(n):
                        s0, q0, q1 = SCORES[n]
                        i = nscore(L) * h + n
                        dve.wait_ge(*after("rsc_mm", L, i + 1))
                        cross = s0 < CTX <= q0
                        tab = Dc if cross else Wd
                        y = (q0 - CTX if cross else q0) - s0 + 384
                        if h:
                            dve.wait_ge(*after("pv_mm", L, ntile(L) * h))
                        dve.tensor_tensor(PT[:, PT_AT[n]:PT_AT[n] + q1 - q0], ps[:, n % 4, 0:q1 - q0], tab[:, y:y + q1 - q0],
                                          ALU.mult).then_inc(sem("rsc_ev"), 1)

                    def ret_norm(i):
                        b = 4 + i % 2
                        st6 = rst[:, 6 * (i % 2):6 * (i % 2) + 6]
                        mv = rst[:, 16 + 4 * (i % 2):18 + 4 * (i % 2)]
                        dve.wait_ge(*after("pv_mm", L, i + 1))
                        link(dve.bn_stats(st6, ps[:, b, 0:DV]))
                        dve.bn_aggr(mv, st6).then_inc(sem("rvar"), 1)
                        dve.wait_ge(*after("rr", L, i + 1))
                        if i >= 2:
                            dve.wait_ge(*after("roT_mm", L, i - 1))
                        dve.tensor_scalar(on[:, i % 2, :], ps[:, b, 0:DV], mv[:, 0:1], rst[:, 32 + 4 * (i % 2):33 + 4 * (i % 2)],
                                          ALU.subtract, ALU.mult).then_inc(sem("ro_ev"), 1)

                    for n in range(nscore(L)):
                        scores(n)
                    for i in range(ntile(L) * h, ntile(L) * (h + 1)):
                        ret_norm(i)
                        if i == 1:
                            dve.wait_ge(*after("rg_ld", L, 16))
                        if i:
                            ret_gate(dve, L, i - 1)
                        n = i - ntile(L) * h
                        if h + 1 < HEADS and n in (2, 3):
                            rotate(h + 1, (n - 2,))
                        if h + 1 < HEADS and n == min(4, ntile(L) - 1):
                            tables(h + 1)
                        if h == HEADS - 1 and 1 <= i % ntile(L) < 4:
                            quarter_low(i % ntile(L) - 1)
                ret_gate(dve, L, HEADS * ntile(L) - 1)

                quarter_low(3)
                t0 = first_tile(L) * P
                for m in range(KD):
                    b = 4 * (m % 2)
                    dve.wait_ge(*after("y_mm", L, m + 1))
                    dve.wait_ge(*after(f"gab{m % 2}", L, 32 * (m // 2 + 1)))
                    if m or L:
                        dve.wait_ge(*after("y_ev", L, m))
                    y = merged[:, m, t0:TOK]
                    link(dve.tensor_tensor(ytmp[:, t0:TOK], tokens(b)[:, t0:TOK], gab[m % 2][:, 0, t0:TOK], ALU.mult))
                    link(dve.tensor_tensor(y, tokens(b + 2)[:, t0:TOK], gab[m % 2][:, 1, t0:TOK], ALU.mult))
                    dve.tensor_tensor(y, y, ytmp[:, t0:TOK], ALU.add).then_inc(sem("y_ev"), 1)
                    quarter_low(m + 4)
                dve.wait_ge(*after("x_back", L, 16))
                for m in range(KD):
                    dve.wait_ge(*after("out_mm", L, m + 1))
                    for s0, s1, s in segs(L):
                        dve.scalar_tensor_tensor(out=xT[:, m, s0:s1], in0=tokens(2 * (m % 2))[:, s0:s1], scalar=modT[:, 16 + m, s:s + 1],
                                                 in1=xT[:, m, s0:s1], op0=ALU.mult, op1=ALU.add).then_inc(sem("x_mid"), 1)
                    if m < 4:
                        quarter_low(m + 12)

                norm_scale("_ffn", L, lambda m, s: amod[:, 1, m, s:s + 1], segs(L))
                dve.wait_ge(*after("mc_ld", L, 16))
                dve.wait_ge(*after("Lg_mm", L, 1))
                nt = ntile(L)
                link(dve.tensor_copy(Lg[:, 0:nt], ps[:, 1, 0:nt * 36].rearrange("p (t e) -> p t e", e=36)))

                def r_(off, n, **kw):
                    v = ro[:, off:off + n]
                    return v.rearrange("p (a b) -> p a b", **kw) if kw else v

                gx, d21 = r_(0, NG * nt, a=nt), r_(32, nt)
                pad, mx8, mx8e = r_(64, 8 * nt, a=nt), r_(112, 8 * nt, a=nt), r_(160, 8 * nt, a=nt)
                ein = r_(208, NPG * nt, a=nt)
                gs, grp, e12, w12 = r_(352, nt), r_(360, nt), r_(368, 2 * nt, a=2), r_(380, 2 * nt, a=2)
                tmp4 = r_(400, nt * NE)
                O1, O2 = r_(600, nt * NE, a=nt), r_(800, nt * NE, a=nt)
                rank, cnt = r_(1000, nt * NE, a=nt), r_(1192, NE)
                nb, inc, bs = r_(1224, NE), r_(1256, NE), r_(1288, NE)
                rk, bb, rj, t6 = r_(1320, 2 * nt, a=2), r_(1332, 2 * nt, a=2), r_(1344, 2 * nt, a=2), r_(1356, 2 * nt, a=2)
                one32 = r_(1370, NE)
                sl = r_(1410, 2 * nt, a=2)
                ebf = r_(1440, NBMAX + 2)
                link(dve.memset(pad, -3.0e38))
                link(dve.tensor_copy(pad[:, :, 0:NG], Lg[:, 0:nt, 0:NG]))
                for t in range(nt):
                    ins = dve.max(mx8[:, t, :], pad[:, t, :])
                    ins.then_inc(sem("m8"), 1)
                dve.wait_ge(*after("m8", L, nt))
                for t in range(nt):
                    dve.max_index(u8[:, t, :], mx8[:, t, :], pad[:, t, :]).then_inc(sem("m8"), 1)
                dve.tensor_tensor(gx, Lg[:, 0:nt, 0:NG], mx8[:, :, 0:1].to_broadcast([P, nt, NG]), ALU.subtract).then_inc(sem("gd"), 1)
                dve.wait_ge(*after("m8", L, 2 * nt))
                link(dve.tensor_copy(grp, u8[:, 0:nt, 0]))
                link(dve.tensor_tensor(r_(400, nt * NG, a=nt), io[:, 0:NG].unsqueeze(1).to_broadcast([P, nt, NG]),
                                       grp.unsqueeze(2).to_broadcast([P, nt, NG]), ALU.is_equal))
                for g in range(NG):
                    oh = r_(400, nt * NG, a=nt)[:, :, g:g + 1].to_broadcast([P, nt, NPG])
                    dst = ein if g == 0 else r_(440, nt * NPG, a=nt)
                    link(dve.tensor_tensor(dst, Lg[:, 0:nt, NG + g * NPG:NG + (g + 1) * NPG], oh, ALU.mult))
                    if g:
                        link(dve.tensor_tensor(ein, ein, r_(440, nt * NPG, a=nt), ALU.add))
                for t in range(nt):
                    dve.max(mx8e[:, t, :], ein[:, t, :]).then_inc(sem("m8"), 1)
                dve.wait_ge(*after("m8", L, 3 * nt))
                for t in range(nt):
                    dve.max_index(u8[:, nt + t, :], mx8e[:, t, :], ein[:, t, :]).then_inc(sem("m8"), 1)
                dve.tensor_tensor(d21, mx8e[:, :, 1], mx8e[:, :, 0], ALU.subtract).then_inc(sem("gd"), 1)
                dve.wait_ge(*after("m8", L, 4 * nt))
                link(dve.tensor_copy(e12, u8[:, nt:2 * nt, 0:2].rearrange("p t k -> p k t")))
                link(dve.tensor_scalar(t6[:, 0, :], grp, float(NPG), None, ALU.mult))
                link(dve.tensor_tensor(e12, e12, t6[:, 0:1, :].to_broadcast([P, 2, nt]), ALU.add))
                for i, O in enumerate((O1, O2)):
                    link(dve.tensor_tensor(O, io.unsqueeze(1).to_broadcast([P, nt, NE]),
                                           e12[:, i, :].unsqueeze(2).to_broadcast([P, nt, NE]), ALU.is_equal))
                dve.tensor_tensor(Mb[:, 0:nt], O1, O2, ALU.add).then_inc(sem("Mb"), 1)
                link(dve.tensor_copy(trib[:, 0:P], tri))
                dve.memset(trib[:, P:2 * P], 1.0).then_inc(sem("Mb"), 1)
                dve.wait_ge(*after("rank_mm", L, 1))
                link(dve.tensor_copy(rank, ps[:, 2, 0:nt * NE].rearrange("p (t e) -> p t e", e=NE)))
                link(dve.tensor_copy(cnt, ps[:, 2, nt * NE:(nt + 1) * NE]))
                link(dve.memset(nb, 1.0))
                link(dve.memset(one32, 1.0))
                for n in range(1, nt):
                    link(dve.tensor_scalar(bs, cnt, float(n * BLK), None, ALU.is_gt))
                    link(dve.tensor_tensor(nb, nb, bs, ALU.add))
                link(dve.tensor_tensor_scan(inc, one32, nb, 0.0, ALU.mult, ALU.add))
                link(dve.tensor_tensor(bs, inc, nb, ALU.subtract))
                for i, O in enumerate((O1, O2)):
                    for dst, tab in ((rk, rank), (bb, bs.unsqueeze(1).to_broadcast([P, nt, NE]))):
                        t4 = tmp4.rearrange("p (a b) -> p a b", a=nt)
                        link(dve.tensor_tensor(t4, O, tab, ALU.mult))
                        link(dve.tensor_reduce(dst[:, i, :], t4, AX.X, ALU.add))
                link(dve.tensor_scalar(rj, rk, float(BLK), None, ALU.is_ge))
                for n in range(2, nt):
                    link(dve.tensor_scalar(t6, rk, float(n * BLK), None, ALU.is_ge))
                    link(dve.tensor_tensor(rj, rj, t6, ALU.add))
                link(dve.tensor_tensor(bb, bb, rj, ALU.add))
                link(dve.tensor_scalar(rj, rj, float(-BLK), None, ALU.mult))
                link(dve.tensor_tensor(rk, rk, rj, ALU.add))
                R2, B2 = [x.rearrange("p a b -> p (a b)").unsqueeze(2) for x in (rk, bb)]
                n2 = TOPK * nt
                link(dve.tensor_tensor(OB[:, 0, 0:n2, :], jrow.unsqueeze(1).to_broadcast([P, n2, NBMAX]),
                                       B2.to_broadcast([P, n2, NBMAX]), ALU.is_equal))
                link(dve.tensor_tensor(OP[:, 0:n2, :], prow.unsqueeze(1).to_broadcast([P, n2, P]), R2.to_broadcast([P, n2, P]),
                                       ALU.is_equal))
                link(dve.tensor_scalar(OB[:, 1, 0:n2, :], OB[:, 0, 0:n2, :], pcol, None, ALU.mult))
                for i in range(TOPK):
                    ob = [OB[:, c, i * nt:(i + 1) * nt, :] for c in (0, 2)]
                    ins = dve.tensor_tensor(ob[1], ob[0], tnum[:, first_tile(L):TT].unsqueeze(2).to_broadcast([P, nt, NBMAX]), ALU.mult)
                    if i:
                        ins.then_inc(sem("onehot"), 1)
                    else:
                        link(ins)
                dve.wait_ge(*after("idx_mm", L, 1))
                link(dve.tensor_copy(r_(400, NBMAX), ps[:, 3, 0:NBMAX]))
                dve.scalar_tensor_tensor(out=idxs[:], in0=ps[:, 3, NBMAX:2 * NBMAX], scalar=float(P), in1=r_(400, NBMAX),
                                         op0=ALU.mult, op1=ALU.add).then_inc(sem("idxs"), 1)
                for c0 in range(0, NBMAX, NBMAX // 2):
                    n2 = NBMAX // 2
                    jt = r_(1500, n2 * NE, a=n2)
                    link(dve.tensor_tensor(jt, jm[:, c0:c0 + n2, :], inc.unsqueeze(1).to_broadcast([P, n2, NE]), ALU.is_ge))
                    link(dve.tensor_reduce(ebf[:, c0:c0 + n2], jt, AX.X, ALU.add))
                link(dve.tensor_scalar(ebf[:, 0:NBMAX], ebf[:, 0:NBMAX], float(NE - 1), None, ALU.min))
                hb = r_(2204, NBMAX)
                link(dve.tensor_tensor(hb, jrow, inc[:, NE - 1:NE].to_broadcast([P, NBMAX]), ALU.is_lt))
                link(dve.tensor_reduce(ebf[:, NBMAX:NBMAX + 1], hb[:, 0:NBMAX:2], AX.X, ALU.add))
                link(dve.tensor_scalar(ebf[:, NBMAX + 1:NBMAX + 2], ebf[:, NBMAX:NBMAX + 1], 2.0, -2.0, ALU.mult, ALU.add))
                dve.tensor_copy(ebi[0:1, :], ebf[0:1, :]).then_inc(sem("plan"), 1)
                link(dve.tensor_scalar(t6, bb, float(BLK), None, ALU.mult))
                link(dve.tensor_tensor(sl, t6, rk, ALU.add))
                dve.tensor_copy(slots[:, :, 0:nt], sl).then_inc(sem("slots"), 1)
                dve.wait_ge(*after("gx", L, 2))
                link(dve.tensor_reduce(gs, gx, AX.X, ALU.add))
                link(dve.tensor_scalar(w12[:, 0, :], d21, 1.0, None, ALU.add))
                link(dve.tensor_tensor(gs, gs, w12[:, 0, :], ALU.mult))
                link(dve.reciprocal(w12[:, 0, :], gs))
                dve.tensor_tensor(w12[:, 1, :], w12[:, 0, :], d21, ALU.mult).then_inc(sem("gx"), 1)
                npairs = dve.value_load(ebi[0:1, NBMAX:NBMAX + 1], min_val=NE // 2, max_val=NBMAX // 2)

                last = dve.value_load(ebi[0:1, NBMAX + 1:NBMAX + 2], min_val=NE - 2, max_val=NBMAX - 2)

                def gathered(i, b):
                    j = 2 * i + b
                    if not isinstance(i, int) or i:
                        reg_wait(dve, sem(f"g_mm{L}"), j - 1)
                    reg_wait(dve, sem(f"xt_mm{L}"), j + 1)
                    dve.tensor_copy(XT[b][:, 4:8, :], ps[:, 1, :].rearrange("p (k t) -> p k t", k=4)).then_inc(sem(f"xt_v{L}"), 1)

                def blocks(j0, nth, i=None):
                    first = isinstance(j0, int) and j0 == 0

                    def hidden(b):
                        reg_wait(dve, sem(f"sg{L}"), j0 + b + 1)
                        if not first:
                            reg_wait(dve, sem(f"ht_mm{L}"), j0)
                        dve.tensor_tensor(hid[b], ps[:, 2 + b, DE:2 * DE], sg[b], ALU.mult).then_inc(sem(f"hid{L}"), 1)

                    hidden(0)
                    for b in range(2):
                        reg_wait(dve, sem(f"ht_mm{L}"), j0 + b + 1)
                        dve.tensor_copy(hidT[b], ps[:, 4, 0:256].rearrange("p (k t) -> p k t", k=2)).then_inc(sem(f"hidT{L}"), 1)
                        if b == 0:
                            hidden(1)
                        if i is not None:
                            gathered(i, b)
                        if not first:
                            reg_wait(dve, sem(f"yst{b}_{L}"), nth, 16)
                        reg_wait(dve, sem(f"d_mm{L}"), j0 + b + 1)
                        dve.tensor_copy(YB[b][:, 512:1024], ps[:, 6, :]).then_inc(sem(f"yev_v{L}"), 1)

                for b in range(2):
                    gathered(0, b)
                blocks(0, 0, 1)
                with dve.Fori(2, npairs) as i:
                    blocks(2 * i - 2, 16 * i - 16, i)
                blocks(last, last * 8)
                for t in tiles(L):
                    s = 1 if t < CTX // P else 0
                    i = t - first_tile(L)
                    dve.wait_ge(*after(f"yg{t % 2}", L, 32 * (i // 2 + 1)))
                    y = WE[t % 2]
                    dve.wait_ge(*after("yp", L, i + 1))
                    dve.scalar_tensor_tensor(out=XB[t % 2], in0=y[:, D:2 * D], scalar=w12[:, 1, i:i + 1], in1=XB[t % 2],
                                             op0=ALU.mult, op1=ALU.add).then_inc(sem("yc"), 1)
                    dve.wait_ge(*after("yc_mm", L, i + 1))
                    for m in range(KD):
                        x = xT[:, m, t * P:(t + 1) * P]
                        dve.scalar_tensor_tensor(out=x, in0=pair(2 * (t % 2))[:, m * P:(m + 1) * P], scalar=modT[:, 40 + m, s:s + 1],
                                                 in1=x, op0=ALU.mult, op1=ALU.add).then_inc(sem("x_end"), 1)
                dve.wait_ge(*after("x_end", L, KD * ntile(L)))

            dve.wait_ge(*after("rstd_ffn", DEPTH, 1))
            for m in range(KD):
                for s0, s1, s in SEG[1:]:
                    dve.scalar_tensor_tensor(out=hT[:, m, s0:s1], in0=xT[:, m, s0:s1], scalar=vec[:, V_FIN + m:V_FIN + m + 1],
                                             in1=rstd[:, s0:s1], op0=ALU.mult, op1=ALU.mult).then_inc(sem("h_fin"), 1)


        @block.gpsimd
        def _(pool):
            def after_wait(s, v, c=1):
                pool.wait_ge(s, v)
                pool.tensor_tensor(nil[:, c:c + 1], nil[:, 0:1], nil[:, 0:1], ALU.add)

            pool.memset(nil[:], 0.0).then_inc(sem("clr"), 1)
            pool.memset(zeros, 0.0).then_inc(sem("clr"), 1)
            pool.wait_ge(sem("clr"), 2)
            pool.wait_ge(*after("mod_mm", 0, NMOD - 1))
            for j in range(NE, NBMAX):
                pool.dma_start(yrow[j * BLK:(j + 1) * BLK, :], zeros).then_inc(sem("yclr"), 16)
            for L in range(DEPTH):
                for u in range(UNITS):
                    h, d, n, part = unit(u)
                    pool.wait_ge(*after("ee", L, u + 1))
                    pool.wait_ge(*after("k", L, u + 1))
                    if u:
                        pool.wait_ge(*(after("pS_mm", L, 2 * u) if silent(L, u - 1) else after("o_mmh", L, 2 * spoken(L, u))))
                    i0, i1 = (0, KPOOL) if not silent(L, u) else (6, 7) if d == 0 else (0, 1)
                    pool.tensor_tensor(KL[:, i0:i1, :], E[:, 1 - d + i0:1 - d + i1, :], kk[:, u % 2, :].unsqueeze(1).to_broadcast([P, i1 - i0, PART]),
                                       ALU.mult).then_inc(sem("kl"), 1)
                for i in range(HEADS * ntile(L)):
                    h, t = divmod(i, ntile(L))
                    t += first_tile(L)
                    at = slice(2 * h, 2 * h + 2), slice(t * P, (t + 1) * P)
                    pool.wait_ge(*after("rghi", L, i + 1))
                    pool.tensor_tensor(rglo[:, at[0], at[1]], rgate[:, at[0], at[1]], hhi[:, at[0], at[1]].bitcast(F32),
                                       ALU.subtract).then_inc(sem("rglo"), 1)
                s0 = first_tile(L) * P
                for m in range(KD):
                    pool.wait_ge(*after("mhi", L, m + 1))
                    pool.tensor_tensor(mlo[:, m, s0:TOK], merged[:, m, s0:TOK], mhi(m)[:, s0:TOK].bitcast(F32),
                                       ALU.subtract).then_inc(sem("mlo"), 1)
                pool.wait_ge(*after("idxs", L, 1))
                for i in range(2):
                    pool.wait_ge(*after(f"hrow{i}", L, 16 * (ntile(L) // 2)))

                def blocks(i):
                    for b in range(2):
                        j = 2 * i + b
                        if not isinstance(i, int):
                            reg_wait(pool, sem(f"xt_mm{L}"), j - 1)
                        pool.tensor_copy(idxc[:, b:b + 1], idxs[:, bass.ds(j, 1)]).then_inc(sem(f"idxc{L}"), 1)
                        after_wait(sem(f"idxc{L}"), j + 1)
                        pool.indirect_dma_start(
                            out=XB[b], out_offset=None, in_=hrow,
                            in_offset=bass.IndirectOffsetOnAxis(ap=idxc[:, b:b + 1].bitcast(U32), axis=0)).then_inc(sem(f"xg{b}_{L}"), 16)

                blocks(0)
                pool.wait_ge(*after("plan", L, 1))
                npairs = pool.value_load(ebi[0:1, NBMAX:NBMAX + 1], min_val=NE // 2, max_val=NBMAX // 2)
                with pool.Fori(1, npairs) as i:
                    blocks(i)
                pool.wait_ge(*after("slots", L, 1))
                for b in range(2):
                    after_wait(sem(f"yst{b}_{L}"), 16 * npairs, 2 + b)
                for t in tiles(L):
                    n = t - first_tile(L)
                    if n >= 2:
                        pool.wait_ge(*after("yc", L, n - 1))
                    for i in range(2):
                        pool.indirect_dma_start(
                            out=WE[t % 2][:, i * D:(i + 1) * D], out_offset=None, in_=yrow,
                            in_offset=bass.IndirectOffsetOnAxis(ap=slots[:, i, n:n + 1], axis=0)).then_inc(sem(f"yg{t % 2}"), 16)


def HEADS_S(u, n):
    scan, part = divmod(u, NPART)
    return 13 * scan + 1 + 4 * part + n


SCORES = [(s, CTX, TOK) for s in range(0, TOK, P)] + [(s, 0, CTX) for s in range(0, CTX, P)]
PT_AT = [sum(q1 - q0 for _, q0, q1 in SCORES[:n]) for n in range(len(SCORES))]




def nscore(L):
    return len(SCORES) if L < DEPTH - 1 else len(SCORES) - CTX // P


def tile_start(L, name):
    return 0 if name in ("ff", "fb", "rk", "v", "rv0", "rv1") else first_tile(L) * P


_INS = ["x", "c", "ctx", "c_ctx", "w_mod", "b_mod", "norm_mix_w", "norm_ffn_w", "w_in", "hgrn_lb_logits", "hgrn_norm_w",
        "ret_decay_logit", "ret_gn_w", "w_o_hgrn", "w_o_ret", "w_out", "router_group_w", "router_group_b",
        "router_expert_w", "router_expert_b", "expert_w_gate", "expert_w_up", "expert_w_down", "final_norm_w"]


def tables():
    import numpy as np
    f = np.float32
    cst = np.zeros((P, 2 * P + 2 * 7 * C), f)
    cst[:, 0:P] = np.eye(P)
    cst[:, P:2 * P] = 1.0 / D
    s, t = np.meshgrid(np.arange(C), np.arange(C), indexing="ij")
    for d in range(2):
        m = np.zeros((C, 7, C), f)
        for l in range(LEVELS):
            w = C >> l
            same = s // w == t // w
            first, second = (s, t) if d == 0 else (t, s)
            m[:, l, :] = same & (first % w < w // 2) & (second % w >= w // 2)
        m[:, 6, :] = np.eye(C) * QSCALE
        cst[:, 2 * P + d * 7 * C:2 * P + (d + 1) * 7 * C] = np.tile(m.reshape(C, -1), (2, 1))
    rc = np.zeros((P, 2 * LAT + P + 3 * XW), f)
    pos = np.arange(LAT)
    inv = (10000.0 ** (-np.arange(0, 64, 2, dtype=f) / f(64))).astype(f)
    for half, x in enumerate((pos // 64, pos % 64)):
        ang = (inv[:, None] * x[None, :].astype(f)).astype(f)
        for i, sign in ((0, -1.0), (1, 1.0)):
            r = slice(64 * half + 32 * i, 64 * half + 32 * (i + 1))
            rc[r, 0:512] = np.cos(ang)
            rc[r, 512:1024] = sign * np.sin(ang)
    for i in range(P):
        rc[i ^ 32, 1024 + i] = 1.0
    xx = np.arange(XW)[None, :] - 384 - np.arange(P)[:, None]
    rc[:, 1152:1152 + XW] = xx
    rc[:, 1152 + XW:1152 + 2 * XW] = np.maximum(xx, 0)
    rc[:, 1152 + 2 * XW:] = np.maximum(-xx, 0)
    mc = np.zeros((P, MC), f)
    mc[:, 0:P] = np.triu(np.ones((P, P)), 1)
    mc[:, P:P + NBMAX * NE] = np.repeat(np.arange(NBMAX), NE)[None, :]
    mc[:, P + NBMAX * NE:P + NBMAX * NE + NE] = np.arange(NE)[None, :]
    mc[:, P + NBMAX * NE + NE:MC - P - TT - 1] = np.arange(NBMAX)[None, :]
    mc[:, MC - P - TT - 1:MC - TT - 1] = np.arange(P)[None, :]
    mc[:, MC - TT - 1:MC - 1] = np.arange(TT)[None, :]
    mc[:, MC - 1] = np.arange(P)
    return {"cst": cst, "rc": rc, "mc": mc}


def kernel(**inputs):
    import numpy as _np
    import concourse.bacc as _bacc
    from concourse import mybir as _mybir
    from concourse.bass_utils import run_bass_kernel_spmd as _run

    nc = _bacc.Bacc("TRN2", target_bir_lowering=False, num_devices=1)
    arrays, aps = {}, {}
    data = {n: _np.ascontiguousarray(inputs[n]) for n in _INS}
    data.update(tables())
    for name, x in data.items():
        arrays[f"in_{name}"] = x
        aps[name] = nc.dram_tensor(f"in_{name}", x.shape, _mybir.dt.from_np(x.dtype), kind="ExternalInput").ap()
    aps["out"] = nc.dram_tensor("out_0", (1, LAT, D), _mybir.dt.float32, kind="ExternalOutput").ap()
    build(nc, aps)
    r = _run(nc, [arrays], core_ids=[0])
    return r.results[0]["out_0"]
```
